# Optimizing a Trainium2 kernel written in Bass

```python
import math
import jax, jax.numpy as jnp
from jax import lax
import numpy as np

D_MODEL = 1024
BATCH = 1
SEQ = 1024
DEPTH = 2
DEC_BATCH = 8
DEC_SEQ = 4
PAST_LEN = 1024
PAGE_SIZE = 128

N_MIXERS = 2
EXPAND = 2
BRANCH_W = EXPAND * D_MODEL
CONV_WIDTH = 31
HEAD_DIM = 64
VAL_DIM = 2 * HEAD_DIM
N_HEADS = BRANCH_W // VAL_DIM
N_KV_HEADS = N_HEADS // 4
GROUP = N_HEADS // N_KV_HEADS
Q_W = N_HEADS * 2 * HEAD_DIM
KV_W = N_KV_HEADS * 2 * HEAD_DIM
ROT_DIM = HEAD_DIM // 4
ROPE_THETA = 500000.0
BLOCK_Q = 128
RMS_EPS = 1e-6
LN_EPS = 1e-5
SCALE = HEAD_DIM ** -0.5
N_CONV_LAYERS = (DEPTH + N_MIXERS - 1) // N_MIXERS
N_ATTN_LAYERS = DEPTH // N_MIXERS

kernel_name = 'hybrid_conformer_conv_diff_attn_step'

def rmsnorm(x, g, eps=RMS_EPS):
    xf = x.astype(jnp.float32)
    y = xf * lax.rsqrt(jnp.mean(xf * xf, axis=-1, keepdims=True) + eps)
    return (y * g.astype(jnp.float32)).astype(x.dtype)

def layernorm(x, g, b, eps=LN_EPS):
    xf = x.astype(jnp.float32)
    mu = jnp.mean(xf, axis=-1, keepdims=True)
    xc = xf - mu
    y = xc * lax.rsqrt(jnp.mean(xc * xc, axis=-1, keepdims=True) + eps)
    return (y * g.astype(jnp.float32) + b.astype(jnp.float32)).astype(x.dtype)

def conv_mixer(h, prev, w_in, dw_w, dw_b, ln_g, ln_b, w_out):
    z = jnp.einsum('ntd,de->nte', h, w_in)
    a, b, gate = jnp.split(z, 3, axis=-1)
    u = a * jax.nn.sigmoid(b)
    u_pad = jnp.concatenate([prev.astype(u.dtype), u], axis=1)
    c = lax.conv_general_dilated(u_pad, dw_w[:, None, :].astype(u.dtype), (1,), 'VALID',
                                 dimension_numbers=('NWC', 'WIO', 'NWC'),
                                 feature_group_count=BRANCH_W) + dw_b
    c = jax.nn.silu(layernorm(c, ln_g, ln_b))
    y = jnp.einsum('nte,ed->ntd', c * jax.nn.silu(gate), w_out)
    return y, u_pad[:, -(CONV_WIDTH - 1):]

def rope(x, pos):
    half = ROT_DIM // 2
    inv_freq = ROPE_THETA ** (-jnp.arange(half, dtype=jnp.float32) / half)
    ang = pos.astype(jnp.float32)[:, None] * inv_freq[None, :]
    cos = jnp.cos(ang)[:, None, None, :]
    sin = jnp.sin(ang)[:, None, None, :]
    xr = x[..., :ROT_DIM].astype(jnp.float32)
    x1, x2 = xr[..., :half], xr[..., half:]
    rot = jnp.concatenate([x1 * cos - x2 * sin, x2 * cos + x1 * sin], axis=-1).astype(x.dtype)
    return jnp.concatenate([rot, x[..., ROT_DIM:]], axis=-1)

def diff_lambda(lq1, lk1, lq2, lk2, lam_init):
    f = lambda a, b: jnp.exp(jnp.sum(a.astype(jnp.float32) * b.astype(jnp.float32)))
    return f(lq1, lk1) - f(lq2, lk2) + lam_init

def attn_project(h, pos, w_in):
    n, t = h.shape[:2]
    z = jnp.einsum('ntd,de->nte', h, w_in)
    q, k, v, gate = jnp.split(z, [Q_W, Q_W + KV_W, Q_W + 2 * KV_W], axis=-1)
    q = rope(q.reshape(n, t, N_HEADS, 2, HEAD_DIM), pos).reshape(n, t, N_KV_HEADS, GROUP, 2, HEAD_DIM)
    k = rope(k.reshape(n, t, N_KV_HEADS, 2, HEAD_DIM), pos)
    v = v.reshape(n, t, N_KV_HEADS, VAL_DIM)
    return q, k, v, gate

def diff_attend(q, k, v, q_pos, k_pos, lam):
    s = jnp.einsum('ntkgch,nskch->nkgcts', q, k, preferred_element_type=jnp.float32) * SCALE
    mask = k_pos[None, :] <= q_pos[:, None]
    s = jnp.where(mask, s, -jnp.inf)
    p = jax.nn.softmax(s, axis=-1)
    a = p[:, :, :, 0] - lam * p[:, :, :, 1]
    return jnp.einsum('nkgts,nskv->ntkgv', a, v.astype(jnp.float32))

def attn_output(o, gate, subln_g, lam_init, w_out):
    n, t = gate.shape[:2]
    o = rmsnorm(o, subln_g) * (1.0 - lam_init)
    o = o.reshape(n, t, BRANCH_W).astype(gate.dtype)
    return jnp.einsum('nte,ed->ntd', o * jax.nn.silu(gate), w_out)

def attn_prompt(h, w_in, lam, subln_g, lam_init, w_out):
    n, t = h.shape[:2]
    pos = jnp.arange(t, dtype=jnp.int32)
    q, k, v, gate = attn_project(h, pos, w_in)
    nb = t // BLOCK_Q
    qb = jnp.moveaxis(q.reshape((n, nb, BLOCK_Q) + q.shape[2:]), 1, 0)
    pb = pos.reshape(nb, BLOCK_Q)
    o = lax.map(lambda qp: diff_attend(qp[0], k, v, qp[1], pos, lam), (qb, pb))
    o = jnp.moveaxis(o, 0, 1).reshape((n, t) + o.shape[3:])
    y = attn_output(o, gate, subln_g, lam_init, w_out)
    return y, k.reshape(n, t, N_KV_HEADS, 2 * HEAD_DIM), v

def attn_sample(h, k_pages, v_pages, page_table, w_in, lam, subln_g, lam_init, w_out):
    n, t = h.shape[:2]
    past = page_table.shape[1] * PAGE_SIZE
    pos = past + jnp.arange(t, dtype=jnp.int32)
    q, k, v, gate = attn_project(h, pos, w_in)
    k_past = k_pages[page_table].reshape(n, past, N_KV_HEADS, 2, HEAD_DIM).astype(k.dtype)
    v_past = v_pages[page_table].reshape(n, past, N_KV_HEADS, VAL_DIM).astype(v.dtype)
    k_all = jnp.concatenate([k_past, k], axis=1)
    v_all = jnp.concatenate([v_past, v], axis=1)
    k_pos = jnp.arange(past + t, dtype=jnp.int32)
    o = diff_attend(q, k_all, v_all, pos, k_pos, lam)
    y = attn_output(o, gate, subln_g, lam_init, w_out)
    return y, k.reshape(n, t, N_KV_HEADS, 2 * HEAD_DIM), v

def setup_inputs(seed: int = 0) -> dict:
    key = jax.random.key(seed)
    ks = jax.random.split(key, 24)
    f32 = jnp.float32
    nrm = lambda k, shape, s: s * jax.random.normal(k, shape, f32)
    n_pages = PAST_LEN // PAGE_SIZE
    n_phys = (DEC_BATCH * n_pages * 5) // 4
    page_table = jax.random.permutation(ks[5], n_phys)[:DEC_BATCH * n_pages]
    page_table = page_table.reshape(DEC_BATCH, n_pages).astype(jnp.int32)
    return {
        'x_prompt': nrm(ks[0], (BATCH, SEQ, D_MODEL), 1.0),
        'x_sample': nrm(ks[1], (DEC_BATCH, DEC_SEQ, D_MODEL), 1.0),
        'state_conv': nrm(ks[2], (N_CONV_LAYERS, DEC_BATCH, CONV_WIDTH - 1, BRANCH_W), 0.5),
        'cache_k': nrm(ks[3], (N_ATTN_LAYERS, n_phys, PAGE_SIZE, N_KV_HEADS, 2 * HEAD_DIM), 1.0),
        'cache_v': nrm(ks[4], (N_ATTN_LAYERS, n_phys, PAGE_SIZE, N_KV_HEADS, VAL_DIM), 1.0),
        'page_table': page_table,
        'norm_g': 1.0 + nrm(ks[6], (DEPTH, D_MODEL), 0.02),
        'final_norm_g': 1.0 + nrm(ks[7], (D_MODEL,), 0.02),
        'conv_w_in': nrm(ks[8], (N_CONV_LAYERS, D_MODEL, 3 * BRANCH_W), D_MODEL ** -0.5),
        'conv_dw_w': nrm(ks[9], (N_CONV_LAYERS, CONV_WIDTH, BRANCH_W), CONV_WIDTH ** -0.5),
        'conv_dw_b': nrm(ks[10], (N_CONV_LAYERS, BRANCH_W), 0.01),
        'conv_ln_g': 1.0 + nrm(ks[11], (N_CONV_LAYERS, BRANCH_W), 0.02),
        'conv_ln_b': nrm(ks[12], (N_CONV_LAYERS, BRANCH_W), 0.01),
        'conv_w_out': nrm(ks[13], (N_CONV_LAYERS, BRANCH_W, D_MODEL), BRANCH_W ** -0.5),
        'attn_w_in': nrm(ks[14], (N_ATTN_LAYERS, D_MODEL, Q_W + 2 * KV_W + BRANCH_W), D_MODEL ** -0.5),
        'attn_lambda_q1': nrm(ks[15], (N_ATTN_LAYERS, HEAD_DIM), 0.1),
        'attn_lambda_k1': nrm(ks[16], (N_ATTN_LAYERS, HEAD_DIM), 0.1),
        'attn_lambda_q2': nrm(ks[17], (N_ATTN_LAYERS, HEAD_DIM), 0.1),
        'attn_lambda_k2': nrm(ks[18], (N_ATTN_LAYERS, HEAD_DIM), 0.1),
        'attn_subln_g': 1.0 + nrm(ks[19], (N_ATTN_LAYERS, VAL_DIM), 0.02),
        'attn_w_out': nrm(ks[20], (N_ATTN_LAYERS, BRANCH_W, D_MODEL), BRANCH_W ** -0.5),
    }

def reference(x_prompt, x_sample, state_conv, cache_k, cache_v, page_table, norm_g, final_norm_g,
              conv_w_in, conv_dw_w, conv_dw_b, conv_ln_g, conv_ln_b, conv_w_out,
              attn_w_in, attn_lambda_q1, attn_lambda_k1, attn_lambda_q2, attn_lambda_k2,
              attn_subln_g, attn_w_out):
    yp, ys = x_prompt, x_sample
    conv_p, conv_s, k_p, v_p, k_s, v_s = [], [], [], [], [], []
    for i in range(DEPTH):
        j = i // N_MIXERS
        hp = rmsnorm(yp, norm_g[i])
        hs = rmsnorm(ys, norm_g[i])
        if i % N_MIXERS == 0:
            cw = (conv_w_in[j], conv_dw_w[j], conv_dw_b[j], conv_ln_g[j], conv_ln_b[j], conv_w_out[j])
            zeros = jnp.zeros((hp.shape[0], CONV_WIDTH - 1, BRANCH_W), hp.dtype)
            op, sp = conv_mixer(hp, zeros, *cw)
            os_, ss = conv_mixer(hs, state_conv[j], *cw)
            conv_p.append(sp)
            conv_s.append(ss)
        else:
            lam_init = 0.8 - 0.6 * math.exp(-0.3 * i)
            lam = diff_lambda(attn_lambda_q1[j], attn_lambda_k1[j], attn_lambda_q2[j], attn_lambda_k2[j], lam_init)
            op, kp, vp = attn_prompt(hp, attn_w_in[j], lam, attn_subln_g[j], lam_init, attn_w_out[j])
            os_, kq, vq = attn_sample(hs, cache_k[j], cache_v[j], page_table, attn_w_in[j], lam,
                                      attn_subln_g[j], lam_init, attn_w_out[j])
            k_p.append(kp)
            v_p.append(vp)
            k_s.append(kq)
            v_s.append(vq)
        yp = yp + op
        ys = ys + os_
    y_prompt = rmsnorm(yp, final_norm_g)
    y_sample = rmsnorm(ys, final_norm_g)
    return (y_prompt, y_sample, jnp.stack(conv_p), jnp.stack(conv_s),
            jnp.stack(k_p), jnp.stack(v_p), jnp.stack(k_s), jnp.stack(v_s))


_drawn_inputs = setup_inputs


def setup_inputs(seed=0):
    import zlib

    import numpy as np

    out = dict(_drawn_inputs(seed))
    spreads = {}
    factors = {'final_norm_g': 2.861,
     'conv_dw_b': 6.337,
     'conv_ln_g': 5.872,
     'conv_ln_b': 8.0,
     'attn_lambda_q1': 2.691,
     'attn_lambda_k1': 3.695,
     'attn_lambda_q2': 2.873,
     'attn_lambda_k2': 5.814,
     'attn_subln_g': 8.0}
    for name, (base, spread) in spreads.items():
        noise = np.random.default_rng([zlib.crc32(name.encode()), seed]).standard_normal(out[name].shape)
        drawn = base * np.exp(spread * noise) if base else spread * noise
        out[name] = __import__('jax').numpy.asarray(drawn.astype(out[name].dtype))
    for name, factor in factors.items():
        out[name] = (out[name] * factor).astype(out[name].dtype)
    return out
```

```python
from contextlib import ExitStack
import math

import numpy as np

import concourse.bass as bass
from concourse import mybir

F32 = mybir.dt.float32
F32R = mybir.dt.float32r
I32 = mybir.dt.int32
ALU = mybir.AluOpType
ACT = mybir.ActivationFunctionType
AX = mybir.AxisListType

P = 128
D = 1024
KD = D // P
NP_TOK, NB, NT = 1024, 8, 4
NS_TOK = NB * NT
T = NP_TOK + NS_TOK
CH = T // 3
E = 2048
JT = E // P
TAPS = 31
PAD = TAPS - 1
WIN = PAD + NT
NG, GH = 4, 4
HD, VD = 64, 128
ROT = HD // 4
THETA = 500000.0
PAST, PAGE = 1024, 128
PAGES = PAST // PAGE
QT = NP_TOK // P
SCALE = HD ** -0.5
RMS_EPS, LN_EPS = 1e-6, 1e-5
LAM_INIT = 0.8 - 0.6 * math.exp(-0.3)
MASKED = -float(2 ** 100)

C_NG1, C_NG2, C_FNG, C_DWB, C_LNG, C_LNB, C_SUB, N_COLS = 0, 8, 16, 24, 40, 56, 72, 73

U_CONV, U_COUT, U_ATT, U_AOUT, N_UNITS = 0, 48, 64, 104, 120

POOL_TAPS = 10
POOL_FIRST = 4


class Count:

    def __init__(self, sem):
        self.sem, self.n, self.off = sem, 0, 0

    def up(self):
        self.n += 1
        return 1

    def now(self, back=0):
        return self.off + (self.n - back)

    def enter(self, i, first, per):
        self.start, self.per, self.off = self.n, per, (i - first) * per

    def leave(self, trips):
        assert self.n - self.start == self.per, (self.n - self.start, self.per)
        self.n, self.off = self.n + self.per * (trips - 1), 0


def host_constants():
    pos = np.concatenate([np.arange(NP_TOK), np.tile(PAST + np.arange(NT), NB)]).astype(np.float32)
    half = ROT // 2
    inv = np.float32(THETA) ** (-np.arange(half, dtype=np.float32) / np.float32(half))
    ang = pos[None, :] * inv[:, None].astype(np.float32)
    cos, sin = np.ones((P, T), np.float32), np.zeros((P, T), np.float32)
    swap = np.zeros((P, P), np.float32)
    for c in range(2):
        for i in range(half):
            a, b = HD * c + i, HD * c + half + i
            cos[a] = cos[b] = np.cos(ang[i])
            sin[a] = sin[b] = np.sin(ang[i])
            swap[b, a], swap[a, b] = -1.0, 1.0
    t = np.arange(P)
    causal = np.where(t[None, :] <= t[:, None], 0.0, MASKED).astype(np.float32)
    g, c, h, s = np.meshgrid(np.arange(NG), np.arange(2), np.arange(GH), np.arange(NT), indexing="ij")
    g, c, h, s = (v.reshape(-1) for v in (g, c, h, s))
    newmask = np.where(np.arange(NT)[None, :] <= s[:, None], 0.0, MASKED).astype(np.float32)
    rows = np.zeros((P, NG * GH * NT), np.float32)
    rows[np.arange(P), (g * GH + h) * NT + s] = 1.0
    cc = np.stack([1.0 - c, c], 1).astype(np.float32)
    small = np.concatenate([np.eye(P, dtype=np.float32), swap, causal, rows, newmask, cc], 1)
    return {"c_small": small, "c_cos": cos, "c_sin": sin}


N_SMALL = 3 * P + NG * GH * NT + NT + 2


def build(nc, a, o):
    ctx = ExitStack()
    with ctx:
        def sem(name):

            return ctx.enter_context(nc.semaphore(name))

        base = (nc.sbuf_base + 31) // 32 * 32
        cursor = [base]

        def place(name, shape, dt=F32, at=None):
            size = (int(np.prod(shape[1:])) * 4 + 31) // 32 * 32
            if at is None:
                at = cursor
            t = nc.alloc_sbuf_tensor_at(name, list(shape), dt, offset=at[0])
            at[0] += size
            return t

        small = place("small", [P, N_SMALL])
        ident = small[:, 0:P]
        swap = small[:, P:2 * P]
        causal = small[:, 2 * P:3 * P]
        rowsel = small[:, 3 * P:3 * P + 64]
        newmask = small[:, 3 * P + 64:3 * P + 68]
        cc = small[:, 3 * P + 68:3 * P + 70]
        ones = place("ones", [P, P])
        cols = place("cols", [P, N_COLS])
        dww = place("dww", [P, JT, TAPS])
        misc = place("misc", [P, 8])
        eps_rms, eps_ln, neglam, subg, rowcoef = (misc[:, i:i + 1] for i in range(5))
        raw_at = [cursor[0], cursor[0] + 4 * KD * P]
        raw = [place(f"w_raw{s}", [P, KD, P]) for s in range(2)]
        whi = [place(f"w_hi{s}", [P, KD, P], F32R) for s in range(2)]
        wlo = [place(f"w_lo{s}", [P, KD, P], F32R) for s in range(2)]
        SLOT = 4 * T
        slots0 = cursor[0]
        assert slots0 + 46 * SLOT <= 229344, slots0

        def slot(n):
            return [slots0 + n * SLOT]

        ps = nc.alloc_psum_tensor("ps", [P, 8, 512], F32)

        def pset(s):
            return ps[:, 3 * s:3 * s + 3, 0:CH]

        def chunks(ap):
            return ap.rearrange("p (c n) -> p c n", c=3)

        Hhi = place("Hhi", [P, KD, T], F32R, slot(0))
        Hlo = place("Hlo", [P, KD, T], F32R, slot(8))
        Ghi = place("Ghi", [P, JT, T], F32R, slot(0))
        C = place("C", [P, JT, T], F32, slot(16))
        Glo = place("Glo", [P, JT, T], F32R, slot(16))
        Y = place("Y", [P, KD, T], F32, slot(32))
        xres = [place(f"xres{s}", [P, T], F32, slot(40 + s)) for s in range(2)]
        ssum = place("ssum", [P, T], F32, slot(42))
        sq = place("sq", [P, T], F32, slot(43))
        std = place("std", [P, T], F32, slot(44))
        csum = place("csum", [P, T], F32, slot(45))

        def scratch(name, shape):
            return nc.dram_tensor(name, shape, F32, kind="Internal").ap()
        res_d = [scratch("res0", [P, KD, T]), scratch("res1", [P, KD, T])]
        gate_d = [scratch("gate0", [JT, P, T]), scratch("gate1", [JT, P, T])]
        q_d = scratch("q_rot", [JT, P, T])
        k_d = scratch("k_rot", [NG, P, T])

        raw_in = [sem("raw_in0"), sem("raw_in1")]
        w_hi, w_lo, w_used = sem("w_hi"), sem("w_lo"), sem("w_used")
        act_step, dve_step, pool_step = Count(sem("act_step")), Count(sem("dve_step")), Count(sem("pool_step"))

        w_cin = a["conv_w_in"][0].rearrange("(k p) e -> p k e", p=P)
        w_cout = a["conv_w_out"][0].rearrange("(f k p) e -> f p k e", p=P, f=2)
        w_ain = a["attn_w_in"][0].rearrange("(k p) e -> p k e", p=P)
        w_aout = a["attn_w_out"][0].rearrange("(f k p) e -> f p k e", p=P, f=2)

        def conv_src(col, kind):
            return w_cin[:, :, bass.ds(col + (E, 0, 2 * E)[kind], P)]

        def out_src(w, pair, q):
            return w[q // 2][:, :, bass.ds((pair * 2 + q % 2) * P, P)]

        ATT_ORDER = list(range(16)) + list(range(16, 24)) + list(range(24, 40))

        def att_src(u):
            return w_ain[:, :, bass.ds(u * P, P)]

        def load_unit(sp, n, s, src):
            sp.wait_ge(w_lo, n - 1)
            sp.dma_start(raw[s][:, :, :], src).then_inc(raw_in[s], 16)

        def make_hi(act, n, s, turn, reused=True):
            act.wait_ge(raw_in[s], turn * 16)
            if reused:
                act.wait_ge(w_used, n - 1)
            act.activation(whi[s][:, :, :], raw[s][:, :, :], ACT.Copy).then_inc(w_hi, 1)

        def make_lo(pool, n, s):
            pool.wait_ge(w_hi, n + 1)
            pool.tensor_tensor(wlo[s][:, :, :], raw[s][:, :, :], whi[s][:, :, :].bitcast(F32),
                               ALU.subtract).then_inc(w_lo, 1)

        def unit(pe, n, s, dst, rhs_hi, rhs_lo, start=True, stop=True, before_chunk=None):
            pe.wait_ge(w_lo, n + 1)
            for c in range(3):
                if before_chunk:
                    before_chunk(c)
                for k in range(KD):
                    for w, r in ((whi[s], rhs_hi), (whi[s], rhs_lo), (wlo[s], rhs_hi)):
                        mm = pe.matmul(ps[:, 3 * dst + c, 0:CH], w[:, k, :], r(k)[:, c * CH:(c + 1) * CH],
                                       start=start and k == 0 and w is whi[s] and r is rhs_hi,
                                       stop=stop and k == KD - 1 and w is wlo[s])
            mm.then_inc(w_used, 1)

        def h_hi(k):
            return Hhi[:, k, :]

        def h_lo(k):
            return Hlo[:, k, :]

        class Norm:
            sq_ready, sum_ready, total, std_ready = sem("n_sq"), sem("n_sum"), sem("n_total"), sem("n_std")
            rstd_ready, h_ready, hi_ready, lo_ready = sem("n_rstd"), sem("n_h"), sem("n_hi"), sem("n_lo")

            def __init__(self, turn):
                self.t, self.o = KD * turn, turn

        norms = [Norm(i) for i in range(3)]
        nh = [place(f"nh{s}", [P, T], F32, slot(40 + s)) for s in range(2)]

        def norm_square(act, nm, k, ready, y):
            act.wait_ge(*ready)
            act.wait_ge(nm.sum_ready, nm.t + k)
            act.activation(sq[:, :], y, ACT.Square).then_inc(nm.sq_ready, 1)

        def norm_add(pool, nm, k, first):
            pool.wait_ge(nm.sq_ready, nm.t + k + 1)
            if first:
                pool.tensor_scalar(ssum[:, :], sq[:, :], 1.0, 1.0, ALU.mult, ALU.mult).then_inc(nm.sum_ready, 1)
            else:
                pool.wait_ge(nm.sum_ready, nm.t + k)
                pool.tensor_tensor(ssum[:, :], ssum[:, :], sq[:, :], ALU.add).then_inc(nm.sum_ready, 1)

        def norm_total(pe, nm):
            pe.wait_ge(nm.sum_ready, nm.t + KD)
            for c in range(3):
                mm = pe.matmul(ps[:, c, 0:CH], ones[:, :], ssum[:, c * CH:(c + 1) * CH], start=True, stop=True)
            mm.then_inc(nm.total, 1)

        def norm_total_after(pe, op, nm):
            for d in range(2):
                pe.wait_ge(op.y[d], op.b + KD // 2)
            norm_total(pe, nm)

        def norm_std(act, nm):
            act.wait_ge(nm.total, nm.o + 1)
            act.activation(chunks(std[:, :]), pset(0), ACT.Sqrt, scale=1.0 / D, bias=eps_rms).then_inc(nm.std_ready, 1)

        def norm_rstd(dve, nm):
            dve.wait_ge(nm.std_ready, nm.o + 1)
            dve.reciprocal(std[:, :], std[:, :]).then_inc(nm.rstd_ready, 1)

        def norm_apply(dve, nm, k, gcol):
            dve.wait_ge(nm.rstd_ready, nm.o + 1)
            if k >= 2:
                dve.wait_ge(nm.lo_ready, nm.t + k - 1)
            dve.scalar_tensor_tensor(out=nh[k % 2][:, :], in0=Y[:, k, :], scalar=cols[:, gcol + k:gcol + k + 1],
                                     in1=std[:, :], op0=ALU.mult, op1=ALU.mult).then_inc(nm.h_ready, 1)

        def norm_hi(act, nm, k):
            act.wait_ge(nm.h_ready, nm.t + k + 1)
            act.activation(Hhi[:, k, :], nh[k % 2][:, :], ACT.Copy).then_inc(nm.hi_ready, 1)

        def norm_lo(pool, nm, k):
            pool.wait_ge(nm.hi_ready, nm.t + k + 1)
            pool.tensor_tensor(Hlo[:, k, :], nh[k % 2][:, :], Hhi[:, k, :].bitcast(F32),
                               ALU.subtract).then_inc(nm.lo_ready, 1)

        NXT = QT + 1
        xin = place("xin", [P, NXT, D], F32, slot(16))
        vecs = place("vecs", [N_COLS, P], F32, slot(26))
        dwin = place("dwin", [TAPS, E], F32, slot(27))
        lamv = place("lamv", [1, 4, HD], F32, slot(29))
        lamt = place("lamt", [1, 2, HD], F32, slot(30))
        lams = place("lams", [1, 8], F32, slot(31))
        x_in = [sem(f"x_in{t}") for t in range(NXT)]
        small_in, vec_in, dw_in, lam_in = sem("small_in"), sem("vec_in"), sem("dw_in"), sem("lam_in")
        setup = sem("setup")
        x_turned = sem("x_turned")
        xe_act, xe_dve = sem("x_evac_act"), sem("x_evac_dve")
        cols_turned, cols_ready, dw_turned, dw_ready = sem("cols_turned"), sem("cols_ready"), sem("dw_turned"), sem("dw_ready")
        lam_exp, lam_row, lam_all = sem("lam_exp"), sem("lam_row"), sem("lam_all")
        lam_sum = sem("lam_sum")
        res_out = [sem("res_out0"), sem("res_out1")]

        def tok_rows(t):
            return P if t < QT else NS_TOK

        with nc.Block() as block:
            @block.sync
            def _(sp):
                sp.dma_start(small[:, :], a["c_small"]).then_inc(small_in, 16)
                for t in range(QT):
                    sp.dma_start(xin[:, t, :], a["x_prompt"][0, t * P:(t + 1) * P, :]).then_inc(x_in[t], 16)
                sp.dma_start(xin[0:NS_TOK, QT, :], a["x_sample"].rearrange("b t d -> (b t) d")).then_inc(x_in[QT], 16)
                for s, kind in ((0, 0), (1, 1)):
                    sp.dma_start(raw[s][:, :, :], conv_src(0, kind)).then_inc(raw_in[s], 16)
                for r, name, n in ((C_NG1, "norm_g", 16), (C_FNG, "final_norm_g", 8), (C_DWB, "conv_dw_b", 16),
                                   (C_LNG, "conv_ln_g", 16), (C_LNB, "conv_ln_b", 16), (C_SUB, "attn_subln_g", 1)):
                    v = a[name] if name == "final_norm_g" else a[name].rearrange("l d -> (l d)")
                    sp.dma_start(vecs[r:r + n, :], v.rearrange("(k p) -> k p", p=P)).then_inc(vec_in, 16)
                sp.dma_start(dwin[:, :], a["conv_dw_w"][0]).then_inc(dw_in, 16)
                for i, name in enumerate(("attn_lambda_q1", "attn_lambda_k1", "attn_lambda_q2", "attn_lambda_k2")):
                    sp.dma_start(lamv[:, i, :], a[name]).then_inc(lam_in, 16)
                sp.wait_ge(xe_act, NXT)
                sp.wait_ge(xe_dve, NXT)
                sp.dma_start(res_d[0], Y[:, :, :]).then_inc(res_out[0], 16)
                sp.wait_ge(res_out[0], 16)

            @block.tensor
            def _(pe):
                pe.wait_ge(small_in, 16)
                for t in range(NXT):
                    n = tok_rows(t)
                    pe.wait_ge(x_in[t], 16)
                    if t >= 3:
                        pe.wait_ge(xe_act, t - 2)
                        pe.wait_ge(xe_dve, t - 2)
                    for k in range(KD):
                        mm = pe.transpose(ps[:, 2 * (t % 3) + k // 4, (k % 4) * P:(k % 4) * P + n],
                                          xin[0:n, t, k * P:(k + 1) * P], ident[0:n, 0:n])
                    mm.then_inc(x_turned, 1)
                pe.wait_ge(vec_in, 96)
                pe.transpose(ps[:, 6, 0:N_COLS], vecs[:, :], ident[0:N_COLS, 0:N_COLS]).then_inc(cols_turned, 1)
                pe.wait_ge(dw_in, 16)
                for j in range(JT):
                    mm = pe.transpose(ps[:, 7, TAPS * j:TAPS * (j + 1)], dwin[:, j * P:(j + 1) * P], ident[0:TAPS, 0:TAPS])
                mm.then_inc(dw_turned, 1)
                pe.wait_ge(setup, 2)
                pe.wait_ge(lam_row, 1)
                pe.wait_ge(cols_ready, 1)
                pe.matmul(ps[:, 6, 0:2], ones[0:1, :], lams[0:1, 4:6], start=True, stop=True).then_inc(lam_all, 1)
                pe.wait_ge(xe_act, NXT)
                pe.wait_ge(xe_dve, NXT)
                norm_total(pe, norms[0])

            @block.scalar
            def _(act):
                for t in range(NXT):
                    n = tok_rows(t)
                    act.wait_ge(x_turned, t + 1)
                    act.activation(Y[:, 0:4, t * P:t * P + n],
                                   ps[:, 2 * (t % 3), :].rearrange("p (k n) -> p k n", k=4)[:, :, 0:n],
                                   ACT.Copy).then_inc(xe_act, 1)
                act.wait_ge(cols_turned, 1)
                act.activation(cols[:, :], ps[:, 6, 0:N_COLS], ACT.Copy).then_inc(cols_ready, 1)
                act.wait_ge(dw_turned, 1)
                act.activation(dww[:, :, :], ps[:, 7, 0:JT * TAPS].rearrange("p (j k) -> p j k", j=JT),
                               ACT.Copy).then_inc(dw_ready, 1)
                act.wait_ge(lam_sum, 2)
                act.activation(lams[0:1, 2:4], lams[0:1, 0:2], ACT.Exp).then_inc(lam_exp, 1)
                act.wait_ge(xe_act, NXT)
                for k in range(KD):
                    norm_square(act, norms[0], k, (xe_dve, NXT), Y[:, k, :])
                norm_std(act, norms[0])
                for n in range(2):
                    make_hi(act, n, n % 2, 1, reused=False)
                for k in range(KD):
                    norm_hi(act, norms[0], k)

            @block.vector
            def _(dve):
                dve.memset(ones[:, :], 1.0).then_inc(setup, 1)
                dve.memset(eps_rms, RMS_EPS).then_inc(setup, 1)
                dve.memset(eps_ln, LN_EPS).then_inc(setup, 1)
                for t in range(NXT):
                    n = tok_rows(t)
                    dve.wait_ge(x_turned, t + 1)
                    dve.tensor_copy(Y[:, 4:8, t * P:t * P + n],
                                    ps[:, 2 * (t % 3) + 1, :].rearrange("p (k n) -> p k n", k=4)[:, :, 0:n]
                                    ).then_inc(xe_dve, 1)
                dve.wait_ge(lam_in, 64)
                for i in range(2):
                    dve.tensor_tensor(lamt[:, i, :], lamv[:, 2 * i, :], lamv[:, 2 * i + 1, :], ALU.mult
                                      ).then_inc(dve_step.sem, dve_step.up())
                dve.wait_ge(dve_step.sem, dve_step.now())
                for i in range(2):
                    dve.tensor_reduce(lams[0:1, i:i + 1], lamt[:, i, :], AX.X, ALU.add).then_inc(lam_sum, 1)
                dve.wait_ge(lam_exp, 1)
                dve.tensor_tensor(lams[0:1, 6:7], lams[0:1, 3:4], lams[0:1, 2:3], ALU.subtract
                                  ).then_inc(dve_step.sem, dve_step.up())
                dve.wait_ge(dve_step.sem, dve_step.now())
                for i in range(2):
                    dve.tensor_scalar(lams[0:1, 4 + i:5 + i], lams[0:1, 6:7], -LAM_INIT, None, ALU.add
                                      ).then_inc(dve_step.sem, dve_step.up())
                dve.wait_ge(dve_step.sem, dve_step.now())
                dve.sem_inc(lam_row, 1)
                dve.wait_ge(lam_all, 1)
                dve.tensor_copy(neglam, ps[:, 6, 0:1]).then_inc(dve_step.sem, dve_step.up())
                dve.wait_ge(cols_ready, 1)
                dve.tensor_scalar(subg, cols[:, C_SUB:C_SUB + 1], 1.0 - LAM_INIT, None, ALU.mult
                                  ).then_inc(dve_step.sem, dve_step.up())
                dve.wait_ge(small_in, 16)
                dve.wait_ge(dve_step.sem, dve_step.now())
                dve.scalar_tensor_tensor(out=rowcoef, in0=cc[:, 1:2], scalar=neglam, in1=cc[:, 0:1],
                                         op0=ALU.mult, op1=ALU.add).then_inc(dve_step.sem, dve_step.up())
                norm_rstd(dve, norms[0])
                for k in range(KD):
                    norm_apply(dve, norms[0], k, C_NG1)

            @block.gpsimd
            def _(pool):
                for k in range(KD):
                    norm_add(pool, norms[0], k, k == 0)
                for n in range(2):
                    make_lo(pool, n, n % 2)
                for k in range(KD):
                    norm_lo(pool, norms[0], k)

        at = slot(32)
        U = [place(f"U{s}", [P, NP_TOK + P], F32, at) for s in range(2)]
        sigb = place("sigb", [P, T], F32, at)
        odd = place("odd", [P, NP_TOK], F32, at)
        pacc = place("pool_acc", [P, NP_TOK], F32, at)
        prod = [place(f"prod{s}", [P, NP_TOK], F32, at) for s in range(2)]
        sg = [place(f"sg{s}", [P, T], F32, at) for s in range(2)]
        smp = place("smp", [P, NB, NT, TAPS], F32, slot(46))
        win = place("win", [P, NB, WIN], F32, at)
        stin = [place(f"st_in{s}", [P - 8, 2, P], F32, at) for s in range(2)]
        stout = place("st_out", [PAD + NS_TOK, E], F32, at)
        assert at[0] <= slot(45)[0]
        SR = NB * PAD // 2
        st_src = a["state_conv"][0].rearrange("b r c -> (b r) c").rearrange("(h p) c -> p h c", p=SR)

        sig_done, u_done, sg_done = sem("sig_done"), sem("u_done"), sem("sg_done")
        st_loaded = [sem("st_loaded0"), sem("st_loaded1")]
        st_turned, win_state, win_ready, smp_read = sem("st_turned"), sem("win_state"), sem("win_ready"), sem("smp_read")
        prod_ready, prod_free, pacc_ready, merged = sem("prod_ready"), sem("prod_free"), sem("pacc_ready"), sem("merged")
        u_turned, stout_ready = sem("u_turned"), sem("stout_ready")
        sg_out = [sem("sg_out0"), sem("sg_out1")]
        st_out = sem("st_out")
        keep_out = sem("keep_out")
        DVE_TAPS = list(range(POOL_TAPS, TAPS))
        win_ap = win[:, :, :]
        part_step = win_ap.ap[0][0]
        windows = bass.AP(win_ap.tensor, win_ap.offset, [[part_step, P], [WIN, NB], [1, NT], [1, TAPS]])

        with nc.Block() as block:
            @block.sync
            def _(sp):
                for s in range(2):
                    sp.dma_start(stin[s][0:SR, :, :], st_src[:, :, s * P:(s + 1) * P]).then_inc(st_loaded[s], 16)
                sp.dma_start(o["conv_state_sample"][0, :, 0:PAD - NT, :], a["state_conv"][0, :, NT:PAD, :]
                             ).then_inc(keep_out, 16)

                def spill(i, s):
                    sp.wait_ge(sg_done, 2 * i + s + 1)
                    sp.dma_start(gate_d[0][2 * i + s], sg[s][:, :]).then_inc(sg_out[s], 16)

                def body(i, last=False):
                    col = i * 2 * P if last else sp.snap(i * 2 * P)
                    for m in range(2, 8):
                        if last and m >= 6:
                            src = out_src(w_cout, 0, m - 6)
                        else:
                            src = conv_src(col + m // 3 * P, m % 3)
                        load_unit(sp, 6 * i + m, m % 2, src)
                        if m in (3, 7) and not last:
                            s = m // 4
                            sp.wait_ge(st_turned, 2 * i + s + 1)
                            sp.dma_start(stin[s][0:SR, :, :], st_src[:, :, bass.ds((2 * i + 2 + s) * P, P)]
                                         ).then_inc(st_loaded[s], 16)
                    spill(i, 0)
                    spill(i, 1)

                with sp.Fori(0, JT // 2 - 1) as i:
                    body(i)
                body(JT // 2 - 1, last=True)
                sp.wait_ge(stout_ready, JT)
                sp.dma_start(o["conv_state_prompt"][0, 0], stout[0:PAD, :]).then_inc(st_out, 16)
                for b in range(NB):
                    sp.dma_start(o["conv_state_sample"][0, b, PAD - NT:PAD, :],
                                 stout[PAD + NT * b:PAD + NT * (b + 1), :]).then_inc(st_out, 16)
                for s in range(2):
                    sp.wait_ge(sg_out[s], 16 * JT // 2)
                sp.wait_ge(st_out, 16 * (NB + 1))
                sp.wait_ge(keep_out, 16)

            @block.tensor
            def _(pe):
                pe.wait_ge(Norm.lo_ready, norms[0].t + KD)
                with pe.Fori(0, JT // 2) as i:
                    for s in range(2):
                        j = 2 * i + s
                        pe.wait_ge(st_loaded[s], 16 * (i + 1))
                        pe.wait_ge(win_state, j)
                        for h in range(2):
                            mm = pe.transpose(ps[:, 6, h * SR:(h + 1) * SR], stin[s][0:SR, h, :], ident[0:SR, 0:SR])
                        mm.then_inc(st_turned, 1)
                        n, e = 6 * i + 3 * s, s
                        pe.wait_ge(u_done, j)
                        unit(pe, n, e, e, h_hi, h_lo)
                        pe.wait_ge(sg_done, j)
                        unit(pe, n + 1, 1 - e, 1 - e, h_hi, h_lo)
                        pe.wait_ge(sig_done, j + 1)
                        unit(pe, n + 2, e, e, h_hi, h_lo)
                        pe.wait_ge(u_done, j + 1)
                        pe.wait_ge(stout_ready, j)
                        pe.transpose(ps[:, 7, 0:P], U[s][:, NP_TOK:NP_TOK + P], ident).then_inc(u_turned, 1)

            @block.scalar
            def _(act):
                with act.Fori(0, JT // 2) as i:
                    for s in range(2):
                        j, n, e = 2 * i + s, 6 * i + 3 * s, s

                        def products(lo, hi):
                            for q in range(lo, hi):
                                r = s * POOL_TAPS + q
                                act.wait_ge(prod_free, i * 2 * POOL_TAPS + r + 1)
                                act.activation(prod[r % 2][:, :], U[s][:, q:q + NP_TOK], ACT.Copy,
                                               scale=dww[:, bass.ds(j, 1), q]).then_inc(prod_ready, 1)

                        make_hi(act, n + 2, e, 3 * i + (3 * s + 2) // 2 + 1)
                        act.wait_ge(w_used, n + 1)
                        act.wait_ge(u_done, j)
                        act.activation(chunks(sigb[:, :]), pset(e), ACT.Sigmoid).then_inc(sig_done, 1)
                        act.wait_ge(st_turned, j + 1)
                        act.wait_ge(smp_read, j)
                        act.activation(win[:, :, 0:PAD], ps[:, 6, 0:NB * PAD].rearrange("p (b r) -> p b r", b=NB),
                                       ACT.Copy).then_inc(win_state, 1)
                        make_hi(act, n + 3, 1 - e, 3 * i + (3 * s + 3) // 2 + 1)
                        act.wait_ge(u_done, j + 1)
                        products(0, POOL_FIRST)
                        make_hi(act, n + 4, e, 3 * i + (3 * s + 4) // 2 + 1)
                        act.wait_ge(w_used, n + 3)
                        act.wait_ge(sg_out[s], 16 * i)
                        act.activation(chunks(sg[s][:, :]), pset(e), ACT.Silu).then_inc(sg_done, 1)
                        products(POOL_FIRST, POOL_TAPS)

            @block.gpsimd
            def _(pool):
                pool.sem_inc(prod_free, 2)
                with pool.Fori(0, JT // 2) as i:
                    for s in range(2):
                        j, n, e = 2 * i + s, 6 * i + 3 * s, s

                        def adds(lo, hi):
                            for q in range(max(lo, 1), hi):
                                r = i * 2 * POOL_TAPS + s * POOL_TAPS + q
                                pool.wait_ge(prod_ready, r + 1)
                                if q == 1:
                                    pool.wait_ge(merged, j)
                                    pool.tensor_tensor(pacc[:, :], prod[0][:, :], prod[1][:, :], ALU.add
                                                       ).then_inc(prod_free, 2)
                                else:
                                    pool.wait_ge(prod_free, r + 2)
                                    pool.tensor_tensor(pacc[:, :], pacc[:, :], prod[q % 2][:, :], ALU.add
                                                       ).then_inc(prod_free, 1)

                        make_lo(pool, n + 2, e)
                        make_lo(pool, n + 3, 1 - e)
                        adds(0, POOL_FIRST)
                        make_lo(pool, n + 4, e)
                        adds(POOL_FIRST, POOL_TAPS)

            @block.vector
            def _(dve):
                for s in range(2):
                    dve.memset(U[s][:, 0:PAD], 0.0).then_inc(dve_step.sem, dve_step.up())
                    dve.memset(U[s][:, PAD + T:NP_TOK + P], 0.0).then_inc(dve_step.sem, dve_step.up())
                dve.memset(csum[:, :], 0.0).then_inc(dve_step.sem, dve_step.up())
                per_tile = 3 + len(DVE_TAPS) + 2
                with dve.Fori(0, JT // 2) as i:
                    dve_step.enter(i, 0, 2 * per_tile)
                    for s in range(2):
                        j, n, e = 2 * i + s, 6 * i + 3 * s, s
                        c_p = C[:, bass.ds(j, 1), 0:NP_TOK].rearrange("p o n -> p (o n)")
                        c_s = C[:, bass.ds(j, 1), NP_TOK:T].rearrange("p o n -> p (o n)")
                        c_all = C[:, bass.ds(j, 1), :].rearrange("p o n -> p (o n)")
                        dve.wait_ge(w_used, n + 2)
                        dve.wait_ge(sig_done, j + 1)
                        dve.tensor_tensor(chunks(U[s][:, PAD:PAD + T]), pset(1 - e), chunks(sigb[:, :]),
                                          ALU.mult).then_inc(u_done, 1)
                        dve.wait_ge(u_done, j + 1)
                        dve.tensor_copy(win[:, :, PAD:WIN], U[s][:, PAD + NP_TOK:PAD + T].rearrange(
                            "p (b t) -> p b t", b=NB)).then_inc(dve_step.sem, dve_step.up())
                        dve.wait_ge(win_state, j + 1)
                        dve.wait_ge(dve_step.sem, dve_step.now())
                        w_j = dww[:, bass.ds(j, 1), :].rearrange("p o (x k) -> p (o x) k", x=1)
                        dve.tensor_tensor(smp[:, :, :, :].rearrange("p b t k -> p (b t) k"),
                                          windows.rearrange("p b t k -> p b t k"),
                                          w_j.to_broadcast([P, NS_TOK, TAPS]), ALU.mult).then_inc(smp_read, 1)
                        dve.wait_ge(smp_read, j + 1)
                        dve.tensor_reduce(c_s, smp[:, :, :, :].rearrange("p b t k -> p (b t) k"), AX.X, ALU.add
                                          ).then_inc(dve_step.sem, dve_step.up())
                        dve.wait_ge(dve_step.sem, dve_step.now())
                        bias = cols[:, bass.ds(j + C_DWB, 1)]
                        dve.tensor_scalar(c_s, c_s, bias, None, ALU.add).then_inc(dve_step.sem, dve_step.up())
                        for q, k in enumerate(DVE_TAPS):
                            tgt = odd[:, :] if q % 2 else c_p
                            wk = dww[:, bass.ds(j, 1), k]
                            uk = U[s][:, k:k + NP_TOK]
                            dve.wait_ge(dve_step.sem, dve_step.now(1))
                            if q == 0:
                                dve.tensor_scalar(tgt, uk, wk, bias, ALU.mult, ALU.add
                                                  ).then_inc(dve_step.sem, dve_step.up())
                            elif q == 1:
                                dve.tensor_scalar(tgt, uk, wk, None, ALU.mult
                                                  ).then_inc(dve_step.sem, dve_step.up())
                            else:
                                dve.scalar_tensor_tensor(out=tgt, in0=uk, scalar=wk, in1=tgt, op0=ALU.mult,
                                                         op1=ALU.add).then_inc(dve_step.sem, dve_step.up())
                        dve.wait_ge(u_turned, j + 1)
                        dve.tensor_copy(stout[:, bass.ds(j * P, P)], ps[0:PAD + NS_TOK, 7, 0:P]).then_inc(stout_ready, 1)
                        dve.wait_ge(dve_step.sem, dve_step.now())
                        dve.tensor_tensor(c_p, c_p, odd[:, :], ALU.add).then_inc(dve_step.sem, dve_step.up())
                        dve.wait_ge(dve_step.sem, dve_step.now())
                        dve.wait_ge(prod_free, 2 * i * POOL_TAPS + (s + 1) * POOL_TAPS + 2)
                        dve.tensor_tensor(c_p, c_p, pacc[:, :], ALU.add).then_inc(merged, 1)
                        dve.wait_ge(merged, j + 1)
                        dve.tensor_tensor(csum[:, :], csum[:, :], c_all, ALU.add
                                          ).then_inc(dve_step.sem, dve_step.up())
                    dve_step.leave(JT // 2)

        mean = place("mean", [P, T], F32, slot(32))
        lrstd = place("ln_rstd", [P, T], F32, slot(33))
        tt = [place(f"tt{s}", [P, T], F32, slot(34 + s)) for s in range(4)]
        lsq = [tt[0], tt[1]]
        sgl = [place(f"sgl{s}", [P, T], F32, slot(38 + s)) for s in range(2)]
        csum_turned, mean_ready, xc_ready, lsq_ready, lsq_used = (sem(x) for x in (
            "csum_total", "mean_ready", "xc_ready", "lsq_ready", "lsq_used"))
        lstd_ready, lrstd_ready = sem("lstd_ready"), sem("lrstd_ready")
        z_ready, silu_ready, p_ready, ghi_ready, glo_ready = (sem(x) for x in (
            "z_ready", "silu_ready", "p_ready", "ghi_ready", "glo_ready"))
        sgl_in = [sem("sgl_in0"), sem("sgl_in1")]

        class OutProj:
            res_in = [sem(f"res_in{s}") for s in range(2)]
            y = [sem(f"y_done{s}") for s in range(2)]

            def __init__(self, turn):
                self.b = KD // 2 * turn

        outp = [OutProj(0), OutProj(1)]

        def out_proj_pe(pe, op, n0, ready):
            with pe.Fori(0, KD // 2) as p:
                for q in range(4):
                    d, half = q % 2, q // 2
                    n = n0 + 4 * p + q
                    if half == 0:
                        pe.wait_ge(op.y[d], op.b + p)
                    pe.wait_ge(w_lo, n + 1)
                    for k in range(KD):
                        kk = KD * half + k
                        if d == 0:
                            pe.wait_ge(ready, kk + 1)
                        for w, r in ((whi, Ghi), (whi, Glo), (wlo, Ghi)):
                            for c in range(3):
                                mm = pe.matmul(ps[:, 3 * d + c, 0:CH], w[d][:, k, :],
                                               r[:, kk, c * CH:(c + 1) * CH],
                                               start=(kk == 0 and w is whi and r is Ghi),
                                               stop=(kk == JT - 1 and w is wlo))
                    mm.then_inc(w_used, 1)

        def out_proj_act(act, op, nm, n0, prepare):
            def body(p, ahead):
                for q in range(4):
                    n = n0 + 4 * p + q
                    if q < 2 or ahead:
                        make_hi(act, n + 2, q % 2, (n0 + q + 2) // 2 + 1 + 2 * p)
                    if q >= 2:
                        d = q - 2
                        act.wait_ge(op.y[d], op.b + p + 1)
                        act.wait_ge(nm.sum_ready, nm.t + 2 * p + d)
                        act.activation(sq[:, :], Y[:, bass.ds(2 * p + d, 1), :].rearrange("p o n -> p (o n)"),
                                       ACT.Square).then_inc(nm.sq_ready, 1)
            with act.Fori(0, KD // 2 - 1) as p:
                body(p, True)
            body(KD // 2 - 1, prepare)

        def out_proj_pool(pool, nm, n0, prepare):
            def body(p, first, ahead):
                for q in range(4):
                    n = n0 + 4 * p + q
                    if q < 2 or ahead:
                        make_lo(pool, n + 2, q % 2)
                    if q >= 2:
                        k = 2 * p + q - 2
                        norm_add(pool, nm, k, first and q == 2)
            body(0, True, True)
            with pool.Fori(1, KD // 2 - 1) as p:
                body(p, False, True)
            body(KD // 2 - 1, False, prepare)

        def out_proj_dve(dve, op, n0):
            with dve.Fori(0, KD // 2) as p:
                for d in range(2):
                    dve.wait_ge(w_used, n0 + 4 * p + 3 + d)
                    dve.wait_ge(op.res_in[d], 16 * (op.b + p + 1))
                    y = Y[:, bass.ds(2 * p + d, 1), :].rearrange("p o (c n) -> p (o c) n", c=3)
                    dve.tensor_tensor(y, pset(d), chunks(xres[d][:, :]), ALU.add).then_inc(op.y[d], 1)

        def out_proj_sp(sp, op, n0, w, res, nxt):
            for d in range(2):
                sp.dma_start(xres[d][:, :], res[:, d, :]).then_inc(op.res_in[d], 16)

            def body(p, last=False):
                for q in range(2, 6):
                    if last and q >= 4:
                        if nxt is None:
                            continue
                        src = nxt(q - 4)
                    else:
                        src = out_src(w, p if q < 4 else p + 1, q % 4)
                    load_unit(sp, n0 + 4 * p + q, q % 2, src)
                if not last:
                    for d in range(2):
                        sp.wait_ge(op.y[d], op.b + p + 1)
                        sp.dma_start(xres[d][:, :], res[:, bass.ds(2 * p + 2 + d, 1), :].rearrange("p o n -> p (o n)")
                                     ).then_inc(op.res_in[d], 16)
            with sp.Fori(0, KD // 2 - 1) as p:
                body(p)
            body(KD // 2 - 1, last=True)

        with nc.Block() as block:
            @block.sync
            def _(sp):
                for s in range(2):
                    sp.dma_start(sgl[s][:, :], gate_d[0][s]).then_inc(sgl_in[s], 16)
                with sp.Fori(1, JT // 2) as i:
                    for s in range(2):
                        sp.wait_ge(p_ready, 2 * i + s - 1)
                        sp.dma_start(sgl[s][:, :], gate_d[0][2 * i + s]).then_inc(sgl_in[s], 16)
                out_proj_sp(sp, outp[0], U_COUT, w_cout, res_d[0], lambda q: att_src(q))
                for d in range(2):
                    sp.wait_ge(outp[0].y[d], outp[0].b + KD // 2)
                sp.dma_start(res_d[1], Y[:, :, :]).then_inc(res_out[1], 16)
                sp.wait_ge(res_out[1], 16)

            @block.tensor
            def _(pe):
                for c in range(3):
                    mm = pe.matmul(ps[:, c, 0:CH], ones[:, :], csum[:, c * CH:(c + 1) * CH], start=True, stop=True)
                mm.then_inc(csum_turned, 1)

                def add_square(j, s, first, last):
                    pe.wait_ge(lsq_ready, j + 1)
                    for c in range(3):
                        mm = pe.matmul(ps[:, 3 + c, 0:CH], ones[:, :], lsq[s][:, c * CH:(c + 1) * CH],
                                       start=first, stop=last)
                    mm.then_inc(lsq_used, 1)

                add_square(0, 0, True, False)
                add_square(1, 1, False, False)
                with pe.Fori(1, JT // 2 - 1) as i:
                    for s in range(2):
                        add_square(2 * i + s, s, False, False)
                add_square(JT - 2, 0, False, False)
                add_square(JT - 1, 1, False, True)
                pe.wait_ge(lstd_ready, 1)
                out_proj_pe(pe, outp[0], U_COUT, glo_ready)
                norm_total_after(pe, outp[0], norms[1])

            @block.scalar
            def _(act):
                act.wait_ge(csum_turned, 1)
                act.activation(chunks(mean[:, :]), pset(0), ACT.Copy, scale=1.0 / E).then_inc(mean_ready, 1)
                with act.Fori(0, JT // 2) as i:
                    for s in range(2):
                        j = 2 * i + s
                        act.wait_ge(xc_ready, j + 1)
                        if s == 0:
                            act.wait_ge(lsq_used, 2 * i)
                        act.activation(lsq[s][:, :], C[:, bass.ds(j, 1), :].rearrange("p o n -> p (o n)"),
                                       ACT.Square).then_inc(lsq_ready, 1)
                act.wait_ge(lsq_used, JT)
                act.activation(chunks(lrstd[:, :]), pset(1), ACT.Sqrt, scale=1.0 / E, bias=eps_ln).then_inc(lstd_ready, 1)
                with act.Fori(0, JT // 4) as i:
                    for s in range(4):
                        j = 4 * i + s
                        act.wait_ge(z_ready, j + 1)
                        act.activation(tt[s][:, :], tt[s][:, :], ACT.Silu, scale=cols[:, bass.ds(j + C_LNG, 1)],
                                       bias=cols[:, bass.ds(j + C_LNB, 1)]).then_inc(silu_ready, 1)
                    for s in range(4):
                        j = 4 * i + s
                        act.wait_ge(p_ready, j + 1)
                        act.activation(Ghi[:, bass.ds(j, 1), :].rearrange("p o n -> p (o n)"), tt[s][:, :],
                                       ACT.Copy).then_inc(ghi_ready, 1)
                out_proj_act(act, outp[0], norms[1], U_COUT, True)
                norm_std(act, norms[1])
                for k in range(KD):
                    norm_hi(act, norms[1], k)

            @block.vector
            def _(dve):
                dve.wait_ge(mean_ready, 1)
                with dve.Fori(0, JT) as j:
                    cj = C[:, bass.ds(j, 1), :].rearrange("p o n -> p (o n)")
                    dve.tensor_tensor(cj, cj, mean[:, :], ALU.subtract).then_inc(xc_ready, 1)
                dve.wait_ge(lstd_ready, 1)
                dve.reciprocal(lrstd[:, :], lrstd[:, :]).then_inc(lrstd_ready, 1)
                dve.wait_ge(lrstd_ready, 1)
                dve.wait_ge(xc_ready, JT)
                with dve.Fori(0, JT // 4) as i:
                    for s in range(4):
                        j = 4 * i + s
                        dve.wait_ge(glo_ready, 4 * i)
                        dve.tensor_tensor(tt[s][:, :], C[:, bass.ds(j, 1), :].rearrange("p o n -> p (o n)"),
                                          lrstd[:, :], ALU.mult).then_inc(z_ready, 1)
                    for s in range(4):
                        j = 4 * i + s
                        dve.wait_ge(silu_ready, j + 1)
                        dve.wait_ge(sgl_in[s % 2], 16 * (2 * i + s // 2 + 1))
                        dve.tensor_tensor(tt[s][:, :], tt[s][:, :], sgl[s % 2][:, :], ALU.mult).then_inc(p_ready, 1)
                out_proj_dve(dve, outp[0], U_COUT)
                norm_rstd(dve, norms[1])
                for k in range(KD):
                    norm_apply(dve, norms[1], k, C_NG2)

            @block.gpsimd
            def _(pool):
                with pool.Fori(0, JT // 4) as i:
                    for s in range(4):
                        j = 4 * i + s
                        pool.wait_ge(ghi_ready, j + 1)
                        pool.tensor_tensor(Glo[:, bass.ds(j, 1), :].rearrange("p o n -> p (o n)"), tt[s][:, :],
                                           Ghi[:, bass.ds(j, 1), :].rearrange("p o n -> p (o n)").bitcast(F32),
                                           ALU.subtract).then_inc(glo_ready, 1)
                out_proj_pool(pool, norms[1], U_COUT, True)
                for k in range(KD):
                    norm_lo(pool, norms[1], k)

        cos = place("cos", [P, T], F32, slot(16))
        sin = place("sin", [P, T], F32, slot(17))
        qs = [place(f"qs{s}", [P, T], F32, slot(18 + s)) for s in range(2)]
        qc = [place(f"qc{s}", [P, T], F32, slot(20 + s)) for s in range(2)]
        qr = [place(f"qr{s}", [P, T], F32, slot(22 + s)) for s in range(2)]
        sga = [place(f"sga{s}", [P, T], F32, slot(24 + s)) for s in range(2)]
        at = slot(26)
        rows = [place(f"rows{s}", [P, NXT, P], F32, at) for s in range(2)]
        rsn = [place(f"rsn{s}", [P, T], F32, at) for s in range(2)]
        tab_in = sem("tab_in")
        qs_ready, qc_ready, swapped, rs_ready, qr_ready = (sem(x) for x in (
            "qs_ready", "qc_ready", "swapped", "rs_ready", "qr_ready"))
        qr_out = [sem("qr_out0"), sem("qr_out1")]
        rows_turned, rows_ready, rows_free = sem("rows_turned"), sem("rows_ready"), sem("rows_free")
        rows_out = [sem("rows_out0"), sem("rows_out1")]
        sga_done = sem("sga_done")
        sga_out = [sem("sga_out0"), sem("sga_out1")]
        NR = JT + NG
        NQK = JT + 2 * NG

        def row_dst(kind, g, sample):
            t = o[("k_rows" if kind == 0 else "v_rows") + ("_sample" if sample else "_prompt")]
            if sample:
                return t[0].rearrange("b t g e -> (b t) g e")[:, g, :]
            return t[0, 0].rearrange("(n p) g e -> p n g e", p=P)[:, :, g, :]

        def spill_gate(sp, i, s):
            sp.wait_ge(sga_done, 2 * i + s + 1)
            sp.dma_start(gate_d[1][2 * i + s], sga[s][:, :]).then_inc(sga_out[s], 16)

        def out_rows(sp, v):
            s, kind, g = v % 2, (v - JT) // NG, (v - JT) % NG
            sp.wait_ge(rows_ready, 3 * (v - JT + 1))
            sp.dma_start(row_dst(kind, g, False), rows[s][:, 0:QT, :]).then_inc(rows_out[s], 16)
            sp.dma_start(row_dst(kind, g, True), rows[s][0:NS_TOK, QT, :]).then_inc(rows_out[s], 16)

        def swap_mm(pe, u, s):
            pe.wait_ge(qs_ready, u + 1)
            pe.wait_ge(rs_ready, u)
            for c, b in enumerate((6, 7, 3 * s + 2)):
                mm = pe.matmul(ps[:, b, 0:CH], swap, qs[s][:, c * CH:(c + 1) * CH], start=True, stop=True)
            mm.then_inc(swapped, 1)

        def turn_rows_last(pe, v):
            s = v % 2
            pe.wait_ge(qs_ready, v + 1)
            pe.wait_ge(rows_ready, 3 * (v - JT))
            for t in range(QT):
                mm = pe.transpose(ps[:, 6 + t // 4, (t % 4) * P:(t % 4 + 1) * P], qs[s][:, t * P:(t + 1) * P], ident)
                if t % 4 == 3:
                    mm.then_inc(rows_turned, 1)
            pe.wait_ge(rows_ready, 3 * (v - JT) + 1)
            pe.transpose(ps[0:NS_TOK, 6, 0:P], qs[s][:, NP_TOK:T], ident).then_inc(rows_turned, 1)

        def rows_evac(act, v, last=False):
            s = v % 2
            if v - JT >= 2:
                act.wait_ge(rows_out[s], 32 * ((v - JT) // 2))
            for part in range(3):
                act.wait_ge(rows_turned, 3 * (v - JT) + part + 1)
                if part < 2:
                    act.activation(rows[s][:, 4 * part:4 * part + 4, :],
                                   ps[:, 6 + part, :].rearrange("p (t e) -> p t e", t=4), ACT.Copy
                                   ).then_inc(rows_ready, 1)
                else:
                    b = 6 if last else 3 * (1 - s) + 1
                    act.activation(rows[s][0:NS_TOK, QT, :], ps[0:NS_TOK, b, 0:P], ACT.Copy
                                   ).then_inc(rows_ready, 1)

        with nc.Block() as block:
            @block.sync
            def _(sp):
                sp.dma_start(cos[:, :], a["c_cos"]).then_inc(tab_in, 16)
                sp.dma_start(sin[:, :], a["c_sin"]).then_inc(tab_in, 16)
                with sp.Fori(0, JT // 2) as i:
                    for s in range(2):
                        load_unit(sp, U_ATT + 2 * i + s + 2, s, att_src(2 * i + s + 2))
                    for s in range(2):
                        sp.wait_ge(qr_ready, 2 * i + s + 1)
                        sp.dma_start(q_d[2 * i + s], qr[s][:, :]).then_inc(qr_out[s], 16)
                for u in range(JT, NQK):
                    s = u % 2
                    load_unit(sp, U_ATT + u + 2, s, att_src(u + 2))
                    if JT <= u - 1 < NR:
                        sp.wait_ge(qr_ready, u)
                        sp.dma_start(k_d[u - 1 - JT], qr[1 - s][:, :]).then_inc(qr_out[1 - s], 16)
                    v = u - 2
                    if v >= JT:
                        out_rows(sp, v)
                for u in range(NQK, NQK + 2):
                    load_unit(sp, U_ATT + u + 2, u % 2, att_src(u + 2))
                    out_rows(sp, u - 2)
                def gate(i, last):
                    for s in range(2):
                        if not last:
                            load_unit(sp, U_ATT + NQK + 2 * i + s + 2, s, att_src(NQK + 2 * i + s + 2))
                        else:
                            load_unit(sp, U_ATT + NQK + 2 * i + s + 2, s, out_src(w_aout, 0, s))
                    for s in range(2):
                        spill_gate(sp, i, s)
                for s in range(2):
                    spill_gate(sp, 0, s)
                with sp.Fori(1, JT // 2 - 1) as i:
                    gate(i, False)
                gate(JT // 2 - 1, True)
                for s in range(2):
                    sp.wait_ge(sga_out[s], 16 * JT // 2)
                    sp.wait_ge(qr_out[s], 16 * NR // 2)
                    sp.wait_ge(rows_out[s], 32 * NG)

            @block.tensor
            def _(pe):
                pe.wait_ge(Norm.lo_ready, norms[1].t + KD)

                def proj(u, s, first=False):
                    def before(c):
                        if c == 0 and not first:
                            pe.wait_ge(qs_ready, u - 1)
                        if c == 2 and not first:
                            pe.wait_ge(rs_ready, u - 1)
                    unit(pe, U_ATT + u, s, s, h_hi, h_lo, before_chunk=before)

                proj(0, 0, True)
                proj(1, 1, True)
                swap_mm(pe, 0, 0)
                with pe.Fori(1, JT // 2) as i:
                    for s in range(2):
                        u = 2 * i + s
                        proj(u, s)
                        swap_mm(pe, u - 1, 1 - s)

                def turn_rows(v):
                    s = v % 2
                    src = qr[s] if v < NR else qs[s]
                    if v < NR:
                        pe.wait_ge(qr_ready, v + 1)
                        pe.wait_ge(rs_ready, v + 1)
                    else:
                        pe.wait_ge(qs_ready, v + 1)
                        pe.wait_ge(rs_ready, min(v, NR))
                    pe.wait_ge(rows_ready, 3 * (v - JT))
                    for t in range(QT):
                        mm = pe.transpose(ps[:, 6 + t // 4, (t % 4) * P:(t % 4 + 1) * P],
                                          src[:, t * P:(t + 1) * P], ident)
                        if t % 4 == 3:
                            mm.then_inc(rows_turned, 1)
                    b = 3 * (1 - s) + 1
                    pe.wait_ge(qs_ready, v + 2)
                    pe.transpose(ps[0:NS_TOK, b, 0:P], src[:, NP_TOK:T], ident).then_inc(rows_turned, 1)

                for u in range(JT, NQK + 2):
                    s = u % 2

                    def before(c, u=u):
                        if c == 0:
                            pe.wait_ge(qs_ready, min(u - 1, NQK))
                        if c == 1 and u - 3 >= JT:
                            pe.wait_ge(rows_ready, 3 * (u - 3 - JT + 1))
                        if c == 2:
                            pe.wait_ge(rs_ready, min(u - 1, NR))
                    unit(pe, U_ATT + u, s, s, h_hi, h_lo, before_chunk=before)
                    if u - 2 >= JT:
                        turn_rows(u - 2) if u - 1 < NQK else None
                        if u - 1 < NQK:
                            pe.wait_ge(rows_ready, 3 * (u - 2 - JT) + 2)
                    if u - 1 < NR:
                        swap_mm(pe, u - 1, 1 - s)
                    if u == NQK:
                        turn_rows_last(pe, NQK - 1)

                with pe.Fori(1, JT // 2) as i:
                    for s in range(2):
                        u = NQK + 2 * i + s
                        pe.wait_ge(sga_done, 2 * i + s - 1)
                        unit(pe, U_ATT + u, s, s, h_hi, h_lo)

            @block.scalar
            def _(act):
                def copy_out(u, s, turn, first=False, scale=1.0):
                    act.wait_ge(w_used, U_ATT + u + 1)
                    make_hi(act, U_ATT + u + 2, s, turn)
                    if not first:
                        act.wait_ge(qr_ready, u - 1)
                    act.activation(chunks(qs[s][:, :]), pset(s), ACT.Copy, scale=scale).then_inc(qs_ready, 1)

                t0 = U_ATT // 2 + 2
                copy_out(0, 0, t0, True, SCALE)
                copy_out(1, 1, t0, True, SCALE)
                with act.Fori(1, JT // 2) as i:
                    for s in range(2):
                        copy_out(2 * i + s, s, t0 + i, scale=SCALE)
                for u in range(JT, NQK):
                    s = u % 2
                    act.wait_ge(w_used, U_ATT + u + 1)
                    make_hi(act, U_ATT + u + 2, s, t0 + u // 2)
                    act.wait_ge(qr_ready, min(u - 1, NR))
                    if u - 2 >= NR:
                        act.wait_ge(rows_turned, 3 * (u - 2 - JT + 1))
                    act.activation(chunks(qs[s][:, :]), pset(s), ACT.Copy).then_inc(qs_ready, 1)
                    if u - 2 >= JT:
                        rows_evac(act, u - 2)

                def silu(i, s, turn, u):
                    act.wait_ge(w_used, U_ATT + u + 1)
                    make_hi(act, U_ATT + u + 2, s, turn)
                    act.wait_ge(sga_out[s], 16 * i)
                    act.activation(chunks(sga[s][:, :]), pset(s), ACT.Silu).then_inc(sga_done, 1)

                act.wait_ge(w_used, U_ATT + NQK + 1)
                rows_evac(act, NQK - 2)
                silu(0, 0, t0 + NQK // 2, NQK)
                rows_evac(act, NQK - 1, True)
                silu(0, 1, t0 + NQK // 2, NQK + 1)
                with act.Fori(1, JT // 2) as i:
                    for s in range(2):
                        silu(i, s, t0 + NQK // 2 + i, NQK + 2 * i + s)

            @block.gpsimd
            def _(pool):
                pool.wait_ge(tab_in, 32)

                def rot(u, s, first=False):
                    make_lo(pool, U_ATT + u + 2, s)
                    pool.wait_ge(qs_ready, u + 1)
                    if not first:
                        pool.wait_ge(qr_ready, u - 1)
                    pool.tensor_tensor(qc[s][:, :], qs[s][:, :], cos[:, :], ALU.mult).then_inc(qc_ready, 1)
                rot(0, 0, True)
                rot(1, 1, True)
                with pool.Fori(1, JT // 2) as i:
                    for s in range(2):
                        rot(2 * i + s, s)
                for u in range(JT, NR):
                    rot(u, u % 2)
                with pool.Fori(NR // 2, (NQK + JT) // 2) as i:
                    for s in range(2):
                        make_lo(pool, U_ATT + 2 * i + s + 2, s)

            @block.vector
            def _(dve):
                dve.wait_ge(tab_in, 32)

                def rot(u, s, out_turn):
                    dve.wait_ge(swapped, u + 1)
                    for c, b in enumerate((6, 7, 3 * s + 2)):
                        ins = dve.tensor_tensor(rsn[s][:, c * CH:(c + 1) * CH], ps[:, b, 0:CH],
                                                sin[:, c * CH:(c + 1) * CH], ALU.mult)
                        if c == 2:
                            ins.then_inc(rs_ready, 1)
                    dve.wait_ge(rs_ready, u + 1)
                    dve.wait_ge(qc_ready, u + 1)
                    dve.wait_ge(qr_out[s], out_turn)
                    dve.tensor_tensor(qr[s][:, :], qc[s][:, :], rsn[s][:, :], ALU.add).then_inc(qr_ready, 1)
                with dve.Fori(0, JT // 2) as i:
                    for s in range(2):
                        rot(2 * i + s, s, 16 * i)
                for u in range(JT, NR):
                    if u - 2 >= JT:
                        dve.wait_ge(rows_turned, 3 * (u - 2 - JT) + 3)
                    rot(u, u % 2, 16 * (u // 2))

        OG = place("OG", [P, JT, T], F32, slot(16))
        kraw = place("kraw", [P, NP_TOK], F32, slot(32))
        vraw = place("vraw", [P, QT, P], F32, slot(33))
        khi = place("khi", [P, NP_TOK], F32R, slot(34))
        klo = place("klo", [P, NP_TOK], F32R, slot(35))
        vhi = place("vhi", [P, QT, P], F32R, slot(36))
        vlo = place("vlo", [P, QT, P], F32R, slot(37))
        qraw = [place(f"qraw{s}", [P, NP_TOK], F32, slot(38 + s)) for s in range(2)]
        qhi = [place(f"qhi{s}", [P, NP_TOK], F32R, slot(40 + s)) for s in range(2)]
        qlo = [place(f"qlo{s}", [P, NP_TOK], F32R, slot(42 + s)) for s in range(2)]
        sgh = [place(f"sgh{s}", [P, NP_TOK], F32, slot(44 + s)) for s in range(2)]
        at = slot(0)
        aThi = [place("aThi0", [P, 4, 512], F32R, at), place("aThi1", [P, 8, 512], F32R, at)]
        aTlo = [place("aTlo0", [P, 4, 512], F32R, at), place("aTlo1", [P, 8, 512], F32R, at)]
        osq = place("osq", [P, NP_TOK], F32, at)
        ostd = place("ostd", [P, NP_TOK], F32, at)
        identr = place("identr", [P, P], F32R, at)
        causalr = place("causalr", [P, P], F32R, at)
        stats = place("stats", [P, 3, 8], F32, at)
        p1 = [place(f"p1_{s}", [P, NP_TOK], F32, [raw_at[s]]) for s in range(2)]
        p0 = [place("p0_0", [P, NP_TOK], F32, at), place("p0_1", [P, NP_TOK], F32, at),
              place("p0_2", [P, NP_TOK], F32, slot(46))]
        assert at[0] <= slot(16)[0] and slot(46)[0] + 4 * NP_TOK <= 229344
        kraw_in, vraw_in = sem("kraw_in"), sem("vraw_in")
        qraw_in = [sem("qraw_in0"), sem("qraw_in1")]
        sgh_in = [sem("sgh_in0"), sem("sgh_in1")]
        consts_r, kvhi_ready, kv_ready, qhi_ready, qlo_ready = (sem(x) for x in (
            "consts_r", "kvhi_ready", "kv_ready", "qhi_ready", "qlo_ready"))
        s_done, mx_done, exp_done, rc_done, pn_done, comb_done, t_done = (sem(x) for x in (
            "scores_done", "max_done", "exp_done", "recip_done", "p1_scaled", "a_ready", "a_turned"))
        tg_done, hi_done, lo_done, pv_done, oev, n_done, nstd_done, og_done = (sem(x) for x in (
            "turn_group", "aT_hi", "aT_lo", "pv_done", "o_copied", "osq_total", "ostd_ready", "og_done"))
        p1_begun = sem("p1_begun")
        NX = GH * QT

        def tgroups(x):
            j, i = divmod(x, QT)
            first = 12 * j + (i if i < 4 else 4 + 2 * (i - 4))
            return [(first + n, 4 * n, min(4, i + 1 - 4 * n)) for n in range(i // 4 + 1)]

        def score_ap(i, c):
            w = P * (i + 1)
            if i < 4:
                return ps[:, 2 * (i % 2) + c, 0:w]
            return ps[:, 2 * c:2 * c + 2, :].rearrange("p b n -> p (b n)")[:, 0:w]

        with nc.Block() as block:
            @block.sync
            def _(sp):
                def load_q(h, s):
                    sp.dma_start(qraw[s][:, :], q_d[h][:, 0:NP_TOK]).then_inc(qraw_in[s], 16)

                def load_sg(h, s):
                    sp.dma_start(sgh[s][:, :], gate_d[1][h][:, 0:NP_TOK]).then_inc(sgh_in[s], 16)

                def load_kv(g):
                    sp.dma_start(kraw[:, :], k_d[g][:, 0:NP_TOK]).then_inc(kraw_in, 16)
                    sp.dma_start(vraw[:, :, :], v_rows(g)).then_inc(vraw_in, 16)

                def v_rows(g):
                    v = o["v_rows_prompt"][0, 0].rearrange("(n p) g e -> p n (g e)", p=P)
                    return v[:, :, bass.ds(g * VD, VD)]

                load_kv(0)
                for s in range(2):
                    load_q(s, s)
                    load_sg(s, s)

                def body(g, last=False):
                    if not last:
                        sp.wait_ge(kv_ready, 2 * g + 2)
                        load_kv(g + 1)
                    for j in range(GH - 2 if last else GH):
                        sp.wait_ge(qlo_ready, GH * g + j + 1)
                        load_q(GH * g + j + 2, j % 2)
                        sp.wait_ge(og_done, GH * g + j + 1)
                        load_sg(GH * g + j + 2, j % 2)
                with sp.Fori(0, NG - 1) as g:
                    body(g)
                body(NG - 1, True)

            @block.tensor
            def _(pe):
                pe.wait_ge(consts_r, 2)
                with pe.Fori(0, NG) as g:
                    pe.wait_ge(kv_ready, 2 * g + 2)

                    def scores(x, c):
                        j, i = divmod(x, QT)
                        s, w = j % 2, P * (i + 1)
                        if c == 0 and i == 0:
                            pe.wait_ge(qlo_ready, GH * g + j + 1)
                        if x >= 2:
                            if i < 2:
                                need = (x - 1, 0) if i == 0 else (x - 2, 1)
                            elif i < 4:
                                need = (x - 2, c)
                            elif i == 4:
                                need = (x - 2, 1) if c == 0 else (x - 1, 1)
                            else:
                                need = (x - 1, c)
                            pe.wait_ge(exp_done, 2 * NX * g + 2 * need[0] + need[1] + 1)
                        dst = score_ap(i, c)
                        rows_ = slice(HD * c, HD * c + HD)
                        for n, (ql, kr) in enumerate(((qhi, khi), (qhi, klo), (qlo, khi))):
                            for c0 in range(0, w, 512):
                                c1 = min(w, c0 + 512)
                                pe.matmul(dst[:, c0:c1], ql[s][rows_, i * P:(i + 1) * P], kr[rows_, c0:c1],
                                          start=n == 0, stop=n == 2 and c1 < w)
                        pe.matmul(dst[:, i * P:w], identr[:, :], causalr[:, :], start=False, stop=True
                                  ).then_inc(s_done, 1)

                    def turn(x):
                        j, i = divmod(x, QT)
                        pe.wait_ge(comb_done, NX * g + x + 1)
                        for tg, b0, nb in tgroups(x):
                            if tg >= 2:
                                pe.wait_ge(lo_done, 12 * GH * g + tg - 1)
                            for b in range(b0, b0 + nb):
                                mm = pe.transpose(ps[:, 4 + tg % 2, (b - b0) * P:(b - b0 + 1) * P],
                                                  p0[x % 3][:, b * P:(b + 1) * P], ident)
                            mm.then_inc(tg_done, 1)

                    def pv(j, half):
                        pe.wait_ge(lo_done, 12 * GH * g + 12 * j + (4 if half == 0 else 12))
                        pe.wait_ge(nstd_done, GH * g + j)
                        nb = 4 + 4 * half
                        for b in range(nb):
                            c0 = max(0, b - 4 * half) * P
                            for n, (v, at_) in enumerate(((vhi, aThi), (vhi, aTlo), (vlo, aThi))):
                                mm = pe.matmul(ps[:, 6 + half, c0:512], v[:, b, :], at_[half][:, b, c0:512],
                                               start=b == 0 and n == 0, stop=b == nb - 1 and n == 2)
                        mm.then_inc(pv_done, 1)

                    def total(j):
                        pe.wait_ge(oev, 2 * (GH * g + j + 1))
                        for half in range(2):
                            mm = pe.matmul(ps[:, 6 + half, :], ones[:, :], osq[:, 512 * half:512 * half + 512],
                                           start=True, stop=True)
                        mm.then_inc(n_done, 1)

                    for x in range(NX + 6):
                        j, i = divmod(x, QT)
                        if x < NX:
                            scores(x, 0)
                            scores(x, 1)
                        if 0 <= x - 2 < NX:
                            turn(x - 2)
                        if i == 5 and j < GH:
                            pv(j, 0)
                        if i == 1 and j >= 1:
                            pv(j - 1, 1)
                        if i == 3 and j >= 1:
                            total(j - 1)

            @block.scalar
            def _(act):
                act.activation(identr[:, :], ident, ACT.Copy).then_inc(consts_r, 1)
                act.activation(causalr[:, :], causal, ACT.Copy).then_inc(consts_r, 1)
                with act.Fori(0, NG) as g:
                    def q_hi(j):
                        s = j % 2
                        act.wait_ge(qraw_in[s], 16 * (2 * g + j // 2 + 1))
                        if j >= 2:
                            act.wait_ge(s_done, 2 * NX * g + 2 * QT * (j - 1))
                        act.activation(qhi[s][:, :], qraw[s][:, :], ACT.Copy).then_inc(qhi_ready, 1)

                    def exp(x, c):
                        j, i = divmod(x, QT)
                        act.wait_ge(mx_done, 2 * NX * g + 2 * x + c + 1)
                        if c == 0 and x >= 3:
                            act.wait_ge(tg_done, 12 * GH * g + tgroups(x - 3)[-1][0] + 1)
                        if c == 1 and x >= 2:
                            act.wait_ge(comb_done, NX * g + x - 1)
                        dst = p0[x % 3] if c == 0 else p1[x % 2]
                        act.activation(dst[:, 0:P * (i + 1)], score_ap(i, c), ACT.Exp,
                                       bias=stats[:, x % 3, c:c + 1],
                                       accum_out=stats[:, x % 3, 2 + c:3 + c]).then_inc(exp_done, 1)

                    def hi(x):
                        j, i = divmod(x, QT)
                        half = i // 4
                        if j >= 1 and i % 4 == 0:
                            act.wait_ge(pv_done, 2 * (GH * g + j - 1) + half + 1)
                        for tg, b0, nb in tgroups(x):
                            act.wait_ge(tg_done, 12 * GH * g + tg + 1)
                            act.activation(aThi[half][:, b0:b0 + nb, (i % 4) * P:(i % 4 + 1) * P],
                                           ps[:, 4 + tg % 2, 0:nb * P].rearrange("p (b n) -> p b n", b=nb),
                                           ACT.Copy).then_inc(hi_done, 1)

                    def o_evac(j, half):
                        act.wait_ge(pv_done, 2 * (GH * g + j) + half + 1)
                        act.wait_ge(n_done, GH * g + j)
                        act.activation(OG[:, bass.ds(GH * g + j, 1), 512 * half:512 * half + 512].rearrange(
                            "p o n -> p (o n)"), ps[:, 6 + half, :], ACT.Copy)
                        act.activation(osq[:, 512 * half:512 * half + 512], ps[:, 6 + half, :], ACT.Square
                                       ).then_inc(oev, 1)

                    act.wait_ge(kraw_in, 16 * (g + 1))
                    act.wait_ge(pv_done, 2 * GH * g)
                    act.activation(khi[:, :], kraw[:, :], ACT.Copy).then_inc(kvhi_ready, 1)
                    act.wait_ge(vraw_in, 16 * (g + 1))
                    act.activation(vhi[:, :, :], vraw[:, :, :], ACT.Copy).then_inc(kvhi_ready, 1)
                    q_hi(0)
                    for x in range(NX + 6):
                        j, i = divmod(x, QT)
                        if x < NX:
                            exp(x, 0)
                            exp(x, 1)
                        if 0 <= x - 2 < NX:
                            hi(x - 2)
                        if i == 4 and j < GH - 1:
                            q_hi(j + 1)
                        if i == 6 and j < GH:
                            o_evac(j, 0)
                        if i == 2 and j >= 1:
                            o_evac(j - 1, 1)
                        if i == 4 and j >= 1:
                            act.wait_ge(n_done, GH * g + j)
                            act.wait_ge(og_done, GH * g + j - 1)
                            act.activation(ostd[:, :], ps[:, 6:8, :].rearrange("p b n -> p (b n)"), ACT.Sqrt,
                                           scale=1.0 / VD, bias=eps_rms).then_inc(nstd_done, 1)

            @block.vector
            def _(dve):
                with dve.Fori(0, NG) as g:
                    dve_step.enter(g, 0, 2 * GH)
                    dve.wait_ge(kvhi_ready, 2 * g + 2)
                    dve.tensor_tensor(klo[:, :], kraw[:, :], khi[:, :].bitcast(F32), ALU.subtract).then_inc(kv_ready, 1)
                    dve.tensor_tensor(vlo[:, :, :], vraw[:, :, :], vhi[:, :, :].bitcast(F32), ALU.subtract
                                      ).then_inc(kv_ready, 1)

                    def recip(x):
                        dve.wait_ge(exp_done, 2 * NX * g + 2 * x + 2)
                        dve.reciprocal(stats[:, x % 3, 4:6], stats[:, x % 3, 2:4]).then_inc(rc_done, 1)

                    def maxes(x):
                        for c in range(2):
                            dve.wait_ge(s_done, 2 * NX * g + 2 * x + c + 1)
                            dve.tensor_reduce(stats[:, x % 3, c:c + 1], score_ap(x % QT, c), AX.X, ALU.max,
                                              negate=True).then_inc(mx_done, 1)

                    def combine(x):
                        w = P * (x % QT + 1)
                        dve.wait_ge(pn_done, NX * g + x + 1)
                        dve.scalar_tensor_tensor(out=p0[x % 3][:, 0:w], in0=p0[x % 3][:, 0:w],
                                                 scalar=stats[:, x % 3, 4:5], in1=p1[x % 2][:, 0:w],
                                                 op0=ALU.mult, op1=ALU.add).then_inc(comb_done, 1)

                    def lo(x):
                        i = x % QT
                        half = i // 4
                        for tg, b0, nb in tgroups(x):
                            dve.wait_ge(hi_done, 12 * GH * g + tg + 1)
                            cs = slice((i % 4) * P, (i % 4 + 1) * P)
                            dve.tensor_tensor(aTlo[half][:, b0:b0 + nb, cs],
                                              ps[:, 4 + tg % 2, 0:nb * P].rearrange("p (b n) -> p b n", b=nb),
                                              aThi[half][:, b0:b0 + nb, cs].bitcast(F32), ALU.subtract
                                              ).then_inc(lo_done, 1)

                    for x in range(NX + 6):
                        j, i = divmod(x, QT)
                        if 0 <= x - 1 < NX:
                            recip(x - 1)
                        if x < NX:
                            maxes(x)
                        if 0 <= x - 1 < NX:
                            combine(x - 1)
                        if 0 <= x - 2 < NX:
                            lo(x - 2)
                        if i == 5 and j >= 1:
                            h = GH * g + j - 1
                            og = OG[:, bass.ds(h, 1), 0:NP_TOK].rearrange("p o n -> p (o n)")
                            dve.wait_ge(nstd_done, h + 1)
                            dve.reciprocal(ostd[:, :], ostd[:, :]).then_inc(dve_step.sem, dve_step.up())
                            dve.wait_ge(dve_step.sem, dve_step.now())
                            dve.scalar_tensor_tensor(out=og, in0=og, scalar=subg, in1=ostd[:, :], op0=ALU.mult,
                                                     op1=ALU.mult).then_inc(dve_step.sem, dve_step.up())
                            dve.wait_ge(dve_step.sem, dve_step.now())
                            dve.wait_ge(sgh_in[(j - 1) % 2], 16 * (2 * g + (j - 1) // 2 + 1))
                            dve.tensor_tensor(og, og, sgh[(j - 1) % 2][:, :], ALU.mult).then_inc(og_done, 1)
                    dve_step.leave(NG)

            @block.gpsimd
            def _(pool):
                with pool.Fori(0, NG) as g:
                    def q_lo(j):
                        s = j % 2
                        pool.wait_ge(qhi_ready, GH * g + j + 1)
                        pool.tensor_tensor(qlo[s][:, :], qraw[s][:, :], qhi[s][:, :].bitcast(F32), ALU.subtract
                                           ).then_inc(qlo_ready, 1)
                    q_lo(0)
                    for x in range(NX):
                        j, i = divmod(x, QT)
                        w = P * (i + 1)
                        pool.wait_ge(rc_done, NX * g + x + 1)
                        pool.sem_inc(p1_begun, 1)
                        pool.tensor_scalar(p1[x % 2][:, 0:w], p1[x % 2][:, 0:w], stats[:, x % 3, 5:6], neglam,
                                           ALU.mult, ALU.mult).then_inc(pn_done, 1)
                        if i == 4 and j < GH - 1:
                            q_lo(j + 1)

        at = slot(0)
        kpage = [place(f"kpage{s}", [P, PAGES, NG * VD], F32, at) for s in range(2)]
        vpage = [place(f"vpage{s}", [P, PAGES, NG * VD], F32, at) for s in range(2)]
        assert at[0] <= slot(16)[0]
        at = slot(32)
        kT = place("kT", [P, 2, PAST], F32, at)
        pd = place("p_dec", [P, PAST + NT], F32, at)
        aTd = place("aT_dec", [P, PAGES, NG * GH * NT], F32, at)
        aTn = place("aT_new", [NT, NG * GH * NT], F32, at)
        qsT = place("q_samples", [P, JT, NS_TOK], F32, at)
        knew = place("k_new", [P, NG, NS_TOK], F32, at)
        vnew = [place(f"v_new{s}", [NT, NG * VD], F32, at) for s in range(2)]
        Qz = place("Qz", [P, NG, P], F32, at)
        zc = place("zc", [P, NG * GH * NT], F32, at)
        snew = place("snew", [P, NT], F32, at)
        st6 = place("stat_dec", [P, 8], F32, at)
        ptab = nc.alloc_sbuf_tensor_at("ptab", [1, NB * PAGES], I32, offset=at[0])
        at[0] += 256
        sgs = place("sg_samples", [P, JT, NS_TOK], F32, at)
        dsq = place("dsq", [P, JT * NS_TOK], F32, at)
        dstd = place("dstd", [P, JT * NS_TOK], F32, at)
        assert at[0] <= slot(46)[0]
        pt_in, qs_in, kn_in, sgs_in = sem("pt_in"), sem("qs_in"), sem("kn_in"), sem("sgs_in")
        page_in = [sem("page_in0"), sem("page_in1")]
        PAGE_DMAS = 2 * PAGES + 1
        qz_zero, qz_ready, kt_turned, kev_act, kev_dve, ds_done = (sem(x) for x in (
            "qz_zero", "qz_ready", "kt_turned", "kev_act", "kev_dve", "dscore_done"))
        dmx, sn_ready, dexp, zc_ready, at_turned, at_ready, dpv_done, do_ready = (sem(x) for x in (
            "dmax", "snew_ready", "dexp", "zc_ready", "aT_turned", "aT_ready", "dpv_done", "do_ready"))
        dsq_ready, dtotal, dstd_ready, dog = sem("dsq_ready"), sem("dtotal"), sem("dstd_ready"), sem("dog")
        n_phys = a["cache_k"].shape[1]

        with nc.Block() as block:
            @block.sync
            def _(sp):
                sp.dma_start(ptab[:, :], a["page_table"].rearrange("(o b) p -> o (b p)", o=1)).then_inc(pt_in, 16)
                sp.dma_start(qsT[:, :, :], q_d.rearrange("j p n -> p j n")[:, :, NP_TOK:T]).then_inc(qs_in, 16)
                sp.dma_start(knew[:, :, :], k_d.rearrange("g p n -> p g n")[:, :, NP_TOK:T]).then_inc(kn_in, 16)
                sp.dma_start(sgs[:, :, :], gate_d[1].rearrange("j p n -> p j n")[:, :, NP_TOK:T]).then_inc(sgs_in, 16)
                sp.wait_ge(pt_in, 16)

                def load(b, s):
                    for page in range(PAGES):
                        n = sp.value_load(ptab[0:1, bass.ds(b * PAGES + page, 1)], min_val=0, max_val=n_phys - 1)
                        for dst, src in ((kpage, "cache_k"), (vpage, "cache_v")):
                            sp.dma_start(dst[s][:, page, :], a[src][0][bass.ds(n, 1)].rearrange(
                                "o p g e -> (o p) (g e)")).then_inc(page_in[s], 16)
                    sp.dma_start(vnew[s][:, :], o["v_rows_sample"][0][bass.ds(b, 1)].rearrange(
                        "o t g e -> (o t) (g e)")).then_inc(page_in[s], 16)
                for s in range(2):
                    load(s, s)
                with sp.Fori(0, NB // 2 - 1) as i:
                    for s in range(2):
                        sp.wait_ge(dpv_done, 2 * i + s + 1)
                        load(2 * i + s + 2, s)

            @block.tensor
            def _(pe):
                with pe.Fori(0, NB // 2) as i:
                    for s in range(2):
                        b = 2 * i + s

                        def turn_pages(g):
                            if g >= 2:
                                pe.wait_ge(ds_done, NG * b + g - 1)
                            for half in range(2):
                                f = 2 * g + half
                                if f >= 3:
                                    e = kev_act if (f - 3) % 2 == 0 else kev_dve
                                    pe.wait_ge(e, NG * b + (f - 3) // 2 + 1)
                                for q in range(4):
                                    mm = pe.transpose(ps[:, 3 + f % 3, q * P:(q + 1) * P],
                                                      kpage[s][:, 4 * half + q, g * VD:(g + 1) * VD], ident)
                                mm.then_inc(kt_turned, 1)

                        def score(g):
                            for half in range(2):
                                pe.wait_ge(kev_act if half == 0 else kev_dve, NG * b + g + 1)
                                pe.matmul(ps[:, half, :], Qz[:, g, :], kT[:, g % 2, 512 * half:512 * half + 512],
                                          start=g == 0, stop=g == NG - 1)
                            pe.matmul(ps[:, 2, 0:NT], Qz[:, g, :], knew[:, g, bass.ds(NT * b, NT)],
                                      start=g == 0, stop=g == NG - 1).then_inc(ds_done, 1)

                        pe.wait_ge(page_in[s], 16 * PAGE_DMAS * (i + 1))
                        turn_pages(0)
                        pe.wait_ge(kn_in, 16)
                        pe.wait_ge(qz_ready, b + 1)
                        for g in range(NG):
                            if g + 1 < NG:
                                turn_pages(g + 1)
                            score(g)
                        pe.wait_ge(zc_ready, b + 1)
                        pe.wait_ge(at_ready, 2 * b)
                        for page in range(PAGES):
                            pe.matmul(ps[:, 6, 64 * page:64 * page + 64], pd[:, page * P:(page + 1) * P], zc[:, :],
                                      start=True, stop=True)
                        pe.matmul(ps[0:NT, 2, 64:128], pd[:, PAST:PAST + NT], zc[:, :], start=True, stop=True
                                  ).then_inc(at_turned, 1)
                        pe.wait_ge(at_ready, 2 * b + 2)
                        pe.wait_ge(do_ready, b)
                        for g in range(NG):
                            cs = slice(16 * g, 16 * g + 16)
                            for page in range(PAGES):
                                pe.matmul(ps[:, 7, cs], vpage[s][:, page, g * VD:(g + 1) * VD], aTd[:, page, cs],
                                          start=page == 0, stop=False)
                            mm = pe.matmul(ps[:, 7, cs], vnew[s][:, g * VD:(g + 1) * VD], aTn[:, cs],
                                           start=False, stop=True)
                        mm.then_inc(dpv_done, 1)
                pe.wait_ge(dsq_ready, 1)
                pe.matmul(ps[:, 0, :], ones[:, :], dsq[:, :], start=True, stop=True).then_inc(dtotal, 1)

            @block.scalar
            def _(act):
                with act.Fori(0, NB) as b:
                    for g in range(NG):
                        act.wait_ge(kt_turned, 2 * NG * b + 2 * g + 1)
                        if g >= 2:
                            act.wait_ge(ds_done, NG * b + g - 1)
                        act.activation(kT[:, g % 2, 0:512], ps[:, 3 + (2 * g) % 3, :], ACT.Copy).then_inc(kev_act, 1)
                    act.wait_ge(dmx, b + 1)
                    act.activation(pd[:, 0:PAST], ps[:, 0:2, :].rearrange("p b n -> p (b n)"), ACT.Exp,
                                   bias=st6[:, 2:3], accum_out=st6[:, 3:4])
                    act.activation(pd[:, PAST:PAST + NT], snew[:, :], ACT.Exp,
                                   bias=st6[:, 2:3], accum_out=st6[:, 4:5]).then_inc(dexp, 1)
                    act.wait_ge(at_turned, b + 1)
                    act.activation(aTd[:, :, :].rearrange("p a n -> p (a n)"), ps[:, 6, :], ACT.Copy
                                   ).then_inc(at_ready, 1)
                    act.wait_ge(dpv_done, b + 1)
                    act.activation(OG[:, :, bass.ds(NP_TOK + NT * b, NT)],
                                   ps[:, 7, 0:64].rearrange("p (h t) -> p h t", t=NT), ACT.Copy).then_inc(do_ready, 1)
                act.wait_ge(do_ready, NB)
                act.activation(dsq[:, :].rearrange("p (h n) -> p h n", h=JT), OG[:, :, NP_TOK:T], ACT.Square
                               ).then_inc(dsq_ready, 1)
                act.wait_ge(dtotal, 1)
                act.activation(dstd[:, :], ps[:, 0, :], ACT.Sqrt, scale=1.0 / VD, bias=eps_rms).then_inc(dstd_ready, 1)

            @block.vector
            def _(dve):
                dve.memset(Qz[:, :, :], 0.0).then_inc(qz_zero, 1)
                dve.wait_ge(qz_zero, 1)
                dve.wait_ge(qs_in, 16)
                qz_ap = Qz[:, :, :]
                step = qz_ap.ap[0][0]
                with dve.Fori(0, NB) as b:
                    dve_step.enter(b, 0, 5)
                    dve.wait_ge(ds_done, NG * b)
                    for c in range(2):
                        dst = bass.AP(qz_ap.tensor, HD * c * step + 16 * c,
                                      [[step, HD], [P + 32, NG], [NT, GH], [1, NT]])
                        src = qsT[HD * c:HD * c + HD, :, bass.ds(NT * b, NT)].rearrange("p (g h) t -> p g h t", g=NG)
                        ins = dve.tensor_copy(dst, src)
                    ins.then_inc(qz_ready, 1)
                    for g in range(NG):
                        dve.wait_ge(kt_turned, 2 * NG * b + 2 * g + 2)
                        if g >= 2:
                            dve.wait_ge(ds_done, NG * b + g - 1)
                        dve.tensor_copy(kT[:, g % 2, 512:1024], ps[:, 3 + (2 * g + 1) % 3, :]).then_inc(kev_dve, 1)
                    dve.wait_ge(ds_done, NG * b + NG)
                    dve.tensor_tensor(snew[:, :], ps[:, 2, 0:NT], newmask, ALU.add
                                      ).then_inc(dve_step.sem, dve_step.up())
                    dve.tensor_reduce(st6[:, 0:1], ps[:, 0:2, :].rearrange("p b n -> p (b n)"), AX.X, ALU.max,
                                      negate=True)
                    dve.wait_ge(dve_step.sem, dve_step.now())
                    dve.tensor_reduce(st6[:, 1:2], snew[:, :], AX.X, ALU.max, negate=True
                                      ).then_inc(dve_step.sem, dve_step.up())
                    dve.wait_ge(dve_step.sem, dve_step.now())
                    dve.tensor_tensor(st6[:, 2:3], st6[:, 0:1], st6[:, 1:2], ALU.min).then_inc(dmx, 1)
                    dve.wait_ge(dexp, b + 1)
                    dve.tensor_tensor(st6[:, 5:6], st6[:, 3:4], st6[:, 4:5], ALU.add
                                      ).then_inc(dve_step.sem, dve_step.up())
                    dve.wait_ge(dve_step.sem, dve_step.now())
                    dve.reciprocal(st6[:, 6:7], st6[:, 5:6]).then_inc(dve_step.sem, dve_step.up())
                    dve.wait_ge(dve_step.sem, dve_step.now())
                    dve.tensor_tensor(st6[:, 7:8], st6[:, 6:7], rowcoef, ALU.mult
                                      ).then_inc(dve_step.sem, dve_step.up())
                    dve.wait_ge(dve_step.sem, dve_step.now())
                    dve.tensor_scalar(zc[:, :], rowsel, st6[:, 7:8], None, ALU.mult).then_inc(zc_ready, 1)
                    dve.wait_ge(at_turned, b + 1)
                    dve.tensor_copy(aTn[:, :], ps[0:NT, 2, 64:128]).then_inc(at_ready, 1)
                dve_step.leave(NB)
                og = OG[:, :, NP_TOK:T]
                d3 = dstd[:, :].rearrange("p (h n) -> p h n", h=JT)
                dve.wait_ge(dstd_ready, 1)
                dve.reciprocal(dstd[:, :], dstd[:, :]).then_inc(dog, 1)
                dve.wait_ge(dog, 1)
                dve.scalar_tensor_tensor(out=og, in0=og, scalar=subg, in1=d3, op0=ALU.mult, op1=ALU.mult
                                         ).then_inc(dog, 1)
                dve.wait_ge(dog, 2)
                dve.wait_ge(sgs_in, 16)
                dve.tensor_tensor(og, og, sgs[:, :, :], ALU.mult).then_inc(dog, 1)

            @block.gpsimd
            def _(pool):
                pool.wait_ge(dog, 3)

        yo = [place(f"yo{s}", [P, D], F32, slot(0 + s)) for s in range(2)]
        ohi_ready, olo_ready, yn_ready, y_turned, yo_act, yo_dve = (sem(x) for x in (
            "ohi_ready", "olo_ready", "yn_ready", "y_turned", "yo_act", "yo_dve"))
        y_out = [sem("y_out0"), sem("y_out1")]
        with nc.Block() as block:
            @block.sync
            def _(sp):
                out_proj_sp(sp, outp[1], U_AOUT, w_aout, res_d[1], None)
                for t in range(NXT):
                    n = tok_rows(t)
                    sp.wait_ge(yo_act, t + 1)
                    sp.wait_ge(yo_dve, t + 1)
                    dst = o["y_prompt"][0, t * P:(t + 1) * P, :] if t < QT else \
                        o["y_sample"].rearrange("b t d -> (b t) d")
                    sp.dma_start(dst, yo[t % 2][0:n, :]).then_inc(y_out[t % 2], 16)
                sp.wait_ge(y_out[0], 16 * 5)
                sp.wait_ge(y_out[1], 16 * 4)

            @block.tensor
            def _(pe):
                out_proj_pe(pe, outp[1], U_AOUT, olo_ready)
                norm_total_after(pe, outp[1], norms[2])
                pe.wait_ge(Norm.rstd_ready, norms[2].o + 1)
                pe.wait_ge(yn_ready, KD)
                for t in range(NXT):
                    n = tok_rows(t)
                    if t >= 2:
                        pe.wait_ge(yo_act, t - 1)
                        pe.wait_ge(yo_dve, t - 1)
                    for k in range(KD):
                        mm = pe.transpose(ps[0:n, 2 * (t % 2) + k // 4, (k % 4) * P:(k % 4 + 1) * P],
                                          Y[:, k, t * P:t * P + n], ident)
                    mm.then_inc(y_turned, 1)

            @block.scalar
            def _(act):
                with act.Fori(0, JT) as j:
                    act.activation(Ghi[:, bass.ds(j, 1), :].rearrange("p o n -> p (o n)"),
                                   OG[:, bass.ds(j, 1), :].rearrange("p o n -> p (o n)"), ACT.Copy
                                   ).then_inc(ohi_ready, 1)
                out_proj_act(act, outp[1], norms[2], U_AOUT, False)
                norm_std(act, norms[2])
                for t in range(NXT):
                    n = tok_rows(t)
                    act.wait_ge(y_turned, t + 1)
                    if t >= 2:
                        act.wait_ge(y_out[t % 2], 16 * (t // 2))
                    act.activation(yo[t % 2][0:n, 0:512], ps[0:n, 2 * (t % 2), :], ACT.Copy).then_inc(yo_act, 1)

            @block.vector
            def _(dve):
                out_proj_dve(dve, outp[1], U_AOUT)
                norm_rstd(dve, norms[2])
                dve.wait_ge(Norm.rstd_ready, norms[2].o + 1)
                for k in range(KD):
                    dve.scalar_tensor_tensor(out=Y[:, k, :], in0=Y[:, k, :],
                                             scalar=cols[:, C_FNG + k:C_FNG + k + 1],
                                             in1=std[:, :], op0=ALU.mult, op1=ALU.mult).then_inc(yn_ready, 1)
                for t in range(NXT):
                    n = tok_rows(t)
                    dve.wait_ge(y_turned, t + 1)
                    if t >= 2:
                        dve.wait_ge(y_out[t % 2], 16 * (t // 2))
                    dve.tensor_copy(yo[t % 2][0:n, 512:1024], ps[0:n, 2 * (t % 2) + 1, :]).then_inc(yo_dve, 1)

            @block.gpsimd
            def _(pool):
                with pool.Fori(0, JT) as j:
                    pool.wait_ge(ohi_ready, j + 1)
                    pool.tensor_tensor(Glo[:, bass.ds(j, 1), :].rearrange("p o n -> p (o n)"),
                                       OG[:, bass.ds(j, 1), :].rearrange("p o n -> p (o n)"),
                                       Ghi[:, bass.ds(j, 1), :].rearrange("p o n -> p (o n)").bitcast(F32),
                                       ALU.subtract).then_inc(olo_ready, 1)
                out_proj_pool(pool, norms[2], U_AOUT, False)


_INS = ["x_prompt", "x_sample", "state_conv", "cache_k", "cache_v", "page_table", "norm_g", "final_norm_g",
        "conv_w_in", "conv_dw_w", "conv_dw_b", "conv_ln_g", "conv_ln_b", "conv_w_out",
        "attn_w_in", "attn_lambda_q1", "attn_lambda_k1", "attn_lambda_q2", "attn_lambda_k2",
        "attn_subln_g", "attn_w_out"]
_OUTS = [("y_prompt", (1, NP_TOK, D)), ("y_sample", (NB, NT, D)),
         ("conv_state_prompt", (1, 1, PAD, E)), ("conv_state_sample", (1, NB, PAD, E)),
         ("k_rows_prompt", (1, 1, NP_TOK, NG, 2 * HD)), ("v_rows_prompt", (1, 1, NP_TOK, NG, VD)),
         ("k_rows_sample", (1, NB, NT, NG, 2 * HD)), ("v_rows_sample", (1, NB, NT, NG, VD))]


def kernel(**inputs):
    import concourse.bacc as _bacc
    from concourse.bass_utils import run_bass_kernel_spmd as _run

    nc = _bacc.Bacc("TRN2", target_bir_lowering=False, num_devices=1, dynamic_dma_scratch_size=1024)
    arrays = {name: np.ascontiguousarray(inputs[name]) for name in _INS}
    arrays.update(host_constants())
    a = {name: nc.dram_tensor(name, x.shape, mybir.dt.from_np(x.dtype), kind="ExternalInput").ap()
         for name, x in arrays.items()}
    o = {name: nc.dram_tensor(name, shape, F32, kind="ExternalOutput").ap() for name, shape in _OUTS}
    build(nc, a, o)
    r = _run(nc, [arrays], core_ids=[0])
    return tuple(r.results[0][name] for name, _ in _OUTS)
```

```python
from contextlib import ExitStack
import math

import numpy as np

import concourse.bass as bass
from concourse import mybir

F32 = mybir.dt.float32
F32R = mybir.dt.float32r
I32 = mybir.dt.int32
ALU = mybir.AluOpType
ACT = mybir.ActivationFunctionType
AX = mybir.AxisListType

P = 128
D = 1024
KD = D // P
NP_TOK, NB, NT = 1024, 8, 4
NS_TOK = NB * NT
T = NP_TOK + NS_TOK
CH = T // 3
E = 2048
JT = E // P
TAPS = 31
PAD = TAPS - 1
WIN = PAD + NT
NG, GH = 4, 4
HD, VD = 64, 128
ROT = HD // 4
THETA = 500000.0
PAST, PAGE = 1024, 128
PAGES = PAST // PAGE
QT = NP_TOK // P
SCALE = HD ** -0.5
RMS_EPS, LN_EPS = 1e-6, 1e-5
LAM_INIT = 0.8 - 0.6 * math.exp(-0.3)
MASKED = -float(2 ** 100)

C_NG1, C_NG2, C_FNG, C_DWB, C_LNG, C_LNB, C_SUB, N_COLS = 0, 8, 16, 24, 40, 56, 72, 73

U_CONV, U_COUT, U_ATT, U_AOUT, N_UNITS = 0, 48, 64, 104, 120

POOL_TAPS = 10
POOL_FIRST = 4


class Count:

    def __init__(self, sem):
        self.sem, self.n, self.off = sem, 0, 0

    def up(self):
        self.n += 1
        return 1

    def now(self, back=0):
        return self.off + (self.n - back)

    def enter(self, i, first, per):
        self.start, self.per, self.off = self.n, per, (i - first) * per

    def leave(self, trips):
        assert self.n - self.start == self.per, (self.n - self.start, self.per)
        self.n, self.off = self.n + self.per * (trips - 1), 0


def host_constants():
    pos = np.concatenate([np.arange(NP_TOK), np.tile(PAST + np.arange(NT), NB)]).astype(np.float32)
    half = ROT // 2
    inv = np.float32(THETA) ** (-np.arange(half, dtype=np.float32) / np.float32(half))
    ang = pos[None, :] * inv[:, None].astype(np.float32)
    cos, sin = np.ones((P, T), np.float32), np.zeros((P, T), np.float32)
    swap = np.zeros((P, P), np.float32)
    for c in range(2):
        for i in range(half):
            a, b = HD * c + i, HD * c + half + i
            cos[a] = cos[b] = np.cos(ang[i])
            sin[a] = sin[b] = np.sin(ang[i])
            swap[b, a], swap[a, b] = -1.0, 1.0
    t = np.arange(P)
    causal = np.where(t[None, :] <= t[:, None], 0.0, MASKED).astype(np.float32)
    g, c, h, s = np.meshgrid(np.arange(NG), np.arange(2), np.arange(GH), np.arange(NT), indexing="ij")
    g, c, h, s = (v.reshape(-1) for v in (g, c, h, s))
    newmask = np.where(np.arange(NT)[None, :] <= s[:, None], 0.0, MASKED).astype(np.float32)
    rows = np.zeros((P, NG * GH * NT), np.float32)
    rows[np.arange(P), (g * GH + h) * NT + s] = 1.0
    cc = np.stack([1.0 - c, c], 1).astype(np.float32)
    small = np.concatenate([np.eye(P, dtype=np.float32), swap, causal, rows, newmask, cc], 1)
    return {"c_small": small, "c_cos": cos, "c_sin": sin}


N_SMALL = 3 * P + NG * GH * NT + NT + 2


def build(nc, a, o):
    ctx = ExitStack()
    with ctx:
        def sem(name):

            return ctx.enter_context(nc.semaphore(name))

        base = (nc.sbuf_base + 31) // 32 * 32
        cursor = [base]

        def place(name, shape, dt=F32, at=None):
            size = (int(np.prod(shape[1:])) * 4 + 31) // 32 * 32
            if at is None:
                at = cursor
            t = nc.alloc_sbuf_tensor_at(name, list(shape), dt, offset=at[0])
            at[0] += size
            return t

        small = place("small", [P, N_SMALL])
        ident = small[:, 0:P]
        swap = small[:, P:2 * P]
        causal = small[:, 2 * P:3 * P]
        rowsel = small[:, 3 * P:3 * P + 64]
        newmask = small[:, 3 * P + 64:3 * P + 68]
        cc = small[:, 3 * P + 68:3 * P + 70]
        ones = place("ones", [P, P])
        cols = place("cols", [P, N_COLS])
        dww = place("dww", [P, JT, TAPS])
        misc = place("misc", [P, 8])
        eps_rms, eps_ln, neglam, subg, rowcoef = (misc[:, i:i + 1] for i in range(5))
        raw_at = [cursor[0], cursor[0] + 4 * KD * P]
        raw = [place(f"w_raw{s}", [P, KD, P]) for s in range(2)]
        whi = [place(f"w_hi{s}", [P, KD, P], F32R) for s in range(2)]
        wlo = [place(f"w_lo{s}", [P, KD, P], F32R) for s in range(2)]
        SLOT = 4 * T
        slots0 = cursor[0]
        assert slots0 + 46 * SLOT <= 229344, slots0

        def slot(n):
            return [slots0 + n * SLOT]

        ps = nc.alloc_psum_tensor("ps", [P, 8, 512], F32)

        def pset(s):
            return ps[:, 3 * s:3 * s + 3, 0:CH]

        def chunks(ap):
            return ap.rearrange("p (c n) -> p c n", c=3)

        Hhi = place("Hhi", [P, KD, T], F32R, slot(0))
        Hlo = place("Hlo", [P, KD, T], F32R, slot(8))
        Ghi = place("Ghi", [P, JT, T], F32R, slot(0))
        C = place("C", [P, JT, T], F32, slot(16))
        Glo = place("Glo", [P, JT, T], F32R, slot(16))
        Y = place("Y", [P, KD, T], F32, slot(32))
        xres = [place(f"xres{s}", [P, T], F32, slot(40 + s)) for s in range(2)]
        ssum = place("ssum", [P, T], F32, slot(42))
        sq = place("sq", [P, T], F32, slot(43))
        std = place("std", [P, T], F32, slot(44))
        csum = place("csum", [P, T], F32, slot(45))

        def scratch(name, shape):
            return nc.dram_tensor(name, shape, F32, kind="Internal").ap()
        res_d = [scratch("res0", [P, KD, T]), scratch("res1", [P, KD, T])]
        gate_d = [scratch("gate0", [JT, P, T]), scratch("gate1", [JT, P, T])]
        rstd_d = scratch("rstd_heads", [JT, NP_TOK])
        q_d = scratch("q_rot", [JT, P, T])
        k_d = scratch("k_rot", [NG, P, T])

        raw_in = [sem("raw_in0"), sem("raw_in1")]
        w_hi, w_lo, w_used = sem("w_hi"), sem("w_lo"), sem("w_used")
        act_step, dve_step, pool_step = Count(sem("act_step")), Count(sem("dve_step")), Count(sem("pool_step"))

        w_cin = a["conv_w_in"][0].rearrange("(k p) e -> p k e", p=P)
        w_cout = a["conv_w_out"][0].rearrange("(f k p) e -> f p k e", p=P, f=2)
        w_ain = a["attn_w_in"][0].rearrange("(k p) e -> p k e", p=P)
        w_aout = a["attn_w_out"][0].rearrange("(f k p) e -> f p k e", p=P, f=2)

        def conv_src(col, kind):
            return w_cin[:, :, bass.ds(col + (E, 0, 2 * E)[kind], P)]

        def out_src(w, pair, q):
            return w[q // 2][:, :, bass.ds((pair * 2 + q % 2) * P, P)]

        ATT_ORDER = list(range(16)) + list(range(16, 24)) + list(range(24, 40))

        def att_src(u):
            return w_ain[:, :, bass.ds(u * P, P)]

        def load_unit(sp, n, s, src):
            sp.wait_ge(w_lo, n - 1)
            sp.dma_start(raw[s][:, :, :], src).then_inc(raw_in[s], 16)

        def make_hi(act, n, s, turn, reused=True):
            act.wait_ge(raw_in[s], turn * 16)
            if reused:
                act.wait_ge(w_used, n - 1)
            act.activation(whi[s][:, :, :], raw[s][:, :, :], ACT.Copy).then_inc(w_hi, 1)

        def make_lo(pool, n, s):
            pool.wait_ge(w_hi, n + 1)
            pool.tensor_tensor(wlo[s][:, :, :], raw[s][:, :, :], whi[s][:, :, :].bitcast(F32),
                               ALU.subtract).then_inc(w_lo, 1)

        def unit(pe, n, s, dst, rhs_hi, rhs_lo, start=True, stop=True, before_chunk=None):
            pe.wait_ge(w_lo, n + 1)
            for c in range(3):
                if before_chunk:
                    before_chunk(c)
                for k in range(KD):
                    for w, r in ((whi[s], rhs_hi), (whi[s], rhs_lo), (wlo[s], rhs_hi)):
                        mm = pe.matmul(ps[:, 3 * dst + c, 0:CH], w[:, k, :], r(k)[:, c * CH:(c + 1) * CH],
                                       start=start and k == 0 and w is whi[s] and r is rhs_hi,
                                       stop=stop and k == KD - 1 and w is wlo[s])
            mm.then_inc(w_used, 1)

        def h_hi(k):
            return Hhi[:, k, :]

        def h_lo(k):
            return Hlo[:, k, :]

        class Norm:
            sq_ready, sum_ready, total, std_ready = sem("n_sq"), sem("n_sum"), sem("n_total"), sem("n_std")
            rstd_ready, h_ready, hi_ready, lo_ready = sem("n_rstd"), sem("n_h"), sem("n_hi"), sem("n_lo")

            def __init__(self, turn):
                self.t, self.o = KD * turn, turn

        norms = [Norm(i) for i in range(3)]
        nh = [place(f"nh{s}", [P, T], F32, slot(40 + s)) for s in range(2)]

        def norm_square(act, nm, k, ready, y):
            act.wait_ge(*ready)
            act.wait_ge(nm.sum_ready, nm.t + k)
            act.activation(sq[:, :], y, ACT.Square).then_inc(nm.sq_ready, 1)

        def norm_add(pool, nm, k, first):
            pool.wait_ge(nm.sq_ready, nm.t + k + 1)
            if first:
                pool.tensor_scalar(ssum[:, :], sq[:, :], 1.0, 1.0, ALU.mult, ALU.mult).then_inc(nm.sum_ready, 1)
            else:
                pool.wait_ge(nm.sum_ready, nm.t + k)
                pool.tensor_tensor(ssum[:, :], ssum[:, :], sq[:, :], ALU.add).then_inc(nm.sum_ready, 1)

        def norm_total(pe, nm):
            pe.wait_ge(nm.sum_ready, nm.t + KD)
            for c in range(3):
                mm = pe.matmul(ps[:, c, 0:CH], ones[:, :], ssum[:, c * CH:(c + 1) * CH], start=True, stop=True)
            mm.then_inc(nm.total, 1)

        def norm_total_after(pe, op, nm):
            for d in range(2):
                pe.wait_ge(op.y[d], op.b + KD // 2)
            norm_total(pe, nm)

        def norm_std(act, nm):
            act.wait_ge(nm.total, nm.o + 1)
            act.activation(chunks(std[:, :]), pset(0), ACT.Sqrt, scale=1.0 / D, bias=eps_rms).then_inc(nm.std_ready, 1)

        def norm_rstd(dve, nm):
            dve.wait_ge(nm.std_ready, nm.o + 1)
            dve.reciprocal(std[:, :], std[:, :]).then_inc(nm.rstd_ready, 1)

        def norm_apply(dve, nm, k, gcol):
            dve.wait_ge(nm.rstd_ready, nm.o + 1)
            if k >= 2:
                dve.wait_ge(nm.lo_ready, nm.t + k - 1)
            dve.scalar_tensor_tensor(out=nh[k % 2][:, :], in0=Y[:, k, :], scalar=cols[:, gcol + k:gcol + k + 1],
                                     in1=std[:, :], op0=ALU.mult, op1=ALU.mult).then_inc(nm.h_ready, 1)

        def norm_hi(act, nm, k):
            act.wait_ge(nm.h_ready, nm.t + k + 1)
            act.activation(Hhi[:, k, :], nh[k % 2][:, :], ACT.Copy).then_inc(nm.hi_ready, 1)

        def norm_lo(pool, nm, k):
            pool.wait_ge(nm.hi_ready, nm.t + k + 1)
            pool.tensor_tensor(Hlo[:, k, :], nh[k % 2][:, :], Hhi[:, k, :].bitcast(F32),
                               ALU.subtract).then_inc(nm.lo_ready, 1)

        NXT = QT + 1
        xin = place("xin", [P, NXT, D], F32, slot(16))
        vecs = place("vecs", [N_COLS, P], F32, slot(26))
        dwin = place("dwin", [TAPS, E], F32, slot(27))
        lamv = place("lamv", [1, 4, HD], F32, slot(29))
        lamt = place("lamt", [1, 2, HD], F32, slot(30))
        lams = place("lams", [1, 8], F32, slot(31))
        x_in = [sem(f"x_in{t}") for t in range(NXT)]
        small_in, vec_in, dw_in, lam_in = sem("small_in"), sem("vec_in"), sem("dw_in"), sem("lam_in")
        setup = sem("setup")
        x_turned = sem("x_turned")
        xe_act, xe_dve = sem("x_evac_act"), sem("x_evac_dve")
        cols_turned, cols_ready, dw_turned, dw_ready = sem("cols_turned"), sem("cols_ready"), sem("dw_turned"), sem("dw_ready")
        lam_exp, lam_row, lam_all = sem("lam_exp"), sem("lam_row"), sem("lam_all")
        lam_sum = sem("lam_sum")
        res_out = [sem("res_out0"), sem("res_out1")]

        def tok_rows(t):
            return P if t < QT else NS_TOK

        with nc.Block() as block:
            @block.sync
            def _(sp):
                sp.dma_start(small[:, :], a["c_small"]).then_inc(small_in, 16)
                for t in range(QT):
                    sp.dma_start(xin[:, t, :], a["x_prompt"][0, t * P:(t + 1) * P, :]).then_inc(x_in[t], 16)
                sp.dma_start(xin[0:NS_TOK, QT, :], a["x_sample"].rearrange("b t d -> (b t) d")).then_inc(x_in[QT], 16)
                for s, kind in ((0, 0), (1, 1)):
                    sp.dma_start(raw[s][:, :, :], conv_src(0, kind)).then_inc(raw_in[s], 16)
                for r, name, n in ((C_NG1, "norm_g", 16), (C_FNG, "final_norm_g", 8), (C_DWB, "conv_dw_b", 16),
                                   (C_LNG, "conv_ln_g", 16), (C_LNB, "conv_ln_b", 16), (C_SUB, "attn_subln_g", 1)):
                    v = a[name] if name == "final_norm_g" else a[name].rearrange("l d -> (l d)")
                    sp.dma_start(vecs[r:r + n, :], v.rearrange("(k p) -> k p", p=P)).then_inc(vec_in, 16)
                sp.dma_start(dwin[:, :], a["conv_dw_w"][0]).then_inc(dw_in, 16)
                for i, name in enumerate(("attn_lambda_q1", "attn_lambda_k1", "attn_lambda_q2", "attn_lambda_k2")):
                    sp.dma_start(lamv[:, i, :], a[name]).then_inc(lam_in, 16)
                sp.wait_ge(xe_act, NXT)
                sp.wait_ge(xe_dve, NXT)
                sp.dma_start(res_d[0], Y[:, :, :]).then_inc(res_out[0], 16)
                sp.wait_ge(res_out[0], 16)

            @block.tensor
            def _(pe):
                pe.wait_ge(small_in, 16)
                for t in range(NXT):
                    n = tok_rows(t)
                    pe.wait_ge(x_in[t], 16)
                    if t >= 3:
                        pe.wait_ge(xe_act, t - 2)
                        pe.wait_ge(xe_dve, t - 2)
                    for k in range(KD):
                        mm = pe.transpose(ps[:, 2 * (t % 3) + k // 4, (k % 4) * P:(k % 4) * P + n],
                                          xin[0:n, t, k * P:(k + 1) * P], ident[0:n, 0:n])
                    mm.then_inc(x_turned, 1)
                pe.wait_ge(vec_in, 96)
                pe.transpose(ps[:, 6, 0:N_COLS], vecs[:, :], ident[0:N_COLS, 0:N_COLS]).then_inc(cols_turned, 1)
                pe.wait_ge(dw_in, 16)
                for j in range(JT):
                    mm = pe.transpose(ps[:, 7, TAPS * j:TAPS * (j + 1)], dwin[:, j * P:(j + 1) * P], ident[0:TAPS, 0:TAPS])
                mm.then_inc(dw_turned, 1)
                pe.wait_ge(setup, 2)
                pe.wait_ge(lam_row, 1)
                pe.wait_ge(cols_ready, 1)
                pe.matmul(ps[:, 6, 0:2], ones[0:1, :], lams[0:1, 4:6], start=True, stop=True).then_inc(lam_all, 1)
                pe.wait_ge(xe_act, NXT)
                pe.wait_ge(xe_dve, NXT)
                norm_total(pe, norms[0])

            @block.scalar
            def _(act):
                for t in range(NXT):
                    n = tok_rows(t)
                    act.wait_ge(x_turned, t + 1)
                    act.activation(Y[:, 0:4, t * P:t * P + n],
                                   ps[:, 2 * (t % 3), :].rearrange("p (k n) -> p k n", k=4)[:, :, 0:n],
                                   ACT.Copy).then_inc(xe_act, 1)
                act.wait_ge(cols_turned, 1)
                act.activation(cols[:, :], ps[:, 6, 0:N_COLS], ACT.Copy).then_inc(cols_ready, 1)
                act.wait_ge(dw_turned, 1)
                act.activation(dww[:, :, :], ps[:, 7, 0:JT * TAPS].rearrange("p (j k) -> p j k", j=JT),
                               ACT.Copy).then_inc(dw_ready, 1)
                act.wait_ge(lam_sum, 2)
                act.activation(lams[0:1, 2:4], lams[0:1, 0:2], ACT.Exp).then_inc(lam_exp, 1)
                act.wait_ge(xe_act, NXT)
                for k in range(KD):
                    norm_square(act, norms[0], k, (xe_dve, NXT), Y[:, k, :])
                norm_std(act, norms[0])
                for n in range(2):
                    make_hi(act, n, n % 2, 1, reused=False)
                for k in range(KD):
                    norm_hi(act, norms[0], k)

            @block.vector
            def _(dve):
                dve.memset(ones[:, :], 1.0).then_inc(setup, 1)
                dve.memset(eps_rms, RMS_EPS).then_inc(setup, 1)
                dve.memset(eps_ln, LN_EPS).then_inc(setup, 1)
                for t in range(NXT):
                    n = tok_rows(t)
                    dve.wait_ge(x_turned, t + 1)
                    dve.tensor_copy(Y[:, 4:8, t * P:t * P + n],
                                    ps[:, 2 * (t % 3) + 1, :].rearrange("p (k n) -> p k n", k=4)[:, :, 0:n]
                                    ).then_inc(xe_dve, 1)
                dve.wait_ge(lam_in, 64)
                for i in range(2):
                    dve.tensor_tensor(lamt[:, i, :], lamv[:, 2 * i, :], lamv[:, 2 * i + 1, :], ALU.mult
                                      ).then_inc(dve_step.sem, dve_step.up())
                dve.wait_ge(dve_step.sem, dve_step.now())
                for i in range(2):
                    dve.tensor_reduce(lams[0:1, i:i + 1], lamt[:, i, :], AX.X, ALU.add).then_inc(lam_sum, 1)
                dve.wait_ge(lam_exp, 1)
                dve.tensor_tensor(lams[0:1, 6:7], lams[0:1, 3:4], lams[0:1, 2:3], ALU.subtract
                                  ).then_inc(dve_step.sem, dve_step.up())
                dve.wait_ge(dve_step.sem, dve_step.now())
                for i in range(2):
                    dve.tensor_scalar(lams[0:1, 4 + i:5 + i], lams[0:1, 6:7], -LAM_INIT, None, ALU.add
                                      ).then_inc(dve_step.sem, dve_step.up())
                dve.wait_ge(dve_step.sem, dve_step.now())
                dve.sem_inc(lam_row, 1)
                dve.wait_ge(lam_all, 1)
                dve.tensor_copy(neglam, ps[:, 6, 0:1]).then_inc(dve_step.sem, dve_step.up())
                dve.wait_ge(cols_ready, 1)
                dve.tensor_scalar(subg, cols[:, C_SUB:C_SUB + 1], 1.0 - LAM_INIT, None, ALU.mult
                                  ).then_inc(dve_step.sem, dve_step.up())
                dve.wait_ge(small_in, 16)
                dve.wait_ge(dve_step.sem, dve_step.now())
                dve.scalar_tensor_tensor(out=rowcoef, in0=cc[:, 1:2], scalar=neglam, in1=cc[:, 0:1],
                                         op0=ALU.mult, op1=ALU.add).then_inc(dve_step.sem, dve_step.up())
                norm_rstd(dve, norms[0])
                for k in range(KD):
                    norm_apply(dve, norms[0], k, C_NG1)

            @block.gpsimd
            def _(pool):
                for k in range(KD):
                    norm_add(pool, norms[0], k, k == 0)
                for n in range(2):
                    make_lo(pool, n, n % 2)
                for k in range(KD):
                    norm_lo(pool, norms[0], k)

        at = slot(32)
        U = [place(f"U{s}", [P, NP_TOK + P], F32, at) for s in range(2)]
        sigb = place("sigb", [P, T], F32, at)
        odd = place("odd", [P, NP_TOK], F32, at)
        pacc = place("pool_acc", [P, NP_TOK], F32, at)
        prod = [place(f"prod{s}", [P, NP_TOK], F32, at) for s in range(2)]
        sg = [place(f"sg{s}", [P, T], F32, at) for s in range(2)]
        smp = place("smp", [P, NB, NT, TAPS], F32, slot(46))
        win = place("win", [P, NB, WIN], F32, at)
        stin = [place(f"st_in{s}", [P - 8, 2, P], F32, at) for s in range(2)]
        stout = place("st_out", [PAD + NS_TOK, E], F32, at)
        assert at[0] <= slot(45)[0]
        SR = NB * PAD // 2
        st_src = a["state_conv"][0].rearrange("b r c -> (b r) c").rearrange("(h p) c -> p h c", p=SR)

        sig_done, u_done, sg_done = sem("sig_done"), sem("u_done"), sem("sg_done")
        st_loaded = [sem("st_loaded0"), sem("st_loaded1")]
        st_turned, win_state, win_ready, smp_read = sem("st_turned"), sem("win_state"), sem("win_ready"), sem("smp_read")
        prod_ready, prod_free, pacc_ready, merged = sem("prod_ready"), sem("prod_free"), sem("pacc_ready"), sem("merged")
        u_turned, stout_ready = sem("u_turned"), sem("stout_ready")
        sg_out = [sem("sg_out0"), sem("sg_out1")]
        st_out = sem("st_out")
        keep_out = sem("keep_out")
        DVE_TAPS = list(range(POOL_TAPS, TAPS))
        win_ap = win[:, :, :]
        part_step = win_ap.ap[0][0]
        windows = bass.AP(win_ap.tensor, win_ap.offset, [[part_step, P], [WIN, NB], [1, NT], [1, TAPS]])

        with nc.Block() as block:
            @block.sync
            def _(sp):
                for s in range(2):
                    sp.dma_start(stin[s][0:SR, :, :], st_src[:, :, s * P:(s + 1) * P]).then_inc(st_loaded[s], 16)
                sp.dma_start(o["conv_state_sample"][0, :, 0:PAD - NT, :], a["state_conv"][0, :, NT:PAD, :]
                             ).then_inc(keep_out, 16)

                def spill(i, s):
                    sp.wait_ge(sg_done, 2 * i + s + 1)
                    sp.dma_start(gate_d[0][2 * i + s], sg[s][:, :]).then_inc(sg_out[s], 16)

                def body(i, last=False):
                    col = i * 2 * P if last else sp.snap(i * 2 * P)
                    for m in range(2, 8):
                        if last and m >= 6:
                            src = out_src(w_cout, 0, m - 6)
                        else:
                            src = conv_src(col + m // 3 * P, m % 3)
                        load_unit(sp, 6 * i + m, m % 2, src)
                        if m in (3, 7) and not last:
                            s = m // 4
                            sp.wait_ge(st_turned, 2 * i + s + 1)
                            sp.dma_start(stin[s][0:SR, :, :], st_src[:, :, bass.ds((2 * i + 2 + s) * P, P)]
                                         ).then_inc(st_loaded[s], 16)
                    spill(i, 0)
                    spill(i, 1)

                with sp.Fori(0, JT // 2 - 1) as i:
                    body(i)
                body(JT // 2 - 1, last=True)
                sp.wait_ge(stout_ready, JT)
                sp.dma_start(o["conv_state_prompt"][0, 0], stout[0:PAD, :]).then_inc(st_out, 16)
                for b in range(NB):
                    sp.dma_start(o["conv_state_sample"][0, b, PAD - NT:PAD, :],
                                 stout[PAD + NT * b:PAD + NT * (b + 1), :]).then_inc(st_out, 16)
                for s in range(2):
                    sp.wait_ge(sg_out[s], 16 * JT // 2)
                sp.wait_ge(st_out, 16 * (NB + 1))
                sp.wait_ge(keep_out, 16)

            @block.tensor
            def _(pe):
                pe.wait_ge(Norm.lo_ready, norms[0].t + KD)
                with pe.Fori(0, JT // 2) as i:
                    for s in range(2):
                        j = 2 * i + s
                        pe.wait_ge(st_loaded[s], 16 * (i + 1))
                        pe.wait_ge(win_state, j)
                        for h in range(2):
                            mm = pe.transpose(ps[:, 6, h * SR:(h + 1) * SR], stin[s][0:SR, h, :], ident[0:SR, 0:SR])
                        mm.then_inc(st_turned, 1)
                        n, e = 6 * i + 3 * s, s
                        pe.wait_ge(u_done, j)
                        unit(pe, n, e, e, h_hi, h_lo)
                        pe.wait_ge(sg_done, j)
                        unit(pe, n + 1, 1 - e, 1 - e, h_hi, h_lo)
                        pe.wait_ge(sig_done, j + 1)
                        unit(pe, n + 2, e, e, h_hi, h_lo)
                        pe.wait_ge(u_done, j + 1)
                        pe.wait_ge(stout_ready, j)
                        pe.transpose(ps[:, 7, 0:P], U[s][:, NP_TOK:NP_TOK + P], ident).then_inc(u_turned, 1)

            @block.scalar
            def _(act):
                with act.Fori(0, JT // 2) as i:
                    for s in range(2):
                        j, n, e = 2 * i + s, 6 * i + 3 * s, s

                        def products(lo, hi):
                            for q in range(lo, hi):
                                r = s * POOL_TAPS + q
                                act.wait_ge(prod_free, i * 2 * POOL_TAPS + r + 1)
                                act.activation(prod[r % 2][:, :], U[s][:, q:q + NP_TOK], ACT.Copy,
                                               scale=dww[:, bass.ds(j, 1), q]).then_inc(prod_ready, 1)

                        make_hi(act, n + 2, e, 3 * i + (3 * s + 2) // 2 + 1)
                        act.wait_ge(w_used, n + 1)
                        act.wait_ge(u_done, j)
                        act.activation(chunks(sigb[:, :]), pset(e), ACT.Sigmoid).then_inc(sig_done, 1)
                        act.wait_ge(st_turned, j + 1)
                        act.wait_ge(smp_read, j)
                        act.activation(win[:, :, 0:PAD], ps[:, 6, 0:NB * PAD].rearrange("p (b r) -> p b r", b=NB),
                                       ACT.Copy).then_inc(win_state, 1)
                        make_hi(act, n + 3, 1 - e, 3 * i + (3 * s + 3) // 2 + 1)
                        act.wait_ge(u_done, j + 1)
                        products(0, POOL_FIRST)
                        make_hi(act, n + 4, e, 3 * i + (3 * s + 4) // 2 + 1)
                        act.wait_ge(w_used, n + 3)
                        act.wait_ge(sg_out[s], 16 * i)
                        act.activation(chunks(sg[s][:, :]), pset(e), ACT.Silu).then_inc(sg_done, 1)
                        products(POOL_FIRST, POOL_TAPS)

            @block.gpsimd
            def _(pool):
                pool.sem_inc(prod_free, 2)
                with pool.Fori(0, JT // 2) as i:
                    for s in range(2):
                        j, n, e = 2 * i + s, 6 * i + 3 * s, s

                        def adds(lo, hi):
                            for q in range(max(lo, 1), hi):
                                r = i * 2 * POOL_TAPS + s * POOL_TAPS + q
                                pool.wait_ge(prod_ready, r + 1)
                                if q == 1:
                                    pool.wait_ge(merged, j)
                                    pool.tensor_tensor(pacc[:, :], prod[0][:, :], prod[1][:, :], ALU.add
                                                       ).then_inc(prod_free, 2)
                                else:
                                    pool.wait_ge(prod_free, r + 2)
                                    pool.tensor_tensor(pacc[:, :], pacc[:, :], prod[q % 2][:, :], ALU.add
                                                       ).then_inc(prod_free, 1)

                        make_lo(pool, n + 2, e)
                        make_lo(pool, n + 3, 1 - e)
                        adds(0, POOL_FIRST)
                        make_lo(pool, n + 4, e)
                        adds(POOL_FIRST, POOL_TAPS)

            @block.vector
            def _(dve):
                for s in range(2):
                    dve.memset(U[s][:, 0:PAD], 0.0).then_inc(dve_step.sem, dve_step.up())
                    dve.memset(U[s][:, PAD + T:NP_TOK + P], 0.0).then_inc(dve_step.sem, dve_step.up())
                dve.memset(csum[:, :], 0.0).then_inc(dve_step.sem, dve_step.up())
                per_tile = 3 + len(DVE_TAPS) + 2
                with dve.Fori(0, JT // 2) as i:
                    dve_step.enter(i, 0, 2 * per_tile)
                    for s in range(2):
                        j, n, e = 2 * i + s, 6 * i + 3 * s, s
                        c_p = C[:, bass.ds(j, 1), 0:NP_TOK].rearrange("p o n -> p (o n)")
                        c_s = C[:, bass.ds(j, 1), NP_TOK:T].rearrange("p o n -> p (o n)")
                        c_all = C[:, bass.ds(j, 1), :].rearrange("p o n -> p (o n)")
                        dve.wait_ge(w_used, n + 2)
                        dve.wait_ge(sig_done, j + 1)
                        dve.tensor_tensor(chunks(U[s][:, PAD:PAD + T]), pset(1 - e), chunks(sigb[:, :]),
                                          ALU.mult).then_inc(u_done, 1)
                        dve.wait_ge(u_done, j + 1)
                        dve.tensor_copy(win[:, :, PAD:WIN], U[s][:, PAD + NP_TOK:PAD + T].rearrange(
                            "p (b t) -> p b t", b=NB)).then_inc(dve_step.sem, dve_step.up())
                        dve.wait_ge(win_state, j + 1)
                        dve.wait_ge(dve_step.sem, dve_step.now())
                        w_j = dww[:, bass.ds(j, 1), :].rearrange("p o (x k) -> p (o x) k", x=1)
                        dve.tensor_tensor(smp[:, :, :, :].rearrange("p b t k -> p (b t) k"),
                                          windows.rearrange("p b t k -> p b t k"),
                                          w_j.to_broadcast([P, NS_TOK, TAPS]), ALU.mult).then_inc(smp_read, 1)
                        dve.wait_ge(smp_read, j + 1)
                        dve.tensor_reduce(c_s, smp[:, :, :, :].rearrange("p b t k -> p (b t) k"), AX.X, ALU.add
                                          ).then_inc(dve_step.sem, dve_step.up())
                        dve.wait_ge(dve_step.sem, dve_step.now())
                        bias = cols[:, bass.ds(j + C_DWB, 1)]
                        dve.tensor_scalar(c_s, c_s, bias, None, ALU.add).then_inc(dve_step.sem, dve_step.up())
                        for q, k in enumerate(DVE_TAPS):
                            tgt = odd[:, :] if q % 2 else c_p
                            wk = dww[:, bass.ds(j, 1), k]
                            uk = U[s][:, k:k + NP_TOK]
                            dve.wait_ge(dve_step.sem, dve_step.now(1))
                            if q == 0:
                                dve.tensor_scalar(tgt, uk, wk, bias, ALU.mult, ALU.add
                                                  ).then_inc(dve_step.sem, dve_step.up())
                            elif q == 1:
                                dve.tensor_scalar(tgt, uk, wk, None, ALU.mult
                                                  ).then_inc(dve_step.sem, dve_step.up())
                            else:
                                dve.scalar_tensor_tensor(out=tgt, in0=uk, scalar=wk, in1=tgt, op0=ALU.mult,
                                                         op1=ALU.add).then_inc(dve_step.sem, dve_step.up())
                        dve.wait_ge(u_turned, j + 1)
                        dve.tensor_copy(stout[:, bass.ds(j * P, P)], ps[0:PAD + NS_TOK, 7, 0:P]).then_inc(stout_ready, 1)
                        dve.wait_ge(dve_step.sem, dve_step.now())
                        dve.tensor_tensor(c_p, c_p, odd[:, :], ALU.add).then_inc(dve_step.sem, dve_step.up())
                        dve.wait_ge(dve_step.sem, dve_step.now())
                        dve.wait_ge(prod_free, 2 * i * POOL_TAPS + (s + 1) * POOL_TAPS + 2)
                        dve.tensor_tensor(c_p, c_p, pacc[:, :], ALU.add).then_inc(merged, 1)
                        dve.wait_ge(merged, j + 1)
                        dve.tensor_tensor(csum[:, :], csum[:, :], c_all, ALU.add
                                          ).then_inc(dve_step.sem, dve_step.up())
                    dve_step.leave(JT // 2)

        mean = place("mean", [P, T], F32, slot(32))
        lrstd = place("ln_rstd", [P, T], F32, slot(33))
        tt = [place(f"tt{s}", [P, T], F32, slot(34 + s)) for s in range(4)]
        lsq = [tt[0], tt[1]]
        sgl = [place(f"sgl{s}", [P, T], F32, slot(38 + s)) for s in range(2)]
        csum_turned, mean_ready, xc_ready, lsq_ready, lsq_used = (sem(x) for x in (
            "csum_total", "mean_ready", "xc_ready", "lsq_ready", "lsq_used"))
        lstd_ready, lrstd_ready = sem("lstd_ready"), sem("lrstd_ready")
        z_ready, silu_ready, p_ready, ghi_ready, glo_ready = (sem(x) for x in (
            "z_ready", "silu_ready", "p_ready", "ghi_ready", "glo_ready"))
        sgl_in = [sem("sgl_in0"), sem("sgl_in1")]

        class OutProj:
            res_in = [sem(f"res_in{s}") for s in range(2)]
            y = [sem(f"y_done{s}") for s in range(2)]

            def __init__(self, turn):
                self.b = KD // 2 * turn

        outp = [OutProj(0), OutProj(1)]

        def out_proj_pe(pe, op, n0, ready):
            with pe.Fori(0, KD // 2) as p:
                for q in range(4):
                    d, half = q % 2, q // 2
                    n = n0 + 4 * p + q
                    if half == 0:
                        pe.wait_ge(op.y[d], op.b + p)
                    pe.wait_ge(w_lo, n + 1)
                    for k in range(KD):
                        kk = KD * half + k
                        if d == 0:
                            pe.wait_ge(ready, kk + 1)
                        for w, r in ((whi, Ghi), (whi, Glo), (wlo, Ghi)):
                            for c in range(3):
                                mm = pe.matmul(ps[:, 3 * d + c, 0:CH], w[d][:, k, :],
                                               r[:, kk, c * CH:(c + 1) * CH],
                                               start=(kk == 0 and w is whi and r is Ghi),
                                               stop=(kk == JT - 1 and w is wlo))
                    mm.then_inc(w_used, 1)

        def out_proj_act(act, op, nm, n0, prepare):
            def body(p, ahead):
                for q in range(4):
                    n = n0 + 4 * p + q
                    if q < 2 or ahead:
                        make_hi(act, n + 2, q % 2, (n0 + q + 2) // 2 + 1 + 2 * p)
                    if q >= 2:
                        d = q - 2
                        act.wait_ge(op.y[d], op.b + p + 1)
                        act.wait_ge(nm.sum_ready, nm.t + 2 * p + d)
                        act.activation(sq[:, :], Y[:, bass.ds(2 * p + d, 1), :].rearrange("p o n -> p (o n)"),
                                       ACT.Square).then_inc(nm.sq_ready, 1)
            with act.Fori(0, KD // 2 - 1) as p:
                body(p, True)
            body(KD // 2 - 1, prepare)

        def out_proj_pool(pool, nm, n0, prepare):
            def body(p, first, ahead):
                for q in range(4):
                    n = n0 + 4 * p + q
                    if q < 2 or ahead:
                        make_lo(pool, n + 2, q % 2)
                    if q >= 2:
                        k = 2 * p + q - 2
                        norm_add(pool, nm, k, first and q == 2)
            body(0, True, True)
            with pool.Fori(1, KD // 2 - 1) as p:
                body(p, False, True)
            body(KD // 2 - 1, False, prepare)

        def out_proj_dve(dve, op, n0):
            with dve.Fori(0, KD // 2) as p:
                for d in range(2):
                    dve.wait_ge(w_used, n0 + 4 * p + 3 + d)
                    dve.wait_ge(op.res_in[d], 16 * (op.b + p + 1))
                    y = Y[:, bass.ds(2 * p + d, 1), :].rearrange("p o (c n) -> p (o c) n", c=3)
                    dve.tensor_tensor(y, pset(d), chunks(xres[d][:, :]), ALU.add).then_inc(op.y[d], 1)

        def out_proj_sp(sp, op, n0, w, res, nxt):
            for d in range(2):
                sp.dma_start(xres[d][:, :], res[:, d, :]).then_inc(op.res_in[d], 16)

            def body(p, last=False):
                for q in range(2, 6):
                    if last and q >= 4:
                        if nxt is None:
                            continue
                        src = nxt(q - 4)
                    else:
                        src = out_src(w, p if q < 4 else p + 1, q % 4)
                    load_unit(sp, n0 + 4 * p + q, q % 2, src)
                if not last:
                    for d in range(2):
                        sp.wait_ge(op.y[d], op.b + p + 1)
                        sp.dma_start(xres[d][:, :], res[:, bass.ds(2 * p + 2 + d, 1), :].rearrange("p o n -> p (o n)")
                                     ).then_inc(op.res_in[d], 16)
            with sp.Fori(0, KD // 2 - 1) as p:
                body(p)
            body(KD // 2 - 1, last=True)

        with nc.Block() as block:
            @block.sync
            def _(sp):
                for s in range(2):
                    sp.dma_start(sgl[s][:, :], gate_d[0][s]).then_inc(sgl_in[s], 16)
                with sp.Fori(1, JT // 2) as i:
                    for s in range(2):
                        sp.wait_ge(p_ready, 2 * i + s - 1)
                        sp.dma_start(sgl[s][:, :], gate_d[0][2 * i + s]).then_inc(sgl_in[s], 16)
                out_proj_sp(sp, outp[0], U_COUT, w_cout, res_d[0], lambda q: att_src(q))
                for d in range(2):
                    sp.wait_ge(outp[0].y[d], outp[0].b + KD // 2)
                sp.dma_start(res_d[1], Y[:, :, :]).then_inc(res_out[1], 16)
                sp.wait_ge(res_out[1], 16)

            @block.tensor
            def _(pe):
                for c in range(3):
                    mm = pe.matmul(ps[:, c, 0:CH], ones[:, :], csum[:, c * CH:(c + 1) * CH], start=True, stop=True)
                mm.then_inc(csum_turned, 1)

                def add_square(j, s, first, last):
                    pe.wait_ge(lsq_ready, j + 1)
                    for c in range(3):
                        mm = pe.matmul(ps[:, 3 + c, 0:CH], ones[:, :], lsq[s][:, c * CH:(c + 1) * CH],
                                       start=first, stop=last)
                    mm.then_inc(lsq_used, 1)

                add_square(0, 0, True, False)
                add_square(1, 1, False, False)
                with pe.Fori(1, JT // 2 - 1) as i:
                    for s in range(2):
                        add_square(2 * i + s, s, False, False)
                add_square(JT - 2, 0, False, False)
                add_square(JT - 1, 1, False, True)
                pe.wait_ge(lstd_ready, 1)
                out_proj_pe(pe, outp[0], U_COUT, glo_ready)
                norm_total_after(pe, outp[0], norms[1])

            @block.scalar
            def _(act):
                act.wait_ge(csum_turned, 1)
                act.activation(chunks(mean[:, :]), pset(0), ACT.Copy, scale=1.0 / E).then_inc(mean_ready, 1)
                with act.Fori(0, JT // 2) as i:
                    for s in range(2):
                        j = 2 * i + s
                        act.wait_ge(xc_ready, j + 1)
                        if s == 0:
                            act.wait_ge(lsq_used, 2 * i)
                        act.activation(lsq[s][:, :], C[:, bass.ds(j, 1), :].rearrange("p o n -> p (o n)"),
                                       ACT.Square).then_inc(lsq_ready, 1)
                act.wait_ge(lsq_used, JT)
                act.activation(chunks(lrstd[:, :]), pset(1), ACT.Sqrt, scale=1.0 / E, bias=eps_ln).then_inc(lstd_ready, 1)
                with act.Fori(0, JT // 4) as i:
                    for s in range(4):
                        j = 4 * i + s
                        act.wait_ge(z_ready, j + 1)
                        act.activation(tt[s][:, :], tt[s][:, :], ACT.Silu, scale=cols[:, bass.ds(j + C_LNG, 1)],
                                       bias=cols[:, bass.ds(j + C_LNB, 1)]).then_inc(silu_ready, 1)
                    for s in range(4):
                        j = 4 * i + s
                        act.wait_ge(p_ready, j + 1)
                        act.activation(Ghi[:, bass.ds(j, 1), :].rearrange("p o n -> p (o n)"), tt[s][:, :],
                                       ACT.Copy).then_inc(ghi_ready, 1)
                out_proj_act(act, outp[0], norms[1], U_COUT, True)
                norm_std(act, norms[1])
                for k in range(KD):
                    norm_hi(act, norms[1], k)

            @block.vector
            def _(dve):
                dve.wait_ge(mean_ready, 1)
                with dve.Fori(0, JT) as j:
                    cj = C[:, bass.ds(j, 1), :].rearrange("p o n -> p (o n)")
                    dve.tensor_tensor(cj, cj, mean[:, :], ALU.subtract).then_inc(xc_ready, 1)
                dve.wait_ge(lstd_ready, 1)
                dve.reciprocal(lrstd[:, :], lrstd[:, :]).then_inc(lrstd_ready, 1)
                dve.wait_ge(lrstd_ready, 1)
                dve.wait_ge(xc_ready, JT)
                with dve.Fori(0, JT // 4) as i:
                    for s in range(4):
                        j = 4 * i + s
                        dve.wait_ge(glo_ready, 4 * i)
                        dve.tensor_tensor(tt[s][:, :], C[:, bass.ds(j, 1), :].rearrange("p o n -> p (o n)"),
                                          lrstd[:, :], ALU.mult).then_inc(z_ready, 1)
                    for s in range(4):
                        j = 4 * i + s
                        dve.wait_ge(silu_ready, j + 1)
                        dve.wait_ge(sgl_in[s % 2], 16 * (2 * i + s // 2 + 1))
                        dve.tensor_tensor(tt[s][:, :], tt[s][:, :], sgl[s % 2][:, :], ALU.mult).then_inc(p_ready, 1)
                out_proj_dve(dve, outp[0], U_COUT)
                norm_rstd(dve, norms[1])
                for k in range(KD):
                    norm_apply(dve, norms[1], k, C_NG2)

            @block.gpsimd
            def _(pool):
                with pool.Fori(0, JT // 4) as i:
                    for s in range(4):
                        j = 4 * i + s
                        pool.wait_ge(ghi_ready, j + 1)
                        pool.tensor_tensor(Glo[:, bass.ds(j, 1), :].rearrange("p o n -> p (o n)"), tt[s][:, :],
                                           Ghi[:, bass.ds(j, 1), :].rearrange("p o n -> p (o n)").bitcast(F32),
                                           ALU.subtract).then_inc(glo_ready, 1)
                out_proj_pool(pool, norms[1], U_COUT, True)
                for k in range(KD):
                    norm_lo(pool, norms[1], k)

        cos = place("cos", [P, T], F32, slot(16))
        sin = place("sin", [P, T], F32, slot(17))
        qs = [place(f"qs{s}", [P, T], F32, slot(18 + s)) for s in range(2)]
        qc = [place(f"qc{s}", [P, T], F32, slot(20 + s)) for s in range(2)]
        qr = [place(f"qr{s}", [P, T], F32, slot(22 + s)) for s in range(2)]
        sga = [place(f"sga{s}", [P, T], F32, slot(24 + s)) for s in range(2)]
        at = slot(26)
        rows = [place(f"rows{s}", [P, NXT, P], F32, at) for s in range(2)]
        rsn = [place(f"rsn{s}", [P, T], F32, at) for s in range(2)]
        tab_in = sem("tab_in")
        qs_ready, qc_ready, swapped, rs_ready, qr_ready = (sem(x) for x in (
            "qs_ready", "qc_ready", "swapped", "rs_ready", "qr_ready"))
        qr_out = [sem("qr_out0"), sem("qr_out1")]
        rows_turned, rows_ready, rows_free = sem("rows_turned"), sem("rows_ready"), sem("rows_free")
        rows_out = [sem("rows_out0"), sem("rows_out1")]
        sga_done = sem("sga_done")
        sga_out = [sem("sga_out0"), sem("sga_out1")]
        NR = JT + NG
        NQK = JT + 2 * NG

        def row_dst(kind, g, sample):
            t = o[("k_rows" if kind == 0 else "v_rows") + ("_sample" if sample else "_prompt")]
            if sample:
                return t[0].rearrange("b t g e -> (b t) g e")[:, g, :]
            return t[0, 0].rearrange("(n p) g e -> p n g e", p=P)[:, :, g, :]

        def spill_gate(sp, i, s):
            sp.wait_ge(sga_done, 2 * i + s + 1)
            sp.dma_start(gate_d[1][2 * i + s], sga[s][:, :]).then_inc(sga_out[s], 16)

        def out_rows(sp, v):
            s, kind, g = v % 2, (v - JT) // NG, (v - JT) % NG
            sp.wait_ge(rows_ready, 3 * (v - JT + 1))
            sp.dma_start(row_dst(kind, g, False), rows[s][:, 0:QT, :]).then_inc(rows_out[s], 16)
            sp.dma_start(row_dst(kind, g, True), rows[s][0:NS_TOK, QT, :]).then_inc(rows_out[s], 16)

        def swap_mm(pe, u, s):
            pe.wait_ge(qs_ready, u + 1)
            pe.wait_ge(rs_ready, u)
            for c, b in enumerate((6, 7, 3 * s + 2)):
                mm = pe.matmul(ps[:, b, 0:CH], swap, qs[s][:, c * CH:(c + 1) * CH], start=True, stop=True)
            mm.then_inc(swapped, 1)

        def turn_rows_last(pe, v):
            s = v % 2
            pe.wait_ge(qs_ready, v + 1)
            pe.wait_ge(rows_ready, 3 * (v - JT))
            for t in range(QT):
                mm = pe.transpose(ps[:, 6 + t // 4, (t % 4) * P:(t % 4 + 1) * P], qs[s][:, t * P:(t + 1) * P], ident)
                if t % 4 == 3:
                    mm.then_inc(rows_turned, 1)
            pe.wait_ge(rows_ready, 3 * (v - JT) + 1)
            pe.transpose(ps[0:NS_TOK, 6, 0:P], qs[s][:, NP_TOK:T], ident).then_inc(rows_turned, 1)

        def rows_evac(act, v, last=False):
            s = v % 2
            if v - JT >= 2:
                act.wait_ge(rows_out[s], 32 * ((v - JT) // 2))
            for part in range(3):
                act.wait_ge(rows_turned, 3 * (v - JT) + part + 1)
                if part < 2:
                    act.activation(rows[s][:, 4 * part:4 * part + 4, :],
                                   ps[:, 6 + part, :].rearrange("p (t e) -> p t e", t=4), ACT.Copy
                                   ).then_inc(rows_ready, 1)
                else:
                    b = 6 if last else 3 * (1 - s) + 1
                    act.activation(rows[s][0:NS_TOK, QT, :], ps[0:NS_TOK, b, 0:P], ACT.Copy
                                   ).then_inc(rows_ready, 1)

        with nc.Block() as block:
            @block.sync
            def _(sp):
                sp.dma_start(cos[:, :], a["c_cos"]).then_inc(tab_in, 16)
                sp.dma_start(sin[:, :], a["c_sin"]).then_inc(tab_in, 16)
                with sp.Fori(0, JT // 2) as i:
                    for s in range(2):
                        load_unit(sp, U_ATT + 2 * i + s + 2, s, att_src(2 * i + s + 2))
                    for s in range(2):
                        sp.wait_ge(qr_ready, 2 * i + s + 1)
                        sp.dma_start(q_d[2 * i + s], qr[s][:, :]).then_inc(qr_out[s], 16)
                for u in range(JT, NQK):
                    s = u % 2
                    load_unit(sp, U_ATT + u + 2, s, att_src(u + 2))
                    if JT <= u - 1 < NR:
                        sp.wait_ge(qr_ready, u)
                        sp.dma_start(k_d[u - 1 - JT], qr[1 - s][:, :]).then_inc(qr_out[1 - s], 16)
                    v = u - 2
                    if v >= JT:
                        out_rows(sp, v)
                for u in range(NQK, NQK + 2):
                    load_unit(sp, U_ATT + u + 2, u % 2, att_src(u + 2))
                    out_rows(sp, u - 2)
                def gate(i, last):
                    for s in range(2):
                        if not last:
                            load_unit(sp, U_ATT + NQK + 2 * i + s + 2, s, att_src(NQK + 2 * i + s + 2))
                        else:
                            load_unit(sp, U_ATT + NQK + 2 * i + s + 2, s, out_src(w_aout, 0, s))
                    for s in range(2):
                        spill_gate(sp, i, s)
                for s in range(2):
                    spill_gate(sp, 0, s)
                with sp.Fori(1, JT // 2 - 1) as i:
                    gate(i, False)
                gate(JT // 2 - 1, True)
                for s in range(2):
                    sp.wait_ge(sga_out[s], 16 * JT // 2)
                    sp.wait_ge(qr_out[s], 16 * NR // 2)
                    sp.wait_ge(rows_out[s], 32 * NG)

            @block.tensor
            def _(pe):
                pe.wait_ge(Norm.lo_ready, norms[1].t + KD)

                def proj(u, s, first=False):
                    def before(c):
                        if c == 0 and not first:
                            pe.wait_ge(qs_ready, u - 1)
                        if c == 2 and not first:
                            pe.wait_ge(rs_ready, u - 1)
                    unit(pe, U_ATT + u, s, s, h_hi, h_lo, before_chunk=before)

                proj(0, 0, True)
                proj(1, 1, True)
                swap_mm(pe, 0, 0)
                with pe.Fori(1, JT // 2) as i:
                    for s in range(2):
                        u = 2 * i + s
                        proj(u, s)
                        swap_mm(pe, u - 1, 1 - s)

                def turn_rows(v):
                    s = v % 2
                    src = qr[s] if v < NR else qs[s]
                    if v < NR:
                        pe.wait_ge(qr_ready, v + 1)
                        pe.wait_ge(rs_ready, v + 1)
                    else:
                        pe.wait_ge(qs_ready, v + 1)
                        pe.wait_ge(rs_ready, min(v, NR))
                    pe.wait_ge(rows_ready, 3 * (v - JT))
                    for t in range(QT):
                        mm = pe.transpose(ps[:, 6 + t // 4, (t % 4) * P:(t % 4 + 1) * P],
                                          src[:, t * P:(t + 1) * P], ident)
                        if t % 4 == 3:
                            mm.then_inc(rows_turned, 1)
                    b = 3 * (1 - s) + 1
                    pe.wait_ge(qs_ready, v + 2)
                    pe.transpose(ps[0:NS_TOK, b, 0:P], src[:, NP_TOK:T], ident).then_inc(rows_turned, 1)

                for u in range(JT, NQK + 2):
                    s = u % 2

                    def before(c, u=u):
                        if c == 0:
                            pe.wait_ge(qs_ready, min(u - 1, NQK))
                        if c == 1 and u - 3 >= JT:
                            pe.wait_ge(rows_ready, 3 * (u - 3 - JT + 1))
                        if c == 2:
                            pe.wait_ge(rs_ready, min(u - 1, NR))
                    unit(pe, U_ATT + u, s, s, h_hi, h_lo, before_chunk=before)
                    if u - 2 >= JT:
                        turn_rows(u - 2) if u - 1 < NQK else None
                        if u - 1 < NQK:
                            pe.wait_ge(rows_ready, 3 * (u - 2 - JT) + 2)
                    if u - 1 < NR:
                        swap_mm(pe, u - 1, 1 - s)
                    if u == NQK:
                        turn_rows_last(pe, NQK - 1)

                with pe.Fori(1, JT // 2) as i:
                    for s in range(2):
                        u = NQK + 2 * i + s
                        pe.wait_ge(sga_done, 2 * i + s - 1)
                        unit(pe, U_ATT + u, s, s, h_hi, h_lo)

            @block.scalar
            def _(act):
                def copy_out(u, s, turn, first=False, scale=1.0):
                    act.wait_ge(w_used, U_ATT + u + 1)
                    make_hi(act, U_ATT + u + 2, s, turn)
                    if not first:
                        act.wait_ge(qr_ready, u - 1)
                    act.activation(chunks(qs[s][:, :]), pset(s), ACT.Copy, scale=scale).then_inc(qs_ready, 1)

                t0 = U_ATT // 2 + 2
                copy_out(0, 0, t0, True, SCALE)
                copy_out(1, 1, t0, True, SCALE)
                with act.Fori(1, JT // 2) as i:
                    for s in range(2):
                        copy_out(2 * i + s, s, t0 + i, scale=SCALE)
                for u in range(JT, NQK):
                    s = u % 2
                    act.wait_ge(w_used, U_ATT + u + 1)
                    make_hi(act, U_ATT + u + 2, s, t0 + u // 2)
                    act.wait_ge(qr_ready, min(u - 1, NR))
                    if u - 2 >= NR:
                        act.wait_ge(rows_turned, 3 * (u - 2 - JT + 1))
                    act.activation(chunks(qs[s][:, :]), pset(s), ACT.Copy).then_inc(qs_ready, 1)
                    if u - 2 >= JT:
                        rows_evac(act, u - 2)

                def silu(i, s, turn, u):
                    act.wait_ge(w_used, U_ATT + u + 1)
                    make_hi(act, U_ATT + u + 2, s, turn)
                    act.wait_ge(sga_out[s], 16 * i)
                    act.activation(chunks(sga[s][:, :]), pset(s), ACT.Silu).then_inc(sga_done, 1)

                act.wait_ge(w_used, U_ATT + NQK + 1)
                rows_evac(act, NQK - 2)
                silu(0, 0, t0 + NQK // 2, NQK)
                rows_evac(act, NQK - 1, True)
                silu(0, 1, t0 + NQK // 2, NQK + 1)
                with act.Fori(1, JT // 2) as i:
                    for s in range(2):
                        silu(i, s, t0 + NQK // 2 + i, NQK + 2 * i + s)

            @block.gpsimd
            def _(pool):
                pool.wait_ge(tab_in, 32)

                def rot(u, s, first=False):
                    make_lo(pool, U_ATT + u + 2, s)
                    pool.wait_ge(qs_ready, u + 1)
                    if not first:
                        pool.wait_ge(qr_ready, u - 1)
                    pool.tensor_tensor(qc[s][:, :], qs[s][:, :], cos[:, :], ALU.mult).then_inc(qc_ready, 1)
                rot(0, 0, True)
                rot(1, 1, True)
                with pool.Fori(1, JT // 2) as i:
                    for s in range(2):
                        rot(2 * i + s, s)
                for u in range(JT, NR):
                    rot(u, u % 2)
                with pool.Fori(NR // 2, (NQK + JT) // 2) as i:
                    for s in range(2):
                        make_lo(pool, U_ATT + 2 * i + s + 2, s)

            @block.vector
            def _(dve):
                dve.wait_ge(tab_in, 32)

                def rot(u, s, out_turn):
                    dve.wait_ge(swapped, u + 1)
                    for c, b in enumerate((6, 7, 3 * s + 2)):
                        ins = dve.tensor_tensor(rsn[s][:, c * CH:(c + 1) * CH], ps[:, b, 0:CH],
                                                sin[:, c * CH:(c + 1) * CH], ALU.mult)
                        if c == 2:
                            ins.then_inc(rs_ready, 1)
                    dve.wait_ge(rs_ready, u + 1)
                    dve.wait_ge(qc_ready, u + 1)
                    dve.wait_ge(qr_out[s], out_turn)
                    dve.tensor_tensor(qr[s][:, :], qc[s][:, :], rsn[s][:, :], ALU.add).then_inc(qr_ready, 1)
                with dve.Fori(0, JT // 2) as i:
                    for s in range(2):
                        rot(2 * i + s, s, 16 * i)
                for u in range(JT, NR):
                    if u - 2 >= JT:
                        dve.wait_ge(rows_turned, 3 * (u - 2 - JT) + 3)
                    rot(u, u % 2, 16 * (u // 2))

        OG = place("OG", [P, JT, T], F32, slot(16))
        kraw = place("kraw", [P, NP_TOK], F32, slot(32))
        vraw = place("vraw", [P, QT, P], F32, slot(33))
        khi = place("khi", [P, NP_TOK], F32R, slot(34))
        klo = place("klo", [P, NP_TOK], F32R, slot(35))
        vhi = place("vhi", [P, QT, P], F32R, slot(36))
        vlo = place("vlo", [P, QT, P], F32R, slot(37))
        qraw = [place(f"qraw{s}", [P, NP_TOK], F32, slot(38 + s)) for s in range(2)]
        qhi = [place(f"qhi{s}", [P, NP_TOK], F32R, slot(40 + s)) for s in range(2)]
        qlo = [place(f"qlo{s}", [P, NP_TOK], F32R, slot(42 + s)) for s in range(2)]
        ssq = place("ssq", [P, JT * QT], F32, slot(45))
        at = slot(0)
        aThi = [place("aThi0", [P, 4, 512], F32R, at), place("aThi1", [P, 8, 512], F32R, at)]
        aTlo = [place("aTlo0", [P, 4, 512], F32R, at), place("aTlo1", [P, 8, 512], F32R, at)]
        osq = place("osq", [P, 512], F32, at)
        identr = place("identr", [P, P], F32R, at)
        causalr = place("causalr", [P, P], F32R, at)
        stats = place("stats", [P, 4, 8], F32, at)
        p1 = [place(f"p1_{s}", [P, NP_TOK], F32, [raw_at[s]]) for s in range(2)]
        p0 = [place(f"p0_{s}", [P, NP_TOK], F32, slot(46) if s == 3 else at) for s in range(4)]
        assert at[0] <= slot(16)[0] and slot(46)[0] + 4 * NP_TOK <= 229344
        kraw_in, vraw_in = sem("kraw_in"), sem("vraw_in")
        qraw_in = [sem("qraw_in0"), sem("qraw_in1")]
        consts_r, kvhi_ready, k_ready, v_ready, qhi_ready, qlo_ready = (sem(x) for x in (
            "consts_r", "kvhi_ready", "k_ready", "v_ready", "qhi_ready", "qlo_ready"))
        s_done, mx_done, exp_done, rc_done, pn_done, comb_done = (sem(x) for x in (
            "scores_done", "max_done", "exp_done", "recip_done", "p1_scaled", "a_ready"))
        tg_done, hi_done, lo_done, pv_done, oev, n_done, ssq_done, og_done = (sem(x) for x in (
            "turn_group", "aT_hi", "aT_lo", "pv_done", "o_copied", "osq_total", "ssq_copied", "og_done"))
        p1_begun = sem("p1_begun")
        NX = GH * QT
        PRE = 12
        TAIL = 8

        def tgroups(x):
            j, i = divmod(x, QT)
            first = 12 * j + (i if i < 4 else 4 + 2 * (i - 4))
            return [(first + n, 4 * n, min(4, i + 1 - 4 * n)) for n in range(i // 4 + 1)]

        def score_ap(i, c):
            w = P * (i + 1)
            if i < 4:
                return ps[:, 2 * (i % 2) + c, 0:w]
            return ps[:, 2 * c:2 * c + 2, :].rearrange("p b n -> p (b n)")[:, 0:w]

        with nc.Block() as block:
            @block.sync
            def _(sp):
                def load_q(h, s):
                    sp.dma_start(qraw[s][:, :], q_d[h][:, 0:NP_TOK]).then_inc(qraw_in[s], 16)

                def load_k(g):
                    sp.dma_start(kraw[:, :], k_d[g][:, 0:NP_TOK]).then_inc(kraw_in, 16)

                def load_v(g):
                    v = o["v_rows_prompt"][0, 0].rearrange("(n p) g e -> p n (g e)", p=P)
                    sp.dma_start(vraw[:, :, :], v[:, :, bass.ds(g * VD, VD)]).then_inc(vraw_in, 16)

                load_k(0)
                load_q(0, 0)
                load_q(1, 1)
                load_v(0)
                sp.wait_ge(qlo_ready, 1)
                load_q(2, 0)

                def body(g, last=False):
                    for j in range(GH):
                        h = GH * g + j
                        if j == 0 and not last:
                            sp.wait_ge(k_ready, g + 1)
                            load_k(g + 1)
                            sp.wait_ge(v_ready, g + 1)
                            load_v(g + 1)
                        if j + 3 < GH or not last:
                            sp.wait_ge(qlo_ready, h + 2)
                            load_q(h + 3, (j + 3) % 2)
                with sp.Fori(0, NG - 1) as g:
                    body(g)
                body(NG - 1, last=True)

            @block.tensor
            def _(pe):
                def scores(g, x, c):
                    j, i = divmod(x, QT)
                    s, w = j % 2, P * (i + 1)
                    if c == 0 and x % NX == 0:
                        pe.wait_ge(k_ready, g + x // NX + 1)
                    if c == 0 and i == 0:
                        pe.wait_ge(qlo_ready, GH * g + j + 1)
                    if x >= 2:
                        if i < 2:
                            need = (x - 1, 0) if i == 0 else (x - 2, 1)
                        elif i < 4:
                            need = (x - 2, c)
                        elif i == 4:
                            need = (x - 2, 1) if c == 0 else (x - 1, 1)
                        else:
                            need = (x - 1, c)
                        pe.wait_ge(exp_done, 2 * NX * g + 2 * need[0] + need[1] + 1)
                    dst = score_ap(i, c)
                    rows_ = slice(HD * c, HD * c + HD)
                    for n, (ql, kr) in enumerate(((qhi, khi), (qhi, klo), (qlo, khi))):
                        for c0 in range(0, w, 512):
                            c1 = min(w, c0 + 512)
                            pe.matmul(dst[:, c0:c1], ql[s][rows_, i * P:(i + 1) * P], kr[rows_, c0:c1],
                                      start=n == 0, stop=n == 2 and c1 < w)
                    pe.matmul(dst[:, i * P:w], identr[:, :], causalr[:, :], start=False, stop=True
                              ).then_inc(s_done, 1)

                def turn(g, x):
                    pe.wait_ge(comb_done, NX * g + x + 1)
                    for tg, b0, nb in tgroups(x):
                        if tg >= 2:
                            pe.wait_ge(lo_done, 12 * GH * g + tg - 1)
                        for b in range(b0, b0 + nb):
                            mm = pe.transpose(ps[:, 4 + tg % 2, (b - b0) * P:(b - b0 + 1) * P],
                                              p0[x % 4][:, b * P:(b + 1) * P], ident)
                        mm.then_inc(tg_done, 1)

                def values(g, j, half, blocks):
                    nb = 4 + 4 * half
                    if blocks[0] == 0:
                        if half == 0:
                            pe.wait_ge(v_ready, g + j // GH + 1)
                        pe.wait_ge(lo_done, 12 * GH * g + 12 * j + (4 if half == 0 else 12))
                        if j >= 1:
                            pe.wait_ge(ssq_done, 2 * (GH * g + j - 1) + half + 1)
                    for b in blocks:
                        c0 = max(0, b - 4 * half) * P
                        for n, (v, at_) in enumerate(((vhi, aThi), (vhi, aTlo), (vlo, aThi))):
                            mm = pe.matmul(ps[:, 6 + half, c0:512], v[:, b, :], at_[half][:, b, c0:512],
                                           start=b == 0 and n == 0, stop=b == nb - 1 and n == 2)
                    if blocks[-1] == nb - 1:
                        mm.then_inc(pv_done, 1)

                def total(g, j, half):
                    pe.wait_ge(oev, 2 * (GH * g + j) + half + 1)
                    for q in range(4):
                        mm = pe.matmul(ps[:, 6 + half, q:q + 1], osq[:, q * P:(q + 1) * P], ones[:, 0:1],
                                       start=True, stop=True)
                    mm.then_inc(n_done, 1)

                VALUES = {0: (0, (0, 1)), 1: (0, (2, 3)), 2: (1, (0, 1, 2)), 3: (1, (3, 4, 5)), 4: (1, (6, 7))}
                TOTALS = {3: 0, 6: 1}

                def step(g, x, top):
                    j, i = divmod(x, QT)
                    late = x % NX == 0
                    if x < top and not late:
                        scores(g, x, 0)
                        scores(g, x, 1)
                    if 0 <= x - 2 < top:
                        turn(g, x - 2)
                    if i in VALUES and 1 <= j <= top // QT:
                        values(g, j - 1, *VALUES[i])
                    if x < top and late:
                        scores(g, x, 0)
                        scores(g, x, 1)
                    if i in TOTALS and 1 <= j <= top // QT:
                        total(g, j - 1, TOTALS[i])

                pe.wait_ge(consts_r, 2)
                for x in range(PRE):
                    step(0, x, NX)
                with pe.Fori(0, NG - 1) as g:
                    for x in range(PRE, NX + PRE):
                        step(g, x, 2 * NX)
                for x in range(PRE, NX + TAIL):
                    step(NG - 1, x, NX)

            @block.scalar
            def _(act):
                def q_hi(g, j):
                    act.wait_ge(qraw_in[j % 2], 16 * (2 * g + j // 2 + 1))
                    if j >= 2:
                        act.wait_ge(s_done, 2 * NX * g + 2 * QT * (j - 1))
                    act.activation(qhi[j % 2][:, :], qraw[j % 2][:, :], ACT.Copy).then_inc(qhi_ready, 1)

                def k_hi(g):
                    act.wait_ge(kraw_in, 16 * (g + 1))
                    act.wait_ge(s_done, 2 * NX * g)
                    act.activation(khi[:, :], kraw[:, :], ACT.Copy).then_inc(kvhi_ready, 1)

                def v_hi(g):
                    act.wait_ge(vraw_in, 16 * (g + 1))
                    act.wait_ge(pv_done, 2 * GH * g)
                    act.activation(vhi[:, :, :], vraw[:, :, :], ACT.Copy).then_inc(kvhi_ready, 1)

                def exp(g, x, c):
                    i = x % QT
                    act.wait_ge(mx_done, 2 * NX * g + 2 * x + c + 1)
                    if c == 0 and x >= 4:
                        act.wait_ge(tg_done, 12 * GH * g + tgroups(x - 4)[-1][0] + 1)
                    if c == 1 and x >= 2:
                        act.wait_ge(comb_done, NX * g + x - 1)
                    dst = p0[x % 4] if c == 0 else p1[x % 2]
                    act.activation(dst[:, 0:P * (i + 1)], score_ap(i, c), ACT.Exp,
                                   bias=stats[:, x % 4, c:c + 1],
                                   accum_out=stats[:, x % 4, 2 + c:3 + c]).then_inc(exp_done, 1)

                def hi(g, x):
                    j, i = divmod(x, QT)
                    half = i // 4
                    if j >= 1 and i % 4 == 0:
                        act.wait_ge(pv_done, 2 * (GH * g + j - 1) + half + 1)
                    for tg, b0, nb in tgroups(x):
                        act.wait_ge(tg_done, 12 * GH * g + tg + 1)
                        act.activation(aThi[half][:, b0:b0 + nb, (i % 4) * P:(i % 4 + 1) * P],
                                       ps[:, 4 + tg % 2, 0:nb * P].rearrange("p (b n) -> p b n", b=nb),
                                       ACT.Copy).then_inc(hi_done, 1)

                def output(g, j, half):
                    act.wait_ge(pv_done, 2 * (GH * g + j) + half + 1)
                    act.wait_ge(n_done, 2 * (GH * g + j) + half)
                    act.activation(OG[:, bass.ds(GH * g + j, 1), 512 * half:512 * half + 512].rearrange(
                        "p o n -> p (o n)"), ps[:, 6 + half, :], ACT.Copy)
                    act.activation(osq[:, :], ps[:, 6 + half, :], ACT.Square).then_inc(oev, 1)

                def sums(g, j, half):
                    act.wait_ge(n_done, 2 * (GH * g + j) + half + 1)
                    act.activation(ssq[:, bass.ds(QT * (GH * g + j) + 4 * half, 4)], ps[:, 6 + half, 0:4], ACT.Copy
                                   ).then_inc(ssq_done, 1)

                OUTPUTS, SUMS = {2: 0, 5: 1}, {4: 0, 7: 1}

                def step(g, x, top):
                    j, i = divmod(x, QT)
                    if x < top:
                        exp(g, x, 0)
                        exp(g, x, 1)
                    if x == NX - 1 and top > NX:
                        k_hi(g + 1)
                    if 0 <= x - 2 < top:
                        hi(g, x - 2)
                    if x % NX == 5 and x < top:
                        v_hi(g + x // NX)
                    if i == 4 and QT * (j + 1) < top:
                        q_hi(g, j + 1)
                    if i in OUTPUTS and 1 <= j <= top // QT:
                        output(g, j - 1, OUTPUTS[i])
                    if i in SUMS and 1 <= j <= top // QT:
                        sums(g, j - 1, SUMS[i])

                act.activation(identr[:, :], ident, ACT.Copy).then_inc(consts_r, 1)
                act.activation(causalr[:, :], causal, ACT.Copy).then_inc(consts_r, 1)
                k_hi(0)
                q_hi(0, 0)
                for x in range(PRE):
                    step(0, x, NX)
                with act.Fori(0, NG - 1) as g:
                    for x in range(PRE, NX + PRE):
                        step(g, x, 2 * NX)
                for x in range(PRE, NX + TAIL):
                    step(NG - 1, x, NX)

            @block.vector
            def _(dve):
                def k_lo(g):
                    dve.wait_ge(kvhi_ready, 2 * g + 1)
                    dve.tensor_tensor(klo[:, :], kraw[:, :], khi[:, :].bitcast(F32), ALU.subtract).then_inc(k_ready, 1)

                def recip(g, x):
                    dve.wait_ge(exp_done, 2 * NX * g + 2 * x + 2)
                    dve.reciprocal(stats[:, x % 4, 4:6], stats[:, x % 4, 2:4]).then_inc(rc_done, 1)

                def maxes(g, x):
                    for c in range(2):
                        dve.wait_ge(s_done, 2 * NX * g + 2 * x + c + 1)
                        dve.tensor_reduce(stats[:, x % 4, c:c + 1], score_ap(x % QT, c), AX.X, ALU.max,
                                          negate=True).then_inc(mx_done, 1)

                def combine(g, x):
                    w = P * (x % QT + 1)
                    dve.wait_ge(pn_done, NX * g + x + 1)
                    dve.scalar_tensor_tensor(out=p0[x % 4][:, 0:w], in0=p0[x % 4][:, 0:w],
                                             scalar=stats[:, x % 4, 4:5], in1=p1[x % 2][:, 0:w],
                                             op0=ALU.mult, op1=ALU.add).then_inc(comb_done, 1)

                def lo(g, x):
                    i = x % QT
                    half = i // 4
                    for tg, b0, nb in tgroups(x):
                        dve.wait_ge(hi_done, 12 * GH * g + tg + 1)
                        cs = slice((i % 4) * P, (i % 4 + 1) * P)
                        dve.tensor_tensor(aTlo[half][:, b0:b0 + nb, cs],
                                          ps[:, 4 + tg % 2, 0:nb * P].rearrange("p (b n) -> p b n", b=nb),
                                          aThi[half][:, b0:b0 + nb, cs].bitcast(F32), ALU.subtract
                                          ).then_inc(lo_done, 1)

                def step(g, x, top):
                    j, i = divmod(x, QT)
                    if 0 <= x - 1 < top:
                        recip(g, x - 1)
                    if x < top:
                        maxes(g, x)
                    if 0 <= x - 1 < top:
                        combine(g, x - 1)
                    if 0 <= x - 2 < top:
                        lo(g, x - 2)
                    if x == NX - 1 and top > NX:
                        k_lo(g + 1)

                k_lo(0)
                for x in range(PRE):
                    step(0, x, NX)
                with dve.Fori(0, NG - 1) as g:
                    for x in range(PRE, NX + PRE):
                        step(g, x, 2 * NX)
                for x in range(PRE, NX + TAIL):
                    step(NG - 1, x, NX)

            @block.gpsimd
            def _(pool):
                def q_lo(g, j):
                    s = j % 2
                    pool.wait_ge(qhi_ready, GH * g + j + 1)
                    pool.tensor_tensor(qlo[s][:, :], qraw[s][:, :], qhi[s][:, :].bitcast(F32), ALU.subtract
                                       ).then_inc(qlo_ready, 1)

                def v_lo(g):
                    pool.wait_ge(kvhi_ready, 2 * g + 2)
                    pool.tensor_tensor(vlo[:, :, :], vraw[:, :, :], vhi[:, :, :].bitcast(F32), ALU.subtract
                                       ).then_inc(v_ready, 1)

                def step(g, x, top):
                    j, i = divmod(x, QT)
                    if x < top:
                        w = P * (i + 1)
                        pool.wait_ge(rc_done, NX * g + x + 1)
                        pool.sem_inc(p1_begun, 1)
                        pool.tensor_scalar(p1[x % 2][:, 0:w], p1[x % 2][:, 0:w], stats[:, x % 4, 5:6], neglam,
                                           ALU.mult, ALU.mult).then_inc(pn_done, 1)
                    if i == 4 and QT * (j + 1) < top:
                        q_lo(g, j + 1)
                    if x % NX == 5 and x < top:
                        v_lo(g + x // NX)

                q_lo(0, 0)
                for x in range(PRE):
                    step(0, x, NX)
                with pool.Fori(0, NG - 1) as g:
                    for x in range(PRE, NX + PRE):
                        step(g, x, 2 * NX)
                for x in range(PRE, NX + TAIL):
                    step(NG - 1, x, NX)

        at = slot(0)
        kpage = [place(f"kpage{s}", [P, PAGES, NG * VD], F32, at) for s in range(2)]
        vpage = [place(f"vpage{s}", [P, PAGES, NG * VD], F32, at) for s in range(2)]
        assert at[0] <= slot(16)[0]
        at = slot(32)
        kT = place("kT", [P, 2, PAST], F32, at)
        pd = place("p_dec", [P, PAST + NT], F32, at)
        aTd = place("aT_dec", [P, PAGES, NG * GH * NT], F32, at)
        aTn = place("aT_new", [NT, NG * GH * NT], F32, at)
        qsT = place("q_samples", [P, JT, NS_TOK], F32, at)
        knew = place("k_new", [P, NG, NS_TOK], F32, at)
        vnew = [place(f"v_new{s}", [NT, NG * VD], F32, at) for s in range(2)]
        Qz = place("Qz", [P, NG, P], F32, at)
        zc = place("zc", [P, NG * GH * NT], F32, at)
        snew = place("snew", [P, NT], F32, at)
        st6 = place("stat_dec", [P, 8], F32, at)
        ptab = nc.alloc_sbuf_tensor_at("ptab", [1, NB * PAGES], I32, offset=at[0])
        at[0] += 256
        rT = place("rT", [P, P], F32, at)
        rb = [place(f"rb{s}", [P, NP_TOK], F32, at) for s in range(2)]
        sgh = [place(f"sgh{s}", [P, NP_TOK], F32, at) for s in range(2)]
        sgs = place("sg_samples", [P, JT, NS_TOK], F32, at)
        dsq = place("dsq", [P, JT * NS_TOK], F32, at)
        dstd = place("dstd", [P, JT * NS_TOK], F32, at)
        assert at[0] <= slot(45)[0]
        pt_in, qk_in, og_scaled = sem("pt_in"), sem("qk_in"), sem("og_scaled")
        rb_in = [sem("rb_in0"), sem("rb_in1")]
        root_step = sem("root_step")
        keys_in = [sem("keys_in0"), sem("keys_in1")]
        values_in = [sem("values_in0"), sem("values_in1")]
        qz_zero, qz_ready, kt_turned, kev_act, kev_dve, ds_done = (sem(x) for x in (
            "qz_zero", "qz_ready", "kt_turned", "kev_act", "kev_dve", "dscore_done"))
        dmx, dexp, zc_ready, at_turned, at_ready, dpv_done, do_ready = (sem(x) for x in (
            "dmax", "dexp", "zc_ready", "aT_turned", "aT_ready", "dpv_done", "do_ready"))
        smp_step = sem("smp_step")
        n_phys = a["cache_k"].shape[1]
        JOIN_AFTER = 2

        with nc.Block() as block:
            @block.sync
            def _(sp):
                sp.dma_start(ptab[:, :], a["page_table"].rearrange("(o b) p -> o (b p)", o=1)).then_inc(pt_in, 16)
                sp.dma_start(qsT[:, :, :], q_d.rearrange("j p n -> p j n")[:, :, NP_TOK:T]).then_inc(qk_in, 16)
                sp.dma_start(knew[:, :, :], k_d.rearrange("g p n -> p g n")[:, :, NP_TOK:T]).then_inc(qk_in, 16)
                sp.dma_start(sgs[:, :, :], gate_d[1].rearrange("j p n -> p j n")[:, :, NP_TOK:T]).then_inc(qk_in, 16)
                sp.wait_ge(pt_in, 16)

                def page_number(b, page):
                    return sp.value_load(ptab[0:1, bass.ds(b * PAGES + page, 1)], min_val=0, max_val=n_phys - 1)

                def load_keys(b, s, free=None):
                    for page in range(PAGES):
                        n = page_number(b, page)
                        if page == 0 and free is not None:
                            sp.wait_ge(*free)
                        sp.dma_start(kpage[s][:, page, :], a["cache_k"][0][bass.ds(n, 1)].rearrange(
                            "o p g e -> (o p) (g e)")).then_inc(keys_in[s], 16)

                def load_values(b, s, free=None):
                    for page in range(PAGES):
                        n = page_number(b, page)
                        if page == 0 and free is not None:
                            sp.wait_ge(*free)
                        sp.dma_start(vpage[s][:, page, :], a["cache_v"][0][bass.ds(n, 1)].rearrange(
                            "o p g e -> (o p) (g e)")).then_inc(values_in[s], 16)
                    sp.dma_start(vnew[s][:, :], o["v_rows_sample"][0][bass.ds(b, 1)].rearrange(
                        "o t g e -> (o t) (g e)")).then_inc(values_in[s], 16)
                def load_gates(h, s):
                    sp.dma_start(rb[s][:, :], rstd_d[h].partition_broadcast(P)).then_inc(rb_in[s], 16)
                    sp.dma_start(sgh[s][:, :], gate_d[1][h][:, 0:NP_TOK]).then_inc(rb_in[s], 16)

                load_keys(0, 0)
                load_values(0, 0)
                sp.wait_ge(root_step, 4)
                sp.dma_start(rstd_d.rearrange("h (q n) -> (h q) n", q=QT), rT[:, :]).then_inc(root_step, 16)
                load_keys(1, 1)
                sp.wait_ge(root_step, 4 + 16)
                for s in range(2):
                    load_gates(s, s)
                load_values(1, 1)
                with sp.Fori(0, NB // 2 - 1) as i:
                    for s in range(2):
                        b = 2 * i + s
                        load_keys(b + 2, s, free=(kt_turned, 2 * NG * (b + 1)))
                        for t in range(2):
                            sp.wait_ge(og_done, 2 * b + t + 1)
                            load_gates(2 * b + 2 + t, t)
                        load_values(b + 2, s, free=(dpv_done, b + 1))
                for t in range(2):
                    sp.wait_ge(og_done, JT - 4 + t + 1)
                    load_gates(JT - 2 + t, t)

            @block.tensor
            def _(pe):
                def turn_pages(b, s, g):
                    if g >= 2:
                        pe.wait_ge(ds_done, NG * b + g - 1)
                    for half in range(2):
                        f = 2 * g + half
                        if f >= 3:
                            e = kev_act if (f - 3) % 2 == 0 else kev_dve
                            pe.wait_ge(e, NG * b + (f - 3) // 2 + 1)
                        for q in range(4):
                            mm = pe.transpose(ps[:, 3 + f % 3, q * P:(q + 1) * P],
                                              kpage[s][:, 4 * half + q, g * VD:(g + 1) * VD], ident)
                        mm.then_inc(kt_turned, 1)

                def score(b, g):
                    for half in range(2):
                        pe.wait_ge(kev_act if half == 0 else kev_dve, NG * b + g + 1)
                        pe.matmul(ps[:, half, :], Qz[:, g, :], kT[:, g % 2, 512 * half:512 * half + 512],
                                  start=g == 0, stop=g == NG - 1)
                    pe.matmul(ps[:, 2, 0:NT], Qz[:, g, :], knew[:, g, bass.ds(NT * b, NT)],
                              start=g == 0, stop=g == NG - 1).then_inc(ds_done, 1)

                def join(b):
                    pe.wait_ge(zc_ready, b + 1)
                    for page in range(PAGES):
                        pe.matmul(ps[:, 6, 64 * page:64 * page + 64], pd[:, page * P:(page + 1) * P], zc[:, :],
                                  start=True, stop=True)
                    pe.wait_ge(do_ready, b)
                    pe.matmul(ps[0:NT, 7, 64:128], pd[:, PAST:PAST + NT], zc[:, :], start=True, stop=True
                              ).then_inc(at_turned, 1)

                def scores(b, s, i, before=None):
                    pe.wait_ge(keys_in[s], 16 * PAGES * (i + 1))
                    turn_pages(b, s, 0)
                    if before is None:
                        pe.wait_ge(qk_in, 48)
                    for g in range(NG):
                        if g + 1 < NG:
                            turn_pages(b, s, g + 1)
                        if g == 0:
                            pe.wait_ge(qz_ready, b + 1)
                            if before is not None:
                                pe.wait_ge(dexp, b)
                        score(b, g)
                        if g == 1 and before is not None:
                            join(before)

                def values(b, s, i):
                    pe.wait_ge(values_in[s], 16 * (PAGES + 1) * (i + 1))
                    pe.wait_ge(at_ready, 2 * b + 2)
                    for g in range(NG):
                        cs = slice(16 * g, 16 * g + 16)
                        for page in range(PAGES):
                            pe.matmul(ps[:, 7, cs], vpage[s][:, page, g * VD:(g + 1) * VD], aTd[:, page, cs],
                                      start=page == 0, stop=False)
                        mm = pe.matmul(ps[:, 7, cs], vnew[s][:, g * VD:(g + 1) * VD], aTn[:, cs],
                                       start=False, stop=True)
                    mm.then_inc(dpv_done, 1)

                scores(0, 0, 0)
                pe.wait_ge(root_step, 2)
                pe.transpose(ps[:, 7, 0:P], ssq[:, :], ident).then_inc(root_step, 1)
                pe.wait_ge(root_step, 4)
                with pe.Fori(0, NB // 2 - 1) as i:
                    for s in range(2):
                        b = 2 * i + s
                        scores(b + 1, 1 - s, i + s, before=b)
                        values(b, s, i)
                scores(NB - 1, 1, NB // 2 - 1, before=NB - 2)
                values(NB - 2, 0, NB // 2 - 1)
                join(NB - 1)
                values(NB - 1, 1, NB // 2 - 1)
                pe.wait_ge(smp_step, 1)
                pe.matmul(ps[:, 0, :], ones[:, :], dsq[:, :], start=True, stop=True).then_inc(smp_step, 1)

            @block.scalar
            def _(act):
                def keys_out(b, g):
                    act.wait_ge(kt_turned, 2 * NG * b + 2 * g + 1)
                    if g >= 2:
                        act.wait_ge(ds_done, NG * b + g - 1)
                    act.activation(kT[:, g % 2, 0:512], ps[:, 3 + (2 * g) % 3, :], ACT.Copy).then_inc(kev_act, 1)

                def exps(b):
                    act.wait_ge(dmx, b + 1)
                    act.activation(pd[:, 0:PAST], ps[:, 0:2, :].rearrange("p b n -> p (b n)"), ACT.Exp,
                                   bias=st6[:, 2:3], accum_out=st6[:, 3:4])
                    act.activation(pd[:, PAST:PAST + NT], snew[:, :], ACT.Exp,
                                   bias=st6[:, 2:3], accum_out=st6[:, 4:5]).then_inc(dexp, 1)

                def joined_out(b):
                    act.wait_ge(at_turned, b + 1)
                    act.activation(aTd[:, :, :].rearrange("p a n -> p (a n)"), ps[:, 6, :], ACT.Copy
                                   ).then_inc(at_ready, 1)

                def values_out(b):
                    act.wait_ge(dpv_done, b + 1)
                    act.activation(OG[:, :, bass.ds(NP_TOK + NT * b, NT)],
                                   ps[:, 7, 0:64].rearrange("p (h t) -> p h t", t=NT), ACT.Copy).then_inc(do_ready, 1)
                act.activation(ssq[:, :], ssq[:, :], ACT.Sqrt, scale=1.0 / VD, bias=eps_rms).then_inc(root_step, 1)
                for g in range(NG):
                    keys_out(0, g)
                act.wait_ge(root_step, 3)
                act.activation(rT[:, :], ps[:, 7, 0:P], ACT.Copy).then_inc(root_step, 1)
                exps(0)
                with act.Fori(0, NB - 1) as b:
                    for g in range(NG):
                        keys_out(b + 1, g)
                        if g == JOIN_AFTER:
                            joined_out(b)
                    exps(b + 1)
                    values_out(b)
                joined_out(NB - 1)
                values_out(NB - 1)
                act.wait_ge(do_ready, NB)
                act.activation(dsq[:, :].rearrange("p (h n) -> p h n", h=JT), OG[:, :, NP_TOK:T], ACT.Square
                               ).then_inc(smp_step, 1)
                act.wait_ge(smp_step, 2)
                act.activation(dstd[:, :], ps[:, 0, :], ACT.Sqrt, scale=1.0 / VD, bias=eps_rms).then_inc(smp_step, 1)

            @block.vector
            def _(dve):
                dve.memset(Qz[:, :, :], 0.0).then_inc(qz_zero, 1)
                dve.wait_ge(root_step, 1)
                dve.reciprocal(ssq[:, :], ssq[:, :]).then_inc(root_step, 1)
                dve.wait_ge(qz_zero, 1)
                dve.wait_ge(qk_in, 48)
                qz_ap = Qz[:, :, :]
                step = qz_ap.ap[0][0]

                def queries(b):
                    dve.wait_ge(ds_done, NG * b)
                    for c in range(2):
                        dst = bass.AP(qz_ap.tensor, HD * c * step + 16 * c,
                                      [[step, HD], [P + 32, NG], [NT, GH], [1, NT]])
                        src = qsT[HD * c:HD * c + HD, :, bass.ds(NT * b, NT)].rearrange("p (g h) t -> p g h t", g=NG)
                        ins = dve.tensor_copy(dst, src)
                    ins.then_inc(qz_ready, 1)

                def keys_out(b, g):
                    dve.wait_ge(kt_turned, 2 * NG * b + 2 * g + 2)
                    if g >= 2:
                        dve.wait_ge(ds_done, NG * b + g - 1)
                    dve.tensor_copy(kT[:, g % 2, 512:1024], ps[:, 3 + (2 * g + 1) % 3, :]).then_inc(kev_dve, 1)

                def softmax(b):
                    dve.wait_ge(ds_done, NG * b + NG)
                    dve.tensor_tensor(snew[:, :], ps[:, 2, 0:NT], newmask, ALU.add
                                      ).then_inc(dve_step.sem, dve_step.up())
                    dve.tensor_reduce(st6[:, 0:1], ps[:, 0:2, :].rearrange("p b n -> p (b n)"), AX.X, ALU.max,
                                      negate=True)
                    dve.wait_ge(dve_step.sem, dve_step.now())
                    dve.tensor_reduce(st6[:, 1:2], snew[:, :], AX.X, ALU.max, negate=True
                                      ).then_inc(dve_step.sem, dve_step.up())
                    dve.wait_ge(dve_step.sem, dve_step.now())
                    dve.tensor_tensor(st6[:, 2:3], st6[:, 0:1], st6[:, 1:2], ALU.min).then_inc(dmx, 1)
                    dve.wait_ge(dexp, b + 1)
                    dve.tensor_tensor(st6[:, 5:6], st6[:, 3:4], st6[:, 4:5], ALU.add
                                      ).then_inc(dve_step.sem, dve_step.up())
                    dve.wait_ge(dve_step.sem, dve_step.now())
                    dve.reciprocal(st6[:, 6:7], st6[:, 5:6]).then_inc(dve_step.sem, dve_step.up())
                    dve.wait_ge(dve_step.sem, dve_step.now())
                    dve.tensor_tensor(st6[:, 7:8], st6[:, 6:7], rowcoef, ALU.mult
                                      ).then_inc(dve_step.sem, dve_step.up())
                    dve.wait_ge(dve_step.sem, dve_step.now())
                    dve.tensor_scalar(zc[:, :], rowsel, st6[:, 7:8], None, ALU.mult).then_inc(zc_ready, 1)

                def joined_out(b):
                    dve.wait_ge(dpv_done, b)
                    dve.wait_ge(at_turned, b + 1)
                    dve.tensor_copy(aTn[:, :], ps[0:NT, 7, 64:128]).then_inc(at_ready, 1)

                def scale(h, s, n):
                    og = OG[:, bass.ds(h, 1), 0:NP_TOK].rearrange("p o n -> p (o n)")
                    dve.wait_ge(rb_in[s], 32 * (n + 1))
                    dve.scalar_tensor_tensor(out=og, in0=og, scalar=subg, in1=rb[s][:, :], op0=ALU.mult,
                                             op1=ALU.mult).then_inc(og_scaled, 1)
                queries(0)
                for g in range(NG):
                    keys_out(0, g)
                softmax(0)
                with dve.Fori(0, NB - 1) as b:
                    dve_step.enter(b, 0, 5)
                    queries(b + 1)
                    for g in range(NG):
                        keys_out(b + 1, g)
                        if g == JOIN_AFTER:
                            joined_out(b)
                    softmax(b + 1)
                    for s in range(2):
                        scale(2 * b + s, s, b)
                dve_step.leave(NB - 1)
                joined_out(NB - 1)
                for s in range(2):
                    scale(JT - 2 + s, s, NB - 1)
                og = OG[:, :, NP_TOK:T]
                d3 = dstd[:, :].rearrange("p (h n) -> p h n", h=JT)
                dve.wait_ge(smp_step, 3)
                dve.reciprocal(dstd[:, :], dstd[:, :]).then_inc(smp_step, 1)
                dve.wait_ge(smp_step, 4)
                dve.scalar_tensor_tensor(out=og, in0=og, scalar=subg, in1=d3, op0=ALU.mult, op1=ALU.mult
                                         ).then_inc(smp_step, 1)
                dve.wait_ge(smp_step, 5)
                dve.tensor_tensor(og, og, sgs[:, :, :], ALU.mult).then_inc(smp_step, 1)

            @block.gpsimd
            def _(pool):
                with pool.Fori(0, JT // 2) as i:
                    for s in range(2):
                        h = 2 * i + s
                        og = OG[:, bass.ds(h, 1), 0:NP_TOK].rearrange("p o n -> p (o n)")
                        pool.wait_ge(og_scaled, h + 1)
                        pool.tensor_tensor(og, og, sgh[s][:, :], ALU.mult).then_inc(og_done, 1)
                pool.wait_ge(smp_step, 6)

        yo = [place(f"yo{s}", [P, D], F32, slot(0 + s)) for s in range(2)]
        ohi_ready, olo_ready, yn_ready, y_turned, yo_act, yo_dve = (sem(x) for x in (
            "ohi_ready", "olo_ready", "yn_ready", "y_turned", "yo_act", "yo_dve"))
        y_out = [sem("y_out0"), sem("y_out1")]
        with nc.Block() as block:
            @block.sync
            def _(sp):
                out_proj_sp(sp, outp[1], U_AOUT, w_aout, res_d[1], None)
                for t in range(NXT):
                    n = tok_rows(t)
                    sp.wait_ge(yo_act, t + 1)
                    sp.wait_ge(yo_dve, t + 1)
                    dst = o["y_prompt"][0, t * P:(t + 1) * P, :] if t < QT else \
                        o["y_sample"].rearrange("b t d -> (b t) d")
                    sp.dma_start(dst, yo[t % 2][0:n, :]).then_inc(y_out[t % 2], 16)
                sp.wait_ge(y_out[0], 16 * 5)
                sp.wait_ge(y_out[1], 16 * 4)

            @block.tensor
            def _(pe):
                out_proj_pe(pe, outp[1], U_AOUT, olo_ready)
                norm_total_after(pe, outp[1], norms[2])
                pe.wait_ge(Norm.rstd_ready, norms[2].o + 1)
                pe.wait_ge(yn_ready, KD)
                for t in range(NXT):
                    n = tok_rows(t)
                    if t >= 2:
                        pe.wait_ge(yo_act, t - 1)
                        pe.wait_ge(yo_dve, t - 1)
                    for k in range(KD):
                        mm = pe.transpose(ps[0:n, 2 * (t % 2) + k // 4, (k % 4) * P:(k % 4 + 1) * P],
                                          Y[:, k, t * P:t * P + n], ident)
                    mm.then_inc(y_turned, 1)

            @block.scalar
            def _(act):
                with act.Fori(0, JT) as j:
                    act.activation(Ghi[:, bass.ds(j, 1), :].rearrange("p o n -> p (o n)"),
                                   OG[:, bass.ds(j, 1), :].rearrange("p o n -> p (o n)"), ACT.Copy
                                   ).then_inc(ohi_ready, 1)
                out_proj_act(act, outp[1], norms[2], U_AOUT, False)
                norm_std(act, norms[2])
                for t in range(NXT):
                    n = tok_rows(t)
                    act.wait_ge(y_turned, t + 1)
                    if t >= 2:
                        act.wait_ge(y_out[t % 2], 16 * (t // 2))
                    act.activation(yo[t % 2][0:n, 0:512], ps[0:n, 2 * (t % 2), :], ACT.Copy).then_inc(yo_act, 1)

            @block.vector
            def _(dve):
                out_proj_dve(dve, outp[1], U_AOUT)
                norm_rstd(dve, norms[2])
                dve.wait_ge(Norm.rstd_ready, norms[2].o + 1)
                for k in range(KD):
                    dve.scalar_tensor_tensor(out=Y[:, k, :], in0=Y[:, k, :],
                                             scalar=cols[:, C_FNG + k:C_FNG + k + 1],
                                             in1=std[:, :], op0=ALU.mult, op1=ALU.mult).then_inc(yn_ready, 1)
                for t in range(NXT):
                    n = tok_rows(t)
                    dve.wait_ge(y_turned, t + 1)
                    if t >= 2:
                        dve.wait_ge(y_out[t % 2], 16 * (t // 2))
                    dve.tensor_copy(yo[t % 2][0:n, 512:1024], ps[0:n, 2 * (t % 2) + 1, :]).then_inc(yo_dve, 1)

            @block.gpsimd
            def _(pool):
                with pool.Fori(0, JT) as j:
                    pool.wait_ge(ohi_ready, j + 1)
                    pool.tensor_tensor(Glo[:, bass.ds(j, 1), :].rearrange("p o n -> p (o n)"),
                                       OG[:, bass.ds(j, 1), :].rearrange("p o n -> p (o n)"),
                                       Ghi[:, bass.ds(j, 1), :].rearrange("p o n -> p (o n)").bitcast(F32),
                                       ALU.subtract).then_inc(olo_ready, 1)
                out_proj_pool(pool, norms[2], U_AOUT, False)


_INS = ["x_prompt", "x_sample", "state_conv", "cache_k", "cache_v", "page_table", "norm_g", "final_norm_g",
        "conv_w_in", "conv_dw_w", "conv_dw_b", "conv_ln_g", "conv_ln_b", "conv_w_out",
        "attn_w_in", "attn_lambda_q1", "attn_lambda_k1", "attn_lambda_q2", "attn_lambda_k2",
        "attn_subln_g", "attn_w_out"]
_OUTS = [("y_prompt", (1, NP_TOK, D)), ("y_sample", (NB, NT, D)),
         ("conv_state_prompt", (1, 1, PAD, E)), ("conv_state_sample", (1, NB, PAD, E)),
         ("k_rows_prompt", (1, 1, NP_TOK, NG, 2 * HD)), ("v_rows_prompt", (1, 1, NP_TOK, NG, VD)),
         ("k_rows_sample", (1, NB, NT, NG, 2 * HD)), ("v_rows_sample", (1, NB, NT, NG, VD))]


def kernel(**inputs):
    import concourse.bacc as _bacc
    from concourse.bass_utils import run_bass_kernel_spmd as _run

    nc = _bacc.Bacc("TRN2", target_bir_lowering=False, num_devices=1, dynamic_dma_scratch_size=1024)
    arrays = {name: np.ascontiguousarray(inputs[name]) for name in _INS}
    arrays.update(host_constants())
    a = {name: nc.dram_tensor(name, x.shape, mybir.dt.from_np(x.dtype), kind="ExternalInput").ap()
         for name, x in arrays.items()}
    o = {name: nc.dram_tensor(name, shape, F32, kind="ExternalOutput").ap() for name, shape in _OUTS}
    build(nc, a, o)
    r = _run(nc, [arrays], core_ids=[0])
    return tuple(r.results[0][name] for name, _ in _OUTS)
```

```python
from contextlib import ExitStack
import math

import numpy as np

import concourse.bass as bass
from concourse import mybir

F32 = mybir.dt.float32
F32R = mybir.dt.float32r
I32 = mybir.dt.int32
ALU = mybir.AluOpType
ACT = mybir.ActivationFunctionType
AX = mybir.AxisListType

P = 128
D = 1024
KD = D // P
NP_TOK, NB, NT = 1024, 8, 4
NS_TOK = NB * NT
T = NP_TOK + NS_TOK
CH = T // 3
E = 2048
JT = E // P
TAPS = 31
PAD = TAPS - 1
WIN = PAD + NT
NG, GH = 4, 4
HD, VD = 64, 128
ROT = HD // 4
THETA = 500000.0
PAST, PAGE = 1024, 128
PAGES = PAST // PAGE
QT = NP_TOK // P
SCALE = HD ** -0.5
RMS_EPS, LN_EPS = 1e-6, 1e-5
LAM_INIT = 0.8 - 0.6 * math.exp(-0.3)
MASKED = -float(2 ** 100)

C_NG1, C_NG2, C_FNG, C_DWB, C_LNG, C_LNB, C_SUB, N_COLS = 0, 8, 16, 24, 40, 56, 72, 73

U_CONV, U_COUT, U_ATT, U_AOUT, N_UNITS = 0, 48, 64, 104, 120

POOL_TAPS = 10
POOL_FIRST = 4


class Count:

    def __init__(self, sem):
        self.sem, self.n, self.off = sem, 0, 0

    def up(self):
        self.n += 1
        return 1

    def now(self, back=0):
        return self.off + (self.n - back)

    def enter(self, i, first, per):
        self.start, self.per, self.off = self.n, per, (i - first) * per

    def leave(self, trips):
        assert self.n - self.start == self.per, (self.n - self.start, self.per)
        self.n, self.off = self.n + self.per * (trips - 1), 0


def host_constants():
    pos = np.concatenate([np.arange(NP_TOK), np.tile(PAST + np.arange(NT), NB)]).astype(np.float32)
    half = ROT // 2
    inv = np.float32(THETA) ** (-np.arange(half, dtype=np.float32) / np.float32(half))
    ang = pos[None, :] * inv[:, None].astype(np.float32)
    cos, sin = np.ones((P, T), np.float32), np.zeros((P, T), np.float32)
    swap = np.zeros((P, P), np.float32)
    for c in range(2):
        for i in range(half):
            a, b = HD * c + i, HD * c + half + i
            cos[a] = cos[b] = np.cos(ang[i])
            sin[a] = sin[b] = np.sin(ang[i])
            swap[b, a], swap[a, b] = -1.0, 1.0
    t = np.arange(P)
    causal = np.where(t[None, :] <= t[:, None], 0.0, MASKED).astype(np.float32)
    g, c, h, s = np.meshgrid(np.arange(NG), np.arange(2), np.arange(GH), np.arange(NT), indexing="ij")
    g, c, h, s = (v.reshape(-1) for v in (g, c, h, s))
    newmask = np.where(np.arange(NT)[None, :] <= s[:, None], 0.0, MASKED).astype(np.float32)
    rows = np.zeros((P, NG * GH * NT), np.float32)
    rows[np.arange(P), (g * GH + h) * NT + s] = 1.0
    cc = np.stack([1.0 - c, c], 1).astype(np.float32)
    small = np.concatenate([np.eye(P, dtype=np.float32), swap, causal, rows, newmask, cc], 1)
    return {"c_small": small, "c_cos": cos, "c_sin": sin}


N_SMALL = 3 * P + NG * GH * NT + NT + 2


def build(nc, a, o):
    ctx = ExitStack()
    with ctx:
        def sem(name):

            return ctx.enter_context(nc.semaphore(name))

        base = (nc.sbuf_base + 31) // 32 * 32
        cursor = [base]

        def place(name, shape, dt=F32, at=None):
            size = (int(np.prod(shape[1:])) * 4 + 31) // 32 * 32
            if at is None:
                at = cursor
            t = nc.alloc_sbuf_tensor_at(name, list(shape), dt, offset=at[0])
            at[0] += size
            return t

        small = place("small", [P, N_SMALL])
        ident = small[:, 0:P]
        swap = small[:, P:2 * P]
        causal = small[:, 2 * P:3 * P]
        rowsel = small[:, 3 * P:3 * P + 64]
        newmask = small[:, 3 * P + 64:3 * P + 68]
        cc = small[:, 3 * P + 68:3 * P + 70]
        ones = place("ones", [P, P])
        cols = place("cols", [P, N_COLS])
        dww = place("dww", [P, JT, TAPS])
        misc = place("misc", [P, 8])
        ptab = place("ptab", [1, NB * PAGES], I32)
        eps_rms, eps_ln, neglam, subg, rowcoef = (misc[:, i:i + 1] for i in range(5))
        raw_at = [cursor[0], cursor[0] + 4 * KD * P]
        raw = [place(f"w_raw{s}", [P, KD, P]) for s in range(2)]
        whi = [place(f"w_hi{s}", [P, KD, P], F32R) for s in range(2)]
        wlo = [place(f"w_lo{s}", [P, KD, P], F32R) for s in range(2)]
        SLOT = 4 * T
        slots0 = cursor[0]
        assert slots0 + 46 * SLOT <= 229344, slots0

        def slot(n):
            return [slots0 + n * SLOT]

        ps = nc.alloc_psum_tensor("ps", [P, 8, 512], F32)

        def pset(s):
            return ps[:, 3 * s:3 * s + 3, 0:CH]

        def chunks(ap):
            return ap.rearrange("p (c n) -> p c n", c=3)

        Hhi = place("Hhi", [P, KD, T], F32R, slot(0))
        Hlo = place("Hlo", [P, KD, T], F32R, slot(8))
        Ghi = place("Ghi", [P, JT, T], F32R, slot(0))
        C = place("C", [P, JT, T], F32, slot(16))
        Glo = place("Glo", [P, JT, T], F32R, slot(16))
        Y = place("Y", [P, KD, T], F32, slot(32))
        xres = [place(f"xres{s}", [P, T], F32, slot(40 + s)) for s in range(2)]
        ssum = place("ssum", [P, T], F32, slot(42))
        sq = place("sq", [P, T], F32, slot(43))
        csum = place("csum", [P, T], F32, slot(45))

        def scratch(name, shape):
            return nc.dram_tensor(name, shape, F32, kind="Internal").ap()
        res_d = [scratch("res0", [P, KD, T]), scratch("res1", [P, KD, T])]
        gate_d = [scratch("gate0", [JT, P, T]), scratch("gate1", [JT, P, T])]
        rstd_d = scratch("rstd_heads", [JT, NP_TOK])
        q_d = scratch("q_rot", [JT, P, T])
        k_d = scratch("k_rot", [NG, P, T])

        raw_in = [sem("raw_in0"), sem("raw_in1")]
        w_hi, w_lo, w_used = sem("w_hi"), sem("w_lo"), sem("w_used")
        act_step, dve_step = Count(sem("act_step")), Count(sem("dve_step"))

        w_cin = a["conv_w_in"][0].rearrange("(k p) e -> p k e", p=P)
        w_cout = a["conv_w_out"][0].rearrange("(f k p) e -> f p k e", p=P, f=2)
        w_ain = a["attn_w_in"][0].rearrange("(k p) e -> p k e", p=P)
        w_aout = a["attn_w_out"][0].rearrange("(f k p) e -> f p k e", p=P, f=2)

        def conv_src(col, kind):
            return w_cin[:, :, bass.ds(col + (E, 0, 2 * E)[kind], P)]

        def out_src(w, pair, q):
            return w[q // 2][:, :, bass.ds((pair * 2 + q % 2) * P, P)]

        def att_src(u):
            return w_ain[:, :, bass.ds(u * P, P)]

        def load_unit(sp, n, s, src):
            sp.wait_ge(w_lo, n - 1)
            sp.dma_start(raw[s][:, :, :], src).then_inc(raw_in[s], 16)

        def make_hi(act, n, s, turn, reused=True):
            act.wait_ge(raw_in[s], turn * 16)
            if reused:
                act.wait_ge(w_used, n - 1)
            act.activation(whi[s][:, :, :], raw[s][:, :, :], ACT.Copy).then_inc(w_hi, 1)

        def make_lo(pool, n, s):
            pool.wait_ge(w_hi, n + 1)
            pool.tensor_tensor(wlo[s][:, :, :], raw[s][:, :, :], whi[s][:, :, :].bitcast(F32),
                               ALU.subtract).then_inc(w_lo, 1)

        def unit(pe, n, s, dst, rhs_hi, rhs_lo, start=True, stop=True, before_chunk=None):
            pe.wait_ge(w_lo, n + 1)
            for c in range(3):
                if before_chunk:
                    before_chunk(c)
                for k in range(KD):
                    for w, r in ((whi[s], rhs_hi), (whi[s], rhs_lo), (wlo[s], rhs_hi)):
                        mm = pe.matmul(ps[:, 3 * dst + c, 0:CH], w[:, k, :], r(k)[:, c * CH:(c + 1) * CH],
                                       start=start and k == 0 and w is whi[s] and r is rhs_hi,
                                       stop=stop and k == KD - 1 and w is wlo[s])
            mm.then_inc(w_used, 1)

        def h_hi(k):
            return Hhi[:, k, :]

        def h_lo(k):
            return Hlo[:, k, :]

        NXT = QT + 1

        def column_sums(pe, src, bank, start=True, stop=True):
            for t in range(NXT):
                c0 = min(t * P, T - P)
                mm = pe.matmul(ps[:, bank, t:t + 1], src[:, c0:c0 + P], ones[:, 0:1],
                               start=start and t == 0,
                               stop=stop and t == NXT - 1)
            return mm

        def spread(pe, cols9, bank, p0=P - NS_TOK):
            for t in range(NXT):
                n = tok_rows(t)
                a0 = p0 if n < P else 0
                k = P if a0 == P - n else n
                mm = pe.matmul(ps[:, bank + t // 4, (t % 4) * P:(t % 4) * P + n],
                               cols9[0:k, t:t + 1].to_broadcast([k, P]), ident[0:k, a0:a0 + n],
                               start=True, stop=True)
            return mm

        def spread_out(bank):
            return ps[:, bank:bank + 3, :].rearrange("p b n -> p (b n)")[:, 0:T]

        def tok_rows(t):
            return min(P, T - t * P)

        class Norm:
            sq_ready, sum_ready, total, std_ready = sem("n_sq"), sem("n_sum"), sem("n_total"), sem("n_std")
            rstd_ready, spread_done, h_ready, hi_ready = (sem(x) for x in ("n_rstd", "n_spread", "n_h", "n_hi"))
            lo_pool, lo_dve = sem("n_lo_pool"), sem("n_lo_dve")
            BY_DVE = (0, 3, 6)
            GATED_BY_DVE = (11, 13, 15)

            def __init__(self, turn):
                self.o = turn
                self.t, self.sums = KD * turn, (KD - 1) * (turn - 1)
                self.pool, self.dve = (KD - len(self.BY_DVE)) * turn, len(self.BY_DVE) * turn
                if turn >= 1:
                    self.dve += len(self.GATED_BY_DVE)

            def lo(self, k):
                before = sum(x < k for x in self.BY_DVE)
                if k in self.BY_DVE:
                    return self.lo_dve, self.dve + before + 1
                return self.lo_pool, self.pool + k - before + 1

        norms = [Norm(i) for i in range(3)]
        nh = [place(f"nh{s}", [P, T], F32, slot(40 + s)) for s in range(4)]
        ncol = place("norm_cols", [P, NXT], F32, slot(44))

        def norm_add(pool, nm, k, first):
            pool.wait_ge(nm.sq_ready, nm.t - KD + k + 1)
            if first:
                pool.tensor_scalar(ssum[:, :], sq[:, :], 1.0, 1.0, ALU.mult, ALU.mult).then_inc(nm.sum_ready, 1)
            else:
                pool.wait_ge(nm.sum_ready, nm.sums + k)
                pool.tensor_tensor(ssum[:, :], ssum[:, :], sq[:, :], ALU.add).then_inc(nm.sum_ready, 1)

        def norm_total(pe, op, nm):
            for d in range(2):
                pe.wait_ge(op.y[d], op.b + KD // 2)
            pe.wait_ge(nm.sum_ready, nm.sums + KD - 1)
            column_sums(pe, ssum, 0, stop=False)
            pe.wait_ge(nm.sq_ready, nm.t)
            column_sums(pe, sq, 0, start=False).then_inc(nm.total, 1)

        def norm_std(act, nm):
            act.wait_ge(nm.total, nm.o)
            act.activation(ncol[:, :], ps[:, 0, 0:NXT], ACT.Sqrt, scale=1.0 / D, bias=eps_rms).then_inc(nm.std_ready, 1)

        def norm_rstd(dve, nm):
            dve.wait_ge(nm.std_ready, nm.o + 1)
            dve.reciprocal(ncol[:, :], ncol[:, :]).then_inc(nm.rstd_ready, 1)

        def norm_spread(pe, nm, **where):
            pe.wait_ge(nm.rstd_ready, nm.o + 1)
            spread(pe, ncol, 3, **where).then_inc(nm.spread_done, 1)

        def lo_part(engine, nm, k):
            engine.wait_ge(nm.hi_ready, nm.t + k + 1)
            engine.tensor_tensor(Hlo[:, k, :], nh[k % 4][:, :], Hhi[:, k, :].bitcast(F32),
                                 ALU.subtract).then_inc(nm.lo(k)[0], 1)

        def norm_dve(dve, nm, gcol):
            for k in range(KD):
                if k >= 4:
                    dve.wait_ge(*nm.lo(k - 4))
                dve.wait_ge(nm.spread_done, nm.o + 1)
                dve.scalar_tensor_tensor(out=nh[k % 4][:, :], in0=Y[:, k, :], scalar=cols[:, gcol + k:gcol + k + 1],
                                         in1=spread_out(3), op0=ALU.mult, op1=ALU.mult).then_inc(nm.h_ready, 1)
                if k - 1 in nm.BY_DVE:
                    lo_part(dve, nm, k - 1)
            if KD - 1 in nm.BY_DVE:
                lo_part(dve, nm, KD - 1)

        def norm_act(act, nm):
            for k in range(KD):
                act.wait_ge(nm.h_ready, nm.t + k + 1)
                act.activation(Hhi[:, k, :], nh[k % 4][:, :], ACT.Copy).then_inc(nm.hi_ready, 1)

        def norm_pool(pool, nm):
            for k in range(KD):
                if k not in nm.BY_DVE:
                    lo_part(pool, nm, k)

        def unit_by_tile(pe, n, s, dst, nm):
            pe.wait_ge(w_lo, n + 1)
            for k in range(KD):
                pe.wait_ge(*nm.lo(k))
                for w, r in ((whi[s], Hhi), (whi[s], Hlo), (wlo[s], Hhi)):
                    for c in range(3):
                        mm = pe.matmul(ps[:, 3 * dst + c, 0:CH], w[:, k, :], r[:, k, c * CH:(c + 1) * CH],
                                       start=k == 0 and w is whi[s] and r is Hhi, stop=k == KD - 1 and w is wlo[s])
            mm.then_inc(w_used, 1)

        xin = place("xin", [P, NXT, D], F32, slot(16))
        vecs = place("vecs", [N_COLS, P], F32, slot(26))
        dwin = place("dwin", [TAPS, E], F32, slot(27))
        lamv = place("lamv", [1, 4, HD], F32, slot(29))
        lamt = place("lamt", [1, 2, HD], F32, slot(30))
        lams = place("lams", [1, 8], F32, slot(31))
        x_in = [sem(f"x_in{t}") for t in range(NXT)]
        pt_in = sem("pt_in")
        small_in, vec_in, dw_in, lam_in = sem("small_in"), sem("vec_in"), sem("dw_in"), sem("lam_in")
        setup = sem("setup")
        x_turned = sem("x_turned")
        xe_act, xe_dve = sem("x_evac_act"), sem("x_evac_dve")
        cols_turned, cols_ready, dw_turned, dw_ready = sem("cols_turned"), sem("cols_ready"), sem("dw_turned"), sem("dw_ready")
        lam_step = sem("lam_step")
        res_out = [sem("res_out0"), sem("res_out1")]

        with nc.Block() as block:
            @block.sync
            def _(sp):
                sp.dma_start(small[:, :], a["c_small"]).then_inc(small_in, 16)
                for t in range(QT):
                    sp.dma_start(xin[:, t, :], a["x_prompt"][0, t * P:(t + 1) * P, :]).then_inc(x_in[t], 16)
                sp.dma_start(xin[0:NS_TOK, QT, :], a["x_sample"].rearrange("b t d -> (b t) d")).then_inc(x_in[QT], 16)
                for s, kind in ((0, 0), (1, 1)):
                    sp.dma_start(raw[s][:, :, :], conv_src(0, kind)).then_inc(raw_in[s], 16)
                for r, name, n in ((C_NG1, "norm_g", 16), (C_FNG, "final_norm_g", 8), (C_DWB, "conv_dw_b", 16),
                                   (C_LNG, "conv_ln_g", 16), (C_LNB, "conv_ln_b", 16), (C_SUB, "attn_subln_g", 1)):
                    v = a[name] if name == "final_norm_g" else a[name].rearrange("l d -> (l d)")
                    sp.dma_start(vecs[r:r + n, :], v.rearrange("(k p) -> k p", p=P)).then_inc(vec_in, 16)
                sp.dma_start(dwin[:, :], a["conv_dw_w"][0]).then_inc(dw_in, 16)
                for i, name in enumerate(("attn_lambda_q1", "attn_lambda_k1", "attn_lambda_q2", "attn_lambda_k2")):
                    sp.dma_start(lamv[:, i, :], a[name]).then_inc(lam_in, 16)
                sp.dma_start(ptab[:, :], a["page_table"].rearrange("(o b) p -> o (b p)", o=1)).then_inc(pt_in, 16)
                sp.wait_ge(xe_act, NXT)
                sp.wait_ge(xe_dve, NXT)
                sp.dma_start(res_d[0], Y[:, :, :]).then_inc(res_out[0], 16)
                sp.wait_ge(res_out[0], 16)

            @block.tensor
            def _(pe):
                pe.wait_ge(small_in, 16)
                for t in range(NXT):
                    n = tok_rows(t)
                    pe.wait_ge(x_in[t], 16)
                    if t >= 3:
                        pe.wait_ge(xe_act, t - 2)
                        pe.wait_ge(xe_dve, t - 2)
                    for k in range(KD):
                        mm = pe.transpose(ps[:, 2 * (t % 3) + k // 4, (k % 4) * P:(k % 4) * P + n],
                                          xin[0:n, t, k * P:(k + 1) * P], ident[0:n, 0:n])
                    mm.then_inc(x_turned, 1)
                pe.wait_ge(vec_in, 96)
                pe.transpose(ps[:, 6, 0:N_COLS], vecs[:, :], ident[0:N_COLS, 0:N_COLS]).then_inc(cols_turned, 1)
                pe.wait_ge(dw_in, 16)
                for j in range(JT):
                    mm = pe.transpose(ps[:, 7, TAPS * j:TAPS * (j + 1)], dwin[:, j * P:(j + 1) * P], ident[0:TAPS, 0:TAPS])
                mm.then_inc(dw_turned, 1)
                pe.wait_ge(setup, 2)
                pe.wait_ge(lam_step, 4)
                pe.wait_ge(cols_ready, 1)
                pe.matmul(ps[:, 6, 0:2], ones[0:1, :], lams[0:1, 4:6], start=True, stop=True).then_inc(lam_step, 1)
                pe.wait_ge(xe_act, NXT)
                pe.wait_ge(xe_dve, NXT)
                norm_spread(pe, norms[0], p0=0)

            @block.scalar
            def _(act):
                for t in range(NXT):
                    n = tok_rows(t)
                    act.wait_ge(x_turned, t + 1)
                    act.activation(Y[:, 0:4, t * P:t * P + n],
                                   ps[:, 2 * (t % 3), :].rearrange("p (k n) -> p k n", k=4)[:, :, 0:n],
                                   ACT.Copy).then_inc(xe_act, 1)
                    if t >= 1:
                        act.wait_ge(act_step.sem, act_step.now())
                    act.activation(sq[0:n, 0:D], xin[0:n, t, :], ACT.Square, accum_out=ncol[0:n, t:t + 1]
                                   ).then_inc(act_step.sem, act_step.up())
                act.wait_ge(cols_turned, 1)
                act.activation(cols[:, :], ps[:, 6, 0:N_COLS], ACT.Copy).then_inc(cols_ready, 1)
                act.wait_ge(dw_turned, 1)
                act.activation(dww[:, :, :], ps[:, 7, 0:JT * TAPS].rearrange("p (j k) -> p j k", j=JT),
                               ACT.Copy).then_inc(dw_ready, 1)
                act.wait_ge(lam_step, 2)
                act.activation(lams[0:1, 2:4], lams[0:1, 0:2], ACT.Exp).then_inc(lam_step, 1)
                act.wait_ge(setup, 3)
                act.wait_ge(act_step.sem, act_step.now())
                act.activation(ncol[:, 0:QT], ncol[:, 0:QT], ACT.Sqrt, scale=1.0 / D, bias=eps_rms)
                act.activation(ncol[0:NS_TOK, QT:NXT], ncol[0:NS_TOK, QT:NXT], ACT.Sqrt, scale=1.0 / D,
                               bias=eps_rms[0:NS_TOK]).then_inc(Norm.std_ready, 1)
                for n in range(2):
                    make_hi(act, n, n % 2, 1, reused=False)

            @block.vector
            def _(dve):
                dve.memset(ones[:, :], 1.0).then_inc(setup, 1)
                dve.memset(eps_rms, RMS_EPS).then_inc(setup, 1)
                dve.memset(eps_ln, LN_EPS).then_inc(setup, 1)
                for t in range(NXT):
                    n = tok_rows(t)
                    dve.wait_ge(x_turned, t + 1)
                    dve.tensor_copy(Y[:, 4:8, t * P:t * P + n],
                                    ps[:, 2 * (t % 3) + 1, :].rearrange("p (k n) -> p k n", k=4)[:, :, 0:n]
                                    ).then_inc(xe_dve, 1)
                dve.wait_ge(lam_in, 64)
                for i in range(2):
                    dve.tensor_tensor(lamt[:, i, :], lamv[:, 2 * i, :], lamv[:, 2 * i + 1, :], ALU.mult
                                      ).then_inc(dve_step.sem, dve_step.up())
                dve.wait_ge(dve_step.sem, dve_step.now())
                for i in range(2):
                    dve.tensor_reduce(lams[0:1, i:i + 1], lamt[:, i, :], AX.X, ALU.add).then_inc(lam_step, 1)
                dve.wait_ge(lam_step, 3)
                dve.tensor_tensor(lams[0:1, 6:7], lams[0:1, 3:4], lams[0:1, 2:3], ALU.subtract
                                  ).then_inc(dve_step.sem, dve_step.up())
                dve.wait_ge(dve_step.sem, dve_step.now())
                for i in range(2):
                    dve.tensor_scalar(lams[0:1, 4 + i:5 + i], lams[0:1, 6:7], -LAM_INIT, None, ALU.add
                                      ).then_inc(dve_step.sem, dve_step.up())
                dve.wait_ge(dve_step.sem, dve_step.now())
                dve.sem_inc(lam_step, 1)
                dve.wait_ge(lam_step, 5)
                dve.tensor_copy(neglam, ps[:, 6, 0:1]).then_inc(dve_step.sem, dve_step.up())
                dve.wait_ge(cols_ready, 1)
                dve.tensor_scalar(subg, cols[:, C_SUB:C_SUB + 1], 1.0 - LAM_INIT, None, ALU.mult
                                  ).then_inc(dve_step.sem, dve_step.up())
                dve.wait_ge(small_in, 16)
                dve.wait_ge(dve_step.sem, dve_step.now())
                dve.scalar_tensor_tensor(out=rowcoef, in0=cc[:, 1:2], scalar=neglam, in1=cc[:, 0:1],
                                         op0=ALU.mult, op1=ALU.add).then_inc(dve_step.sem, dve_step.up())
                dve.wait_ge(Norm.std_ready, 1)
                dve.reciprocal(ncol[:, 0:QT], ncol[:, 0:QT])
                dve.reciprocal(ncol[0:NS_TOK, QT:NXT], ncol[0:NS_TOK, QT:NXT]).then_inc(Norm.rstd_ready, 1)

            @block.gpsimd
            def _(pool):
                for n in range(2):
                    make_lo(pool, n, n % 2)

        at = slot(32)
        U = [place(f"U{s}", [P, NP_TOK + P], F32, at) for s in range(2)]
        sigb = place("sigb", [P, T], F32, at)
        odd = place("odd", [P, NP_TOK], F32, at)
        pacc = place("pool_acc", [P, NP_TOK], F32, at)
        prod = [place(f"prod{s}", [P, NP_TOK], F32, at) for s in range(2)]
        sg = [place(f"sg{s}", [P, T], F32, at) for s in range(2)]
        smp = place("smp", [P, NB, NT, TAPS], F32, slot(46))
        win = place("win", [P, NB, WIN], F32, at)
        stin = [place(f"st_in{s}", [P - 8, 2, P], F32, [slot(31)[0] + s * 8 * P]) for s in range(2)]
        stout = place("st_out", [PAD + NS_TOK, E], F32, at)
        assert at[0] <= slot(45)[0]
        SR = NB * PAD // 2
        st_src = a["state_conv"][0].rearrange("b r c -> (b r) c").rearrange("(h p) c -> p h c", p=SR)

        sig_done, u_done, sg_done = sem("sig_done"), sem("u_done"), sem("sg_done")
        st_loaded = [sem("st_loaded0"), sem("st_loaded1")]
        st_turned, win_state, smp_read = sem("st_turned"), sem("win_state"), sem("smp_read")
        prod_ready, prod_free, merged = sem("prod_ready"), sem("prod_free"), sem("merged")
        u_turned, stout_ready = sem("u_turned"), sem("stout_ready")
        sg_out = [sem("sg_out0"), sem("sg_out1")]
        st_out = sem("st_out")
        keep_out = sem("keep_out")
        DVE_TAPS = list(range(POOL_TAPS, TAPS))
        win_ap = win[:, :, :]
        part_step = win_ap.ap[0][0]
        windows = bass.AP(win_ap.tensor, win_ap.offset, [[part_step, P], [WIN, NB], [1, NT], [1, TAPS]])

        with nc.Block() as block:
            @block.sync
            def _(sp):
                for s in range(2):
                    sp.dma_start(stin[s][0:SR, :, :], st_src[:, :, s * P:(s + 1) * P]).then_inc(st_loaded[s], 16)
                sp.dma_start(o["conv_state_sample"][0, :, 0:PAD - NT, :], a["state_conv"][0, :, NT:PAD, :]
                             ).then_inc(keep_out, 16)

                def spill(i, s):
                    sp.wait_ge(sg_done, 2 * i + s + 1)
                    sp.dma_start(gate_d[0][2 * i + s], sg[s][:, :]).then_inc(sg_out[s], 16)

                def body(i, last=False):
                    col = i * 2 * P if last else sp.snap(i * 2 * P)
                    for m in range(2, 8):
                        if last and m >= 6:
                            src = out_src(w_cout, 0, m - 6)
                        else:
                            src = conv_src(col + m // 3 * P, m % 3)
                        load_unit(sp, 6 * i + m, m % 2, src)
                        if m in (3, 7) and not last:
                            s = m // 4
                            sp.wait_ge(st_turned, 2 * i + s + 1)
                            sp.dma_start(stin[s][0:SR, :, :], st_src[:, :, bass.ds((2 * i + 2 + s) * P, P)]
                                         ).then_inc(st_loaded[s], 16)
                    spill(i, 0)
                    spill(i, 1)

                with sp.Fori(0, JT // 2 - 1) as i:
                    body(i)
                body(JT // 2 - 1, last=True)
                sp.wait_ge(stout_ready, JT)
                sp.dma_start(o["conv_state_prompt"][0, 0], stout[0:PAD, :]).then_inc(st_out, 16)
                for b in range(NB):
                    sp.dma_start(o["conv_state_sample"][0, b, PAD - NT:PAD, :],
                                 stout[PAD + NT * b:PAD + NT * (b + 1), :]).then_inc(st_out, 16)
                for s in range(2):
                    sp.wait_ge(sg_out[s], 16 * JT // 2)
                sp.wait_ge(st_out, 16 * (NB + 1))
                sp.wait_ge(keep_out, 16)

            @block.tensor
            def _(pe):
                with pe.Fori(0, JT // 2) as i:
                    for s in range(2):
                        j = 2 * i + s
                        pe.wait_ge(st_loaded[s], 16 * (i + 1))
                        pe.wait_ge(win_state, j)
                        for h in range(2):
                            mm = pe.transpose(ps[:, 6, h * SR:(h + 1) * SR], stin[s][0:SR, h, :], ident[0:SR, 0:SR])
                        mm.then_inc(st_turned, 1)
                        n, e = 6 * i + 3 * s, s
                        pe.wait_ge(u_done, j)
                        unit_by_tile(pe, n, e, e, norms[0])
                        pe.wait_ge(sg_done, j)
                        pe.wait_ge(Norm.h_ready, KD)
                        unit(pe, n + 1, 1 - e, 1 - e, h_hi, h_lo)
                        pe.wait_ge(sig_done, j + 1)
                        unit(pe, n + 2, e, e, h_hi, h_lo)
                        pe.wait_ge(u_done, j + 1)
                        pe.wait_ge(stout_ready, j)
                        pe.transpose(ps[:, 7, 0:P], U[s][:, NP_TOK:NP_TOK + P], ident).then_inc(u_turned, 1)

            @block.scalar
            def _(act):
                norm_act(act, norms[0])
                with act.Fori(0, JT // 2) as i:
                    for s in range(2):
                        j, n, e = 2 * i + s, 6 * i + 3 * s, s

                        def products(lo, hi):
                            for q in range(lo, hi):
                                r = s * POOL_TAPS + q
                                act.wait_ge(prod_free, i * 2 * POOL_TAPS + r + 1)
                                act.activation(prod[r % 2][:, :], U[s][:, q:q + NP_TOK], ACT.Copy,
                                               scale=dww[:, bass.ds(j, 1), q]).then_inc(prod_ready, 1)

                        make_hi(act, n + 2, e, 3 * i + (3 * s + 2) // 2 + 1)
                        act.wait_ge(w_used, n + 1)
                        act.wait_ge(u_done, j)
                        act.activation(chunks(sigb[:, :]), pset(e), ACT.Sigmoid).then_inc(sig_done, 1)
                        act.wait_ge(st_turned, j + 1)
                        act.wait_ge(smp_read, j)
                        act.activation(win[:, :, 0:PAD], ps[:, 6, 0:NB * PAD].rearrange("p (b r) -> p b r", b=NB),
                                       ACT.Copy).then_inc(win_state, 1)
                        make_hi(act, n + 3, 1 - e, 3 * i + (3 * s + 3) // 2 + 1)
                        act.wait_ge(u_done, j + 1)
                        products(0, POOL_FIRST)
                        make_hi(act, n + 4, e, 3 * i + (3 * s + 4) // 2 + 1)
                        act.wait_ge(w_used, n + 3)
                        act.wait_ge(sg_out[s], 16 * i)
                        act.activation(chunks(sg[s][:, :]), pset(e), ACT.Silu).then_inc(sg_done, 1)
                        products(POOL_FIRST, POOL_TAPS)

            @block.gpsimd
            def _(pool):
                norm_pool(pool, norms[0])
                pool.sem_inc(prod_free, 2)
                with pool.Fori(0, JT // 2) as i:
                    for s in range(2):
                        j, n, e = 2 * i + s, 6 * i + 3 * s, s

                        def adds(lo, hi):
                            for q in range(max(lo, 1), hi):
                                r = i * 2 * POOL_TAPS + s * POOL_TAPS + q
                                pool.wait_ge(prod_ready, r + 1)
                                if q == 1:
                                    pool.wait_ge(merged, j)
                                    pool.tensor_tensor(pacc[:, :], prod[0][:, :], prod[1][:, :], ALU.add
                                                       ).then_inc(prod_free, 2)
                                else:
                                    pool.wait_ge(prod_free, r + 2)
                                    pool.tensor_tensor(pacc[:, :], pacc[:, :], prod[q % 2][:, :], ALU.add
                                                       ).then_inc(prod_free, 1)

                        make_lo(pool, n + 2, e)
                        make_lo(pool, n + 3, 1 - e)
                        adds(0, POOL_FIRST)
                        make_lo(pool, n + 4, e)
                        adds(POOL_FIRST, POOL_TAPS)

            @block.vector
            def _(dve):
                norm_dve(dve, norms[0], C_NG1)
                for k in range(KD - 4, KD):
                    dve.wait_ge(*norms[0].lo(k))
                for s in range(2):
                    dve.memset(U[s][:, 0:PAD], 0.0).then_inc(dve_step.sem, dve_step.up())
                    dve.memset(U[s][:, PAD + T:NP_TOK + P], 0.0).then_inc(dve_step.sem, dve_step.up())
                dve.memset(csum[:, :], 0.0).then_inc(dve_step.sem, dve_step.up())
                per_tile = 3 + len(DVE_TAPS) + 2
                with dve.Fori(0, JT // 2) as i:
                    dve_step.enter(i, 0, 2 * per_tile)
                    for s in range(2):
                        j, n, e = 2 * i + s, 6 * i + 3 * s, s
                        c_p = C[:, bass.ds(j, 1), 0:NP_TOK].rearrange("p o n -> p (o n)")
                        c_s = C[:, bass.ds(j, 1), NP_TOK:T].rearrange("p o n -> p (o n)")
                        c_all = C[:, bass.ds(j, 1), :].rearrange("p o n -> p (o n)")
                        dve.wait_ge(w_used, n + 2)
                        dve.wait_ge(sig_done, j + 1)
                        dve.tensor_tensor(chunks(U[s][:, PAD:PAD + T]), pset(1 - e), chunks(sigb[:, :]),
                                          ALU.mult).then_inc(u_done, 1)
                        dve.wait_ge(u_done, j + 1)
                        dve.tensor_copy(win[:, :, PAD:WIN], U[s][:, PAD + NP_TOK:PAD + T].rearrange(
                            "p (b t) -> p b t", b=NB)).then_inc(dve_step.sem, dve_step.up())
                        dve.wait_ge(win_state, j + 1)
                        dve.wait_ge(dve_step.sem, dve_step.now())
                        w_j = dww[:, bass.ds(j, 1), :].rearrange("p o (x k) -> p (o x) k", x=1)
                        dve.tensor_tensor(smp[:, :, :, :].rearrange("p b t k -> p (b t) k"),
                                          windows.rearrange("p b t k -> p b t k"),
                                          w_j.to_broadcast([P, NS_TOK, TAPS]), ALU.mult).then_inc(smp_read, 1)
                        dve.wait_ge(smp_read, j + 1)
                        dve.tensor_reduce(c_s, smp[:, :, :, :].rearrange("p b t k -> p (b t) k"), AX.X, ALU.add
                                          ).then_inc(dve_step.sem, dve_step.up())
                        dve.wait_ge(dve_step.sem, dve_step.now())
                        bias = cols[:, bass.ds(j + C_DWB, 1)]
                        dve.tensor_scalar(c_s, c_s, bias, None, ALU.add).then_inc(dve_step.sem, dve_step.up())
                        for q, k in enumerate(DVE_TAPS):
                            tgt = odd[:, :] if q % 2 else c_p
                            wk = dww[:, bass.ds(j, 1), k]
                            uk = U[s][:, k:k + NP_TOK]
                            dve.wait_ge(dve_step.sem, dve_step.now(1))
                            if q == 0:
                                dve.tensor_scalar(tgt, uk, wk, bias, ALU.mult, ALU.add
                                                  ).then_inc(dve_step.sem, dve_step.up())
                            elif q == 1:
                                dve.tensor_scalar(tgt, uk, wk, None, ALU.mult
                                                  ).then_inc(dve_step.sem, dve_step.up())
                            else:
                                dve.scalar_tensor_tensor(out=tgt, in0=uk, scalar=wk, in1=tgt, op0=ALU.mult,
                                                         op1=ALU.add).then_inc(dve_step.sem, dve_step.up())
                        dve.wait_ge(u_turned, j + 1)
                        dve.tensor_copy(stout[:, bass.ds(j * P, P)], ps[0:PAD + NS_TOK, 7, 0:P]).then_inc(stout_ready, 1)
                        dve.wait_ge(dve_step.sem, dve_step.now())
                        dve.tensor_tensor(c_p, c_p, odd[:, :], ALU.add).then_inc(dve_step.sem, dve_step.up())
                        dve.wait_ge(dve_step.sem, dve_step.now())
                        dve.wait_ge(prod_free, 2 * i * POOL_TAPS + (s + 1) * POOL_TAPS + 2)
                        dve.tensor_tensor(c_p, c_p, pacc[:, :], ALU.add).then_inc(merged, 1)
                        dve.wait_ge(merged, j + 1)
                        dve.tensor_tensor(csum[:, :], csum[:, :], c_all, ALU.add
                                          ).then_inc(dve_step.sem, dve_step.up())
                    dve_step.leave(JT // 2)

        mean = place("mean", [P, T], F32, slot(32))
        lrstd = place("ln_rstd", [P, T], F32, slot(33))
        tt = [place(f"tt{s}", [P, T], F32, slot(34 + s if s < 4 else 38 + s)) for s in range(8)]
        lcol = place("ln_cols", [P, NXT], F32, slot(46))
        lsq = tt
        sgl = [place(f"sgl{s}", [P, T], F32, slot(38 + s)) for s in range(4)]
        csum_turned, mean_ready, xc_ready, lsq_ready, lsq_used = (sem(x) for x in (
            "csum_total", "mean_ready", "xc_ready", "lsq_ready", "lsq_used"))
        lpair_ready, lrstd_ready = sem("lpair_ready"), sem("lrstd_ready")
        lroot_step = sem("lroot_step")
        z_ready, silu_ready, p_ready, ghi_ready, glo_ready = (sem(x) for x in (
            "z_ready", "silu_ready", "p_ready", "ghi_ready", "glo_ready"))
        sgl_in = [sem(f"sgl_in{s}") for s in range(4)]

        class OutProj:
            res_in = [sem(f"res_in{s}") for s in range(2)]
            y = [sem(f"y_done{s}") for s in range(2)]

            def __init__(self, turn):
                self.b = KD // 2 * turn

        outp = [OutProj(0), OutProj(1)]

        def out_proj_pe(pe, op, n0, ready):
            with pe.Fori(0, KD // 2) as p:
                for q in range(4):
                    d, half = q % 2, q // 2
                    n = n0 + 4 * p + q
                    if half == 0:
                        pe.wait_ge(op.y[d], op.b + p)
                    pe.wait_ge(w_lo, n + 1)
                    for k in range(KD):
                        kk = KD * half + k
                        if d == 0:
                            pe.wait_ge(*ready(kk))
                        for w, r in ((whi, Ghi), (whi, Glo), (wlo, Ghi)):
                            for c in range(3):
                                mm = pe.matmul(ps[:, 3 * d + c, 0:CH], w[d][:, k, :],
                                               r[:, kk, c * CH:(c + 1) * CH],
                                               start=(kk == 0 and w is whi and r is Ghi),
                                               stop=(kk == JT - 1 and w is wlo))
                    mm.then_inc(w_used, 1)

        def out_proj_act(act, op, nm, n0, prepare, made=0):
            def body(p, ahead, made=0):
                for q in range(4):
                    n = n0 + 4 * p + q
                    if q >= made and (q < 2 or ahead):
                        make_hi(act, n + 2, q % 2, (n0 + q + 2) // 2 + 1 + 2 * p)
                    if q >= 2:
                        d = q - 2
                        act.wait_ge(op.y[d], op.b + p + 1)
                        act.wait_ge(nm.sum_ready, nm.sums + 2 * p + d)
                        act.activation(sq[:, :], Y[:, bass.ds(2 * p + d, 1), :].rearrange("p o n -> p (o n)"),
                                       ACT.Square).then_inc(nm.sq_ready, 1)
            body(0, True, made)
            with act.Fori(1, KD // 2 - 1) as p:
                body(p, True)
            body(KD // 2 - 1, prepare)

        def out_proj_pool(pool, nm, n0, prepare, made=0):
            def body(p, first, ahead, last=False, made=0):
                for q in range(4):
                    n = n0 + 4 * p + q
                    if q >= made and (q < 2 or ahead):
                        make_lo(pool, n + 2, q % 2)
                    if q >= 2:
                        k = 2 * p + q - 2
                        if q == 2 or not last:
                            norm_add(pool, nm, k, first and q == 2)
            body(0, True, True, made=made)
            with pool.Fori(1, KD // 2 - 1) as p:
                body(p, False, True)
            body(KD // 2 - 1, False, prepare, True)

        def out_proj_dve(dve, op, n0):
            with dve.Fori(0, KD // 2) as p:
                for d in range(2):
                    dve.wait_ge(w_used, n0 + 4 * p + 3 + d)
                    dve.wait_ge(op.res_in[d], 16 * (op.b + p + 1))
                    y = Y[:, bass.ds(2 * p + d, 1), :].rearrange("p o (c n) -> p (o c) n", c=3)
                    dve.tensor_tensor(y, pset(d), chunks(xres[d][:, :]), ALU.add).then_inc(op.y[d], 1)

        def out_proj_sp(sp, op, n0, w, res, nxt, loaded=0):
            for d in range(2):
                sp.dma_start(xres[d][:, :], res[:, d, :]).then_inc(op.res_in[d], 16)

            def body(p, last=False, loaded=0):
                for q in range(2 + loaded, 6):
                    if last and q >= 4:
                        if nxt is None:
                            continue
                        src = nxt(q - 4)
                    else:
                        src = out_src(w, p if q < 4 else p + 1, q % 4)
                    load_unit(sp, n0 + 4 * p + q, q % 2, src)
                if not last:
                    for d in range(2):
                        sp.wait_ge(op.y[d], op.b + p + 1)
                        sp.dma_start(xres[d][:, :], res[:, bass.ds(2 * p + 2 + d, 1), :].rearrange("p o n -> p (o n)")
                                     ).then_inc(op.res_in[d], 16)
            body(0, loaded=loaded)
            with sp.Fori(1, KD // 2 - 1) as p:
                body(p)
            body(KD // 2 - 1, last=True)

        def glo_of(j):
            before = sum(x < j for x in Norm.GATED_BY_DVE)
            if j in Norm.GATED_BY_DVE:
                return Norm.lo_dve, len(Norm.BY_DVE) + before + 1
            return glo_ready, j - before + 1

        def gated_lo(engine, j):
            engine.wait_ge(ghi_ready, j + 1)
            engine.tensor_tensor(Glo[:, j, :], tt[j % 8][:, :], Ghi[:, j, :].bitcast(F32), ALU.subtract
                                 ).then_inc(glo_of(j)[0], 1)

        with nc.Block() as block:
            @block.sync
            def _(sp):
                for s in range(4):
                    sp.dma_start(sgl[s][:, :], gate_d[0][s]).then_inc(sgl_in[s], 16)
                for q in range(2, 4):
                    load_unit(sp, U_COUT + q, q % 2, out_src(w_cout, 0, q))
                with sp.Fori(1, JT // 4) as i:
                    for s in range(4):
                        sp.wait_ge(p_ready, 4 * i + s - 3)
                        sp.dma_start(sgl[s][:, :], gate_d[0][4 * i + s]).then_inc(sgl_in[s], 16)
                sp.wait_ge(p_ready, JT)
                out_proj_sp(sp, outp[0], U_COUT, w_cout, res_d[0], lambda q: att_src(q), loaded=2)
                for d in range(2):
                    sp.wait_ge(outp[0].y[d], outp[0].b + KD // 2)
                sp.dma_start(res_d[1], Y[:, :, :]).then_inc(res_out[1], 16)
                sp.wait_ge(res_out[1], 16)

            @block.tensor
            def _(pe):
                for c in range(3):
                    mm = pe.matmul(ps[:, c, 0:CH], ones[:, :], csum[:, c * CH:(c + 1) * CH], start=True, stop=True)
                mm.then_inc(csum_turned, 1)

                for m in range(JT // 2):
                    pe.wait_ge(lpair_ready, m + 1)
                    column_sums(pe, lsq[2 * m % 8], 3, m == 0, m == JT // 2 - 1).then_inc(lsq_used, 1)
                pe.wait_ge(lroot_step, 2)
                spread(pe, lcol, 4).then_inc(lroot_step, 1)
                pe.wait_ge(lrstd_ready, 1)
                out_proj_pe(pe, outp[0], U_COUT, glo_of)
                norm_total(pe, outp[0], norms[1])
                norm_spread(pe, norms[1])

            @block.scalar
            def _(act):
                act.wait_ge(csum_turned, 1)
                act.activation(chunks(mean[:, :]), pset(0), ACT.Copy, scale=1.0 / E).then_inc(mean_ready, 1)

                for j in range(JT):
                    act.wait_ge(xc_ready, j + 1)
                    if j >= 8:
                        act.wait_ge(lsq_used, (j - 8) // 2 + 1)
                    act.activation(lsq[j % 8][:, :], C[:, j, :], ACT.Square).then_inc(lsq_ready, 1)
                act.wait_ge(lsq_used, JT // 2)
                act.activation(lcol[:, :], ps[:, 3, 0:NXT], ACT.Sqrt, scale=1.0 / E, bias=eps_ln
                               ).then_inc(lroot_step, 1)
                act.wait_ge(lroot_step, 3)
                act.activation(lrstd[:, :], spread_out(4), ACT.Copy).then_inc(lrstd_ready, 1)
                for j in range(JT + 3):
                    if j < JT:
                        act.wait_ge(z_ready, j + 1)
                        act.activation(tt[j % 8][:, :], tt[j % 8][:, :], ACT.Silu, scale=cols[:, C_LNG + j:C_LNG + j + 1],
                                       bias=cols[:, C_LNB + j:C_LNB + j + 1]).then_inc(silu_ready, 1)
                    if j >= 3:
                        act.wait_ge(p_ready, j - 2)
                        act.activation(Ghi[:, j - 3, :], tt[(j - 3) % 8][:, :], ACT.Copy).then_inc(ghi_ready, 1)
                out_proj_act(act, outp[0], norms[1], U_COUT, True)
                norm_std(act, norms[1])

            @block.vector
            def _(dve):
                dve.wait_ge(mean_ready, 1)
                with dve.Fori(0, JT) as j:
                    cj = C[:, bass.ds(j, 1), :].rearrange("p o n -> p (o n)")
                    dve.tensor_tensor(cj, cj, mean[:, :], ALU.subtract).then_inc(xc_ready, 1)
                dve.wait_ge(lroot_step, 1)
                dve.reciprocal(lcol[:, :], lcol[:, :]).then_inc(lroot_step, 1)
                dve.wait_ge(lrstd_ready, 1)
                dve.wait_ge(xc_ready, JT)
                for j in range(JT + 2):
                    if j < JT:
                        if j >= 8:
                            dve.wait_ge(glo_ready, j - 7)
                        dve.tensor_tensor(tt[j % 8][:, :], C[:, j, :], lrstd[:, :], ALU.mult).then_inc(z_ready, 1)
                    if j >= 2:
                        dve.wait_ge(silu_ready, j - 1)
                        dve.wait_ge(sgl_in[(j - 2) % 4], 16 * ((j - 2) // 4 + 1))
                        dve.tensor_tensor(tt[(j - 2) % 8][:, :], tt[(j - 2) % 8][:, :], sgl[(j - 2) % 4][:, :],
                                          ALU.mult).then_inc(p_ready, 1)
                for j in Norm.GATED_BY_DVE:
                    gated_lo(dve, j)
                out_proj_dve(dve, outp[0], U_COUT)
                norm_rstd(dve, norms[1])

            @block.gpsimd
            def _(pool):
                with pool.Fori(0, JT // 8) as i:
                    for s in range(4):
                        pool.wait_ge(lsq_ready, 8 * i + 2 * s + 2)
                        pool.tensor_tensor(lsq[2 * s][:, :], lsq[2 * s][:, :], lsq[2 * s + 1][:, :], ALU.add
                                           ).then_inc(lpair_ready, 1)
                for j in range(JT):
                    if j not in Norm.GATED_BY_DVE:
                        gated_lo(pool, j)
                out_proj_pool(pool, norms[1], U_COUT, True)

        cos = place("cos", [P, T], F32, slot(16))
        sin = place("sin", [P, T], F32, slot(17))
        qs = [place(f"qs{s}", [P, T], F32, slot(18 + s)) for s in range(2)]
        qc = [place(f"qc{s}", [P, T], F32, slot(20 + s)) for s in range(2)]
        qr = [place(f"qr{s}", [P, T], F32, slot(22 + s)) for s in range(2)]
        sga = [place(f"sga{s}", [P, T], F32, slot(24 + s)) for s in range(2)]
        at = slot(26)
        rows = [place(f"rows{s}", [P, NXT, P], F32, at) for s in range(2)]
        rsn = [place(f"rsn{s}", [P, T], F32, at) for s in range(2)]
        tab_in = sem("tab_in")
        qs_ready, qc_ready, swapped, rs_ready, qr_ready = (sem(x) for x in (
            "qs_ready", "qc_ready", "swapped", "rs_ready", "qr_ready"))
        qr_out = [sem("qr_out0"), sem("qr_out1")]
        rows_turned, rows_ready = sem("rows_turned"), sem("rows_ready")
        rows_out = [sem("rows_out0"), sem("rows_out1")]
        sga_done = sem("sga_done")
        sga_out = [sem("sga_out0"), sem("sga_out1")]
        NR = JT + NG
        NQK = JT + 2 * NG

        def row_dst(kind, g, sample):
            t = o[("k_rows" if kind == 0 else "v_rows") + ("_sample" if sample else "_prompt")]
            if sample:
                return t[0].rearrange("b t g e -> (b t) g e")[:, g, :]
            return t[0, 0].rearrange("(n p) g e -> p n g e", p=P)[:, :, g, :]

        def spill_gate(sp, i, s):
            sp.wait_ge(sga_done, 2 * i + s + 1)
            sp.dma_start(gate_d[1][2 * i + s], sga[s][:, :]).then_inc(sga_out[s], 16)

        def out_rows(sp, v):
            s, kind, g = v % 2, (v - JT) // NG, (v - JT) % NG
            sp.wait_ge(rows_ready, 3 * (v - JT + 1))
            sp.dma_start(row_dst(kind, g, False), rows[s][:, 0:QT, :]).then_inc(rows_out[s], 16)
            sp.dma_start(row_dst(kind, g, True), rows[s][0:NS_TOK, QT, :]).then_inc(rows_out[s], 16)

        def swap_mm(pe, u, s):
            pe.wait_ge(qs_ready, u + 1)
            pe.wait_ge(rs_ready, u)
            for c, b in enumerate((6, 7, 3 * s + 2)):
                mm = pe.matmul(ps[:, b, 0:CH], swap, qs[s][:, c * CH:(c + 1) * CH], start=True, stop=True)
            mm.then_inc(swapped, 1)

        def turn_rows_last(pe, v):
            s = v % 2
            pe.wait_ge(qs_ready, v + 1)
            pe.wait_ge(rows_ready, 3 * (v - JT))
            for t in range(QT):
                mm = pe.transpose(ps[:, 6 + t // 4, (t % 4) * P:(t % 4 + 1) * P], qs[s][:, t * P:(t + 1) * P], ident)
                if t % 4 == 3:
                    mm.then_inc(rows_turned, 1)
            pe.wait_ge(rows_ready, 3 * (v - JT) + 1)
            pe.transpose(ps[0:NS_TOK, 6, 0:P], qs[s][:, NP_TOK:T], ident).then_inc(rows_turned, 1)

        def rows_evac(act, v, last=False):
            s = v % 2
            if v - JT >= 2:
                act.wait_ge(rows_out[s], 32 * ((v - JT) // 2))
            for part in range(3):
                act.wait_ge(rows_turned, 3 * (v - JT) + part + 1)
                if part < 2:
                    act.activation(rows[s][:, 4 * part:4 * part + 4, :],
                                   ps[:, 6 + part, :].rearrange("p (t e) -> p t e", t=4), ACT.Copy
                                   ).then_inc(rows_ready, 1)
                else:
                    b = 6 if last else 3 * (1 - s) + 1
                    act.activation(rows[s][0:NS_TOK, QT, :], ps[0:NS_TOK, b, 0:P], ACT.Copy
                                   ).then_inc(rows_ready, 1)

        OG = place("OG", [P, JT, T], F32, slot(16))
        kraw = place("kraw", [P, NP_TOK], F32, slot(32))
        vraw = place("vraw", [P, QT, P], F32, slot(33))
        khi = place("khi", [P, NP_TOK], F32R, slot(34))
        klo = place("klo", [P, NP_TOK], F32R, slot(35))
        vhi = place("vhi", [P, QT, P], F32R, slot(36))
        vlo = place("vlo", [P, QT, P], F32R, slot(37))
        qraw = [place(f"qraw{s}", [P, NP_TOK], F32, slot(38 + s)) for s in range(2)]
        qhi = [place(f"qhi{s}", [P, NP_TOK], F32R, slot(40 + s)) for s in range(2)]
        qlo = [place(f"qlo{s}", [P, NP_TOK], F32R, slot(42 + s)) for s in range(2)]
        ssq = place("ssq", [P, JT * QT], F32, slot(45))
        at = slot(0)
        aThi = [place("aThi0", [P, 4, 512], F32R, at), place("aThi1", [P, 8, 512], F32R, at)]
        aTlo = [place("aTlo0", [P, 4, 512], F32R, at), place("aTlo1", [P, 8, 512], F32R, at)]
        osq = place("osq", [P, 512], F32, at)
        identr = place("identr", [P, P], F32R, at)
        causalr = place("causalr", [P, P], F32R, at)
        stats = place("stats", [P, 4, 8], F32, at)
        p1 = [place(f"p1_{s}", [P, NP_TOK], F32, [raw_at[s]]) for s in range(2)]
        p0 = [place(f"p0_{s}", [P, NP_TOK], F32, slot(46) if s == 3 else at) for s in range(4)]
        assert at[0] <= slot(16)[0] and slot(46)[0] + 4 * NP_TOK <= 229344
        kraw_in, vraw_in = sem("kraw_in"), sem("vraw_in")
        qraw_in = [sem("qraw_in0"), sem("qraw_in1")]
        consts_r, kvhi_ready, k_ready, v_ready, qhi_ready, qlo_ready = (sem(x) for x in (
            "consts_r", "kvhi_ready", "k_ready", "v_ready", "qhi_ready", "qlo_ready"))
        s_done, mx_done, exp_done, rc_done, pn_done, comb_done = (sem(x) for x in (
            "scores_done", "max_done", "exp_done", "recip_done", "p1_scaled", "a_ready"))
        tg_done, hi_done, lo_done, pv_done, oev, n_done, ssq_done, og_done = (sem(x) for x in (
            "turn_group", "aT_hi", "aT_lo", "pv_done", "o_copied", "osq_total", "ssq_copied", "og_done"))
        p1_begun = sem("p1_begun")

        def load_q(sp, h, s):
            sp.dma_start(qraw[s][:, :], q_d[h][:, 0:NP_TOK]).then_inc(qraw_in[s], 16)

        def load_k(sp, g):
            sp.dma_start(kraw[:, :], k_d[g][:, 0:NP_TOK]).then_inc(kraw_in, 16)

        def load_v(sp, g):
            v = o["v_rows_prompt"][0, 0].rearrange("(n p) g e -> p n (g e)", p=P)
            sp.dma_start(vraw[:, :, :], v[:, :, bass.ds(g * VD, VD)]).then_inc(vraw_in, 16)

        def q_hi_first(act):
            act.wait_ge(qraw_in[0], 16)
            act.activation(qhi[0][:, :], qraw[0][:, :], ACT.Copy).then_inc(qhi_ready, 1)

        def k_hi_first(act):
            act.wait_ge(kraw_in, 16)
            act.activation(khi[:, :], kraw[:, :], ACT.Copy).then_inc(kvhi_ready, 1)

        def k_lo(dve, g):
            dve.wait_ge(kvhi_ready, 2 * g + 1)
            dve.tensor_tensor(klo[:, :], kraw[:, :], khi[:, :].bitcast(F32), ALU.subtract).then_inc(k_ready, 1)

        def q_lo(pool, g, j):
            s = j % 2
            pool.wait_ge(qhi_ready, GH * g + j + 1)
            pool.tensor_tensor(qlo[s][:, :], qraw[s][:, :], qhi[s][:, :].bitcast(F32), ALU.subtract
                               ).then_inc(qlo_ready, 1)

        with nc.Block() as block:
            @block.sync
            def _(sp):
                sp.dma_start(cos[:, :], a["c_cos"]).then_inc(tab_in, 16)
                sp.dma_start(sin[:, :], a["c_sin"]).then_inc(tab_in, 16)
                with sp.Fori(0, JT // 2) as i:
                    for s in range(2):
                        load_unit(sp, U_ATT + 2 * i + s + 2, s, att_src(2 * i + s + 2))
                    for s in range(2):
                        sp.wait_ge(qr_ready, 2 * i + s + 1)
                        sp.dma_start(q_d[2 * i + s], qr[s][:, :]).then_inc(qr_out[s], 16)
                for u in range(JT, NQK):
                    s = u % 2
                    load_unit(sp, U_ATT + u + 2, s, att_src(u + 2))
                    if JT <= u - 1 < NR:
                        sp.wait_ge(qr_ready, u)
                        sp.dma_start(k_d[u - 1 - JT], qr[1 - s][:, :]).then_inc(qr_out[1 - s], 16)
                    v = u - 2
                    if v >= JT:
                        out_rows(sp, v)
                for u in range(NQK, NQK + 2):
                    load_unit(sp, U_ATT + u + 2, u % 2, att_src(u + 2))
                    out_rows(sp, u - 2)
                def gate(i, last):
                    for s in range(2):
                        if not last:
                            load_unit(sp, U_ATT + NQK + 2 * i + s + 2, s, att_src(NQK + 2 * i + s + 2))
                        else:
                            load_unit(sp, U_ATT + NQK + 2 * i + s + 2, s, out_src(w_aout, 0, s))
                    for s in range(2):
                        spill_gate(sp, i, s)
                for s in range(2):
                    spill_gate(sp, 0, s)
                with sp.Fori(1, JT // 2 - 1) as i:
                    gate(i, False)
                for s in range(2):
                    sp.wait_ge(qr_out[s], 16 * NR // 2)
                    sp.wait_ge(rows_out[s], 32 * NG)
                load_k(sp, 0)
                load_q(sp, 0, 0)
                load_q(sp, 1, 1)
                load_v(sp, 0)
                gate(JT // 2 - 1, True)
                for s in range(2):
                    sp.wait_ge(sga_out[s], 16 * JT // 2)

            @block.tensor
            def _(pe):
                def proj(u, s, first=False):
                    def before(c):
                        if c == 0 and not first:
                            pe.wait_ge(qs_ready, u - 1)
                        if c == 2 and not first:
                            pe.wait_ge(rs_ready, u - 1)
                    unit(pe, U_ATT + u, s, s, h_hi, h_lo, before_chunk=before)

                unit_by_tile(pe, U_ATT, 0, 0, norms[1])
                pe.wait_ge(Norm.h_ready, norms[1].t + KD)
                proj(1, 1, True)
                swap_mm(pe, 0, 0)
                with pe.Fori(1, JT // 2) as i:
                    for s in range(2):
                        u = 2 * i + s
                        proj(u, s)
                        swap_mm(pe, u - 1, 1 - s)

                def turn_rows(v):
                    s = v % 2
                    src = qr[s] if v < NR else qs[s]
                    if v < NR:
                        pe.wait_ge(qr_ready, v + 1)
                        pe.wait_ge(rs_ready, v + 1)
                    else:
                        pe.wait_ge(qs_ready, v + 1)
                        pe.wait_ge(rs_ready, min(v, NR))
                    pe.wait_ge(rows_ready, 3 * (v - JT))
                    for t in range(QT):
                        mm = pe.transpose(ps[:, 6 + t // 4, (t % 4) * P:(t % 4 + 1) * P],
                                          src[:, t * P:(t + 1) * P], ident)
                        if t % 4 == 3:
                            mm.then_inc(rows_turned, 1)
                    b = 3 * (1 - s) + 1
                    pe.wait_ge(qs_ready, v + 2)
                    pe.transpose(ps[0:NS_TOK, b, 0:P], src[:, NP_TOK:T], ident).then_inc(rows_turned, 1)

                for u in range(JT, NQK + 2):
                    s = u % 2

                    def before(c, u=u):
                        if c == 0:
                            pe.wait_ge(qs_ready, min(u - 1, NQK))
                        if c == 1 and u - 3 >= JT:
                            pe.wait_ge(rows_ready, 3 * (u - 3 - JT + 1))
                        if c == 2:
                            pe.wait_ge(rs_ready, min(u - 1, NR))
                    unit(pe, U_ATT + u, s, s, h_hi, h_lo, before_chunk=before)
                    if u - 2 >= JT:
                        if u - 1 < NQK:
                            turn_rows(u - 2)
                            pe.wait_ge(rows_ready, 3 * (u - 2 - JT) + 2)
                    if u - 1 < NR:
                        swap_mm(pe, u - 1, 1 - s)
                    if u == NQK:
                        turn_rows_last(pe, NQK - 1)

                with pe.Fori(1, JT // 2) as i:
                    for s in range(2):
                        u = NQK + 2 * i + s
                        pe.wait_ge(sga_done, 2 * i + s - 1)
                        unit(pe, U_ATT + u, s, s, h_hi, h_lo)

            @block.scalar
            def _(act):
                def copy_out(u, s, turn, first=False, scale=1.0):
                    act.wait_ge(w_used, U_ATT + u + 1)
                    make_hi(act, U_ATT + u + 2, s, turn)
                    if not first:
                        act.wait_ge(qr_ready, u - 1)
                    act.activation(chunks(qs[s][:, :]), pset(s), ACT.Copy, scale=scale).then_inc(qs_ready, 1)

                norm_act(act, norms[1])
                t0 = U_ATT // 2 + 2
                copy_out(0, 0, t0, True, SCALE)
                copy_out(1, 1, t0, True, SCALE)
                with act.Fori(1, JT // 2) as i:
                    for s in range(2):
                        copy_out(2 * i + s, s, t0 + i, scale=SCALE)
                for u in range(JT, NQK):
                    s = u % 2
                    act.wait_ge(w_used, U_ATT + u + 1)
                    make_hi(act, U_ATT + u + 2, s, t0 + u // 2)
                    act.wait_ge(qr_ready, min(u - 1, NR))
                    if u - 2 >= NR:
                        act.wait_ge(rows_turned, 3 * (u - 2 - JT + 1))
                    act.activation(chunks(qs[s][:, :]), pset(s), ACT.Copy).then_inc(qs_ready, 1)
                    if u - 2 >= JT:
                        rows_evac(act, u - 2)

                def silu(i, s, turn, u):
                    act.wait_ge(w_used, U_ATT + u + 1)
                    make_hi(act, U_ATT + u + 2, s, turn)
                    act.wait_ge(sga_out[s], 16 * i)
                    act.activation(chunks(sga[s][:, :]), pset(s), ACT.Silu).then_inc(sga_done, 1)

                act.wait_ge(w_used, U_ATT + NQK + 1)
                rows_evac(act, NQK - 2)
                silu(0, 0, t0 + NQK // 2, NQK)
                rows_evac(act, NQK - 1, True)
                silu(0, 1, t0 + NQK // 2, NQK + 1)
                with act.Fori(1, JT // 2) as i:
                    for s in range(2):
                        silu(i, s, t0 + NQK // 2 + i, NQK + 2 * i + s)
                k_hi_first(act)
                q_hi_first(act)

            @block.gpsimd
            def _(pool):
                norm_pool(pool, norms[1])
                pool.wait_ge(tab_in, 32)

                def rot(u, s, first=False):
                    make_lo(pool, U_ATT + u + 2, s)
                    pool.wait_ge(qs_ready, u + 1)
                    if not first:
                        pool.wait_ge(qr_ready, u - 1)
                    pool.tensor_tensor(qc[s][:, :], qs[s][:, :], cos[:, :], ALU.mult).then_inc(qc_ready, 1)
                rot(0, 0, True)
                rot(1, 1, True)
                with pool.Fori(1, JT // 2) as i:
                    for s in range(2):
                        rot(2 * i + s, s)
                for u in range(JT, NR):
                    rot(u, u % 2)
                with pool.Fori(NR // 2, (NQK + JT) // 2) as i:
                    for s in range(2):
                        make_lo(pool, U_ATT + 2 * i + s + 2, s)
                q_lo(pool, 0, 0)

            @block.vector
            def _(dve):
                norm_dve(dve, norms[1], C_NG2)
                dve.wait_ge(tab_in, 32)

                def rot(u, s, out_turn):
                    dve.wait_ge(swapped, u + 1)
                    for c, b in enumerate((6, 7, 3 * s + 2)):
                        ins = dve.tensor_tensor(rsn[s][:, c * CH:(c + 1) * CH], ps[:, b, 0:CH],
                                                sin[:, c * CH:(c + 1) * CH], ALU.mult)
                        if c == 2:
                            ins.then_inc(rs_ready, 1)
                    dve.wait_ge(rs_ready, u + 1)
                    dve.wait_ge(qc_ready, u + 1)
                    dve.wait_ge(qr_out[s], out_turn)
                    dve.tensor_tensor(qr[s][:, :], qc[s][:, :], rsn[s][:, :], ALU.add).then_inc(qr_ready, 1)
                with dve.Fori(0, JT // 2) as i:
                    for s in range(2):
                        rot(2 * i + s, s, 16 * i)
                for u in range(JT, NR):
                    if u - 2 >= JT:
                        dve.wait_ge(rows_turned, 3 * (u - 2 - JT) + 3)
                    rot(u, u % 2, 16 * (u // 2))
                k_lo(dve, 0)

        kpage = [place("kpage0", [P, PAGES, NG * VD], F32, slot(38))]
        keys_in = [sem("keys_in0"), sem("keys_in1")]
        n_phys = a["cache_k"].shape[1]

        def page_number(sp, b, page):
            return sp.value_load(ptab[0:1, bass.ds(b * PAGES + page, 1)], min_val=0, max_val=n_phys - 1)

        def load_keys(sp, b, s, free=None):
            for page in range(PAGES):
                n = page_number(sp, b, page)
                if page == 0 and free is not None:
                    sp.wait_ge(*free)
                sp.dma_start(kpage[s][:, page, :], a["cache_k"][0][bass.ds(n, 1)].rearrange(
                    "o p g e -> (o p) (g e)")).then_inc(keys_in[s], 16)

        NX = GH * QT
        PRE = 12
        LAG = 2
        VALUES = {8: (0, (0,)), 9: (0, (1, 2, 3)), 10: (1, (0, 1)), 11: (1, (2, 3)), 12: (1, (4, 5)), 13: (1, (6, 7))}
        OUTPUTS, TOTALS, SUMS = {9: 0, 13: 1}, {10: 0, 14: 1}, {11: 0, 15: 1}
        NEW_VALUES = 6
        TAIL = max(SUMS) - QT + 1

        def due(x, top, steps):
            return [(j, steps[x - QT * j]) for j in range(min(x, top - 1) // QT + 1) if x - QT * j in steps]

        def tgroups(x):
            j, i = divmod(x, QT)
            first = 12 * j + (i if i < 4 else 4 + 2 * (i - 4))
            return [(first + n, 4 * n, min(4, i + 1 - 4 * n)) for n in range(i // 4 + 1)]

        def score_ap(i, c):
            w = P * (i + 1)
            if i < 4:
                return ps[:, 2 * (i % 2) + c, 0:w]
            return ps[:, 2 * c:2 * c + 2, :].rearrange("p b n -> p (b n)")[:, 0:w]

        with nc.Block() as block:
            @block.sync
            def _(sp):
                sp.wait_ge(qlo_ready, 1)
                load_q(sp, 2, 0)

                def body(g, last=False):
                    for j in range(GH):
                        h = GH * g + j
                        if j == 0 and not last:
                            sp.wait_ge(k_ready, g + 1)
                            load_k(sp, g + 1)
                            sp.wait_ge(v_ready, g + 1)
                            load_v(sp, g + 1)
                        if j + 3 < GH or not last:
                            sp.wait_ge(qlo_ready, h + 2)
                            load_q(sp, h + 3, (j + 3) % 2)
                with sp.Fori(0, NG - 1) as g:
                    body(g)
                body(NG - 1, last=True)
                sp.wait_ge(pt_in, 16)
                load_keys(sp, 0, 0, free=(s_done, 2 * NX * NG))

            @block.tensor
            def _(pe):
                def scores(g, x, c):
                    j, i = divmod(x, QT)
                    s, w = j % 2, P * (i + 1)
                    if c == 0 and x % NX == 0:
                        pe.wait_ge(k_ready, g + x // NX + 1)
                    if c == 0 and i == 0:
                        pe.wait_ge(qlo_ready, GH * g + j + 1)
                    if x >= 2:
                        if i < 2:
                            need = (x - 1, 0) if i == 0 else (x - 2, 1)
                        elif i < 4:
                            need = (x - 2, c)
                        elif i == 4:
                            need = (x - 2, 1) if c == 0 else (x - 1, 1)
                        else:
                            need = (x - 1, c)
                        pe.wait_ge(exp_done, 2 * NX * g + 2 * need[0] + need[1] + 1)
                    dst = score_ap(i, c)
                    rows_ = slice(HD * c, HD * c + HD)
                    for n, (ql, kr) in enumerate(((qhi, khi), (qhi, klo), (qlo, khi))):
                        for c0 in range(0, w, 512):
                            c1 = min(w, c0 + 512)
                            pe.matmul(dst[:, c0:c1], ql[s][rows_, i * P:(i + 1) * P], kr[rows_, c0:c1],
                                      start=n == 0, stop=n == 2 and c1 < w)
                    pe.matmul(dst[:, i * P:w], identr[:, :], causalr[:, :], start=False, stop=True
                              ).then_inc(s_done, 1)

                def turn(g, x):
                    pe.wait_ge(comb_done, NX * g + x + 1)
                    for tg, b0, nb in tgroups(x):
                        if tg >= 2:
                            pe.wait_ge(lo_done, 12 * GH * g + tg - 1)
                        for b in range(b0, b0 + nb):
                            mm = pe.transpose(ps[:, 4 + tg % 2, (b - b0) * P:(b - b0 + 1) * P],
                                              p0[x % 4][:, b * P:(b + 1) * P], ident)
                        mm.then_inc(tg_done, 1)

                def values(g, j, half, blocks):
                    nb = 4 + 4 * half
                    if blocks[0] == 0:
                        if half == 0:
                            pe.wait_ge(v_ready, g + j // GH + 1)
                        pe.wait_ge(lo_done, 12 * GH * g + 12 * j + (4 if half == 0 else 12))
                        if j >= 1:
                            pe.wait_ge(ssq_done, 2 * (GH * g + j - 1) + half + 1)
                    for b in blocks:
                        c0 = max(0, b - 4 * half) * P
                        for n, (v, at_) in enumerate(((vhi, aThi), (vhi, aTlo), (vlo, aThi))):
                            mm = pe.matmul(ps[:, 6 + half, c0:512], v[:, b, :], at_[half][:, b, c0:512],
                                           start=b == 0 and n == 0, stop=b == nb - 1 and n == 2)
                    if blocks[-1] == nb - 1:
                        mm.then_inc(pv_done, 1)

                def total(g, j, half):
                    pe.wait_ge(oev, 2 * (GH * g + j) + half + 1)
                    for q in range(4):
                        mm = pe.matmul(ps[:, 6 + half, q:q + 1], osq[:, q * P:(q + 1) * P], ones[:, 0:1],
                                       start=True, stop=True)
                    mm.then_inc(n_done, 1)

                def step(g, x, top):
                    j, i = divmod(x, QT)
                    late = x % NX == 0
                    if x < top and not late:
                        scores(g, x, 0)
                        scores(g, x, 1)
                    if 0 <= x - LAG < top:
                        turn(g, x - LAG)
                    for h, part in due(x, top, VALUES):
                        values(g, h, *part)
                    if x < top and late:
                        scores(g, x, 0)
                        scores(g, x, 1)
                    for h, half in due(x, top, TOTALS):
                        total(g, h, half)

                pe.wait_ge(consts_r, 2)
                for x in range(PRE):
                    step(0, x, NX)
                with pe.Fori(0, NG - 1) as g:
                    for x in range(PRE, NX + PRE):
                        step(g, x, 2 * NX)
                for x in range(PRE, NX + TAIL):
                    step(NG - 1, x, NX)

            @block.scalar
            def _(act):
                def q_hi(g, j):
                    act.wait_ge(qraw_in[j % 2], 16 * (2 * g + j // 2 + 1))
                    if j >= 2:
                        act.wait_ge(s_done, 2 * NX * g + 2 * QT * (j - 1))
                    act.activation(qhi[j % 2][:, :], qraw[j % 2][:, :], ACT.Copy).then_inc(qhi_ready, 1)

                def k_hi(g):
                    act.wait_ge(kraw_in, 16 * (g + 1))
                    act.wait_ge(s_done, 2 * NX * g)
                    act.activation(khi[:, :], kraw[:, :], ACT.Copy).then_inc(kvhi_ready, 1)

                def v_hi(g):
                    act.wait_ge(vraw_in, 16 * (g + 1))
                    act.wait_ge(pv_done, 2 * GH * g)
                    act.activation(vhi[:, :, :], vraw[:, :, :], ACT.Copy).then_inc(kvhi_ready, 1)

                def exp(g, x, c):
                    i = x % QT
                    act.wait_ge(mx_done, 2 * NX * g + 2 * x + c + 1)
                    if c == 0 and x >= 4:
                        act.wait_ge(tg_done, 12 * GH * g + tgroups(x - 4)[-1][0] + 1)
                    if c == 1 and x >= 2:
                        act.wait_ge(comb_done, NX * g + x - 1)
                    dst = p0[x % 4] if c == 0 else p1[x % 2]
                    act.activation(dst[:, 0:P * (i + 1)], score_ap(i, c), ACT.Exp,
                                   bias=stats[:, x % 4, c:c + 1],
                                   accum_out=stats[:, x % 4, 2 + c:3 + c]).then_inc(exp_done, 1)

                def hi(g, x):
                    j, i = divmod(x, QT)
                    half = i // 4
                    if j >= 1 and i % 4 == 0:
                        act.wait_ge(pv_done, 2 * (GH * g + j - 1) + half + 1)
                    for tg, b0, nb in tgroups(x):
                        act.wait_ge(tg_done, 12 * GH * g + tg + 1)
                        act.activation(aThi[half][:, b0:b0 + nb, (i % 4) * P:(i % 4 + 1) * P],
                                       ps[:, 4 + tg % 2, 0:nb * P].rearrange("p (b n) -> p b n", b=nb),
                                       ACT.Copy).then_inc(hi_done, 1)

                def output(g, j, half):
                    act.wait_ge(pv_done, 2 * (GH * g + j) + half + 1)
                    act.wait_ge(n_done, 2 * (GH * g + j) + half)
                    act.activation(OG[:, bass.ds(GH * g + j, 1), 512 * half:512 * half + 512].rearrange(
                        "p o n -> p (o n)"), ps[:, 6 + half, :], ACT.Copy)
                    act.activation(osq[:, :], ps[:, 6 + half, :], ACT.Square).then_inc(oev, 1)

                def sums(g, j, half):
                    act.wait_ge(n_done, 2 * (GH * g + j) + half + 1)
                    act.activation(ssq[:, bass.ds(QT * (GH * g + j) + 4 * half, 4)], ps[:, 6 + half, 0:4], ACT.Copy
                                   ).then_inc(ssq_done, 1)

                def step(g, x, top):
                    j, i = divmod(x, QT)
                    if x < top:
                        exp(g, x, 0)
                        exp(g, x, 1)
                    if x == NX - 1 and top > NX:
                        k_hi(g + 1)
                    if 0 <= x - LAG < top:
                        hi(g, x - LAG)
                    if x % NX == NEW_VALUES and x < top:
                        v_hi(g + x // NX)
                    if i == 4 and QT * (j + 1) < top:
                        q_hi(g, j + 1)
                    for h, half in due(x, top, OUTPUTS):
                        output(g, h, half)
                    for h, half in due(x, top, SUMS):
                        sums(g, h, half)

                act.activation(identr[:, :], ident, ACT.Copy).then_inc(consts_r, 1)
                act.activation(causalr[:, :], causal, ACT.Copy).then_inc(consts_r, 1)
                for x in range(PRE):
                    step(0, x, NX)
                with act.Fori(0, NG - 1) as g:
                    for x in range(PRE, NX + PRE):
                        step(g, x, 2 * NX)
                for x in range(PRE, NX + TAIL):
                    step(NG - 1, x, NX)

            @block.vector
            def _(dve):
                def recip(g, x):
                    dve.wait_ge(exp_done, 2 * NX * g + 2 * x + 2)
                    dve.reciprocal(stats[:, x % 4, 4:6], stats[:, x % 4, 2:4]).then_inc(rc_done, 1)

                def maxes(g, x):
                    for c in range(2):
                        dve.wait_ge(s_done, 2 * NX * g + 2 * x + c + 1)
                        dve.tensor_reduce(stats[:, x % 4, c:c + 1], score_ap(x % QT, c), AX.X, ALU.max,
                                          negate=True).then_inc(mx_done, 1)

                def combine(g, x):
                    w = P * (x % QT + 1)
                    dve.wait_ge(pn_done, NX * g + x + 1)
                    dve.scalar_tensor_tensor(out=p0[x % 4][:, 0:w], in0=p0[x % 4][:, 0:w],
                                             scalar=stats[:, x % 4, 4:5], in1=p1[x % 2][:, 0:w],
                                             op0=ALU.mult, op1=ALU.add).then_inc(comb_done, 1)

                def lo(g, x):
                    i = x % QT
                    half = i // 4
                    for tg, b0, nb in tgroups(x):
                        dve.wait_ge(hi_done, 12 * GH * g + tg + 1)
                        cs = slice((i % 4) * P, (i % 4 + 1) * P)
                        dve.tensor_tensor(aTlo[half][:, b0:b0 + nb, cs],
                                          ps[:, 4 + tg % 2, 0:nb * P].rearrange("p (b n) -> p b n", b=nb),
                                          aThi[half][:, b0:b0 + nb, cs].bitcast(F32), ALU.subtract
                                          ).then_inc(lo_done, 1)

                def step(g, x, top):
                    j, i = divmod(x, QT)
                    if 0 <= x - 1 < top:
                        recip(g, x - 1)
                    if x < top:
                        maxes(g, x)
                    if 0 <= x - 1 < top:
                        combine(g, x - 1)
                    if 0 <= x - LAG < top:
                        lo(g, x - LAG)
                    if x == NX - 1 and top > NX:
                        k_lo(dve, g + 1)

                for x in range(PRE):
                    step(0, x, NX)
                with dve.Fori(0, NG - 1) as g:
                    for x in range(PRE, NX + PRE):
                        step(g, x, 2 * NX)
                for x in range(PRE, NX + TAIL):
                    step(NG - 1, x, NX)

            @block.gpsimd
            def _(pool):
                def v_lo(g):
                    pool.wait_ge(kvhi_ready, 2 * g + 2)
                    pool.tensor_tensor(vlo[:, :, :], vraw[:, :, :], vhi[:, :, :].bitcast(F32), ALU.subtract
                                       ).then_inc(v_ready, 1)

                def step(g, x, top):
                    j, i = divmod(x, QT)
                    if x < top:
                        w = P * (i + 1)
                        pool.wait_ge(rc_done, NX * g + x + 1)
                        pool.sem_inc(p1_begun, 1)
                        pool.tensor_scalar(p1[x % 2][:, 0:w], p1[x % 2][:, 0:w], stats[:, x % 4, 5:6], neglam,
                                           ALU.mult, ALU.mult).then_inc(pn_done, 1)
                    if i == 4 and QT * (j + 1) < top:
                        q_lo(pool, g, j + 1)
                    if x % NX == NEW_VALUES and x < top:
                        v_lo(g + x // NX)

                for x in range(PRE):
                    step(0, x, NX)
                with pool.Fori(0, NG - 1) as g:
                    for x in range(PRE, NX + PRE):
                        step(g, x, 2 * NX)
                for x in range(PRE, NX + TAIL):
                    step(NG - 1, x, NX)

        at = slot(0)
        kpage.append(place("kpage1", [P, PAGES, NG * VD], F32, at))
        vpage = [place(f"vpage{s}", [P, PAGES, NG * VD], F32, at) for s in range(2)]
        od = place("o_dec", [NG * GH * NT, NG * VD], F32, at)
        snew = place("snew", [P, NT], F32, at)
        st6 = place("stat_dec", [P, 8], F32, at)
        rT = place("rT", [P, P], F32, at)
        rb = [place(f"rb{s}", [P, NP_TOK], F32, at) for s in range(2)]
        dstd = place("dstd", [P, JT * NS_TOK], F32, at)
        assert at[0] <= slot(16)[0]
        at = slot(32)
        kT = place("kT", [P, 2, PAST], F32, at)
        pd = place("p_dec", [P, PAST + NT], F32, at)
        aTd = place("aT_dec", [P, PAGES, NG * GH * NT], F32, at)
        aTn = place("aT_new", [NT, NG * GH * NT], F32, at)
        qsT = place("q_samples", [P, JT, NS_TOK], F32, at)
        knew = place("k_new", [P, NG, NS_TOK], F32, at)
        vnew = [place(f"v_new{s}", [NT, NG * VD], F32, at) for s in range(2)]
        Qz = place("Qz", [P, NG, P], F32, at)
        zc = place("zc", [P, NG * GH * NT], F32, at)
        assert at[0] <= slot(38)[0]
        at = slot(42)
        sgh = [place(f"sgh{s}", [P, NP_TOK], F32, at) for s in range(2)]
        sgs = place("sg_samples", [P, JT, NS_TOK], F32, at)
        dsq = place("dsq", [P, JT * NS_TOK], F32, at)
        assert at[0] <= slot(45)[0]
        qk_in, og_scaled = sem("qk_in"), sem("og_scaled")
        rb_in = [sem("rb_in0"), sem("rb_in1")]
        od_ready, sel_done = sem("od_ready"), sem("sel_done")
        root_step = sem("root_step")
        values_in = [sem("values_in0"), sem("values_in1")]
        qz_zero, qz_ready, kt_turned, kev_act, kev_dve, ds_done = (sem(x) for x in (
            "qz_zero", "qz_ready", "kt_turned", "kev_act", "kev_dve", "dscore_done"))
        dmx, dexp, zc_ready, at_turned, at_ready, dpv_done, do_ready = (sem(x) for x in (
            "dmax", "dexp", "zc_ready", "aT_turned", "aT_ready", "dpv_done", "do_ready"))
        smp_step = sem("smp_step")
        JOIN_AFTER = 2

        with nc.Block() as block:
            @block.sync
            def _(sp):

                def load_values(b, s, free=None):
                    for page in range(PAGES):
                        n = page_number(sp, b, page)
                        if page == 0 and free is not None:
                            sp.wait_ge(*free)
                        sp.dma_start(vpage[s][:, page, :], a["cache_v"][0][bass.ds(n, 1)].rearrange(
                            "o p g e -> (o p) (g e)")).then_inc(values_in[s], 16)
                    sp.dma_start(vnew[s][:, :], o["v_rows_sample"][0][bass.ds(b, 1)].rearrange(
                        "o t g e -> (o t) (g e)")).then_inc(values_in[s], 16)
                def load_gates(h, s):
                    sp.dma_start(rb[s][:, :], rstd_d[h].partition_broadcast(P)).then_inc(rb_in[s], 16)
                    sp.dma_start(sgh[s][:, :], gate_d[1][h][:, 0:NP_TOK]).then_inc(rb_in[s], 16)

                sp.dma_start(qsT[:, :, :], q_d.rearrange("j p n -> p j n")[:, :, NP_TOK:T]).then_inc(qk_in, 16)
                sp.dma_start(knew[:, :, :], k_d.rearrange("g p n -> p g n")[:, :, NP_TOK:T]).then_inc(qk_in, 16)
                sp.dma_start(sgs[:, :, :], gate_d[1].rearrange("j p n -> p j n")[:, :, NP_TOK:T]).then_inc(qk_in, 16)
                load_keys(sp, 1, 1)
                load_values(0, 0)
                sp.wait_ge(root_step, 4)
                sp.dma_start(rstd_d.rearrange("h (q n) -> (h q) n", q=QT), rT[:, :]).then_inc(root_step, 16)
                sp.wait_ge(root_step, 4 + 16)
                for s in range(2):
                    load_gates(s, s)
                load_values(1, 1)
                with sp.Fori(0, NB // 2 - 1) as i:
                    for s in range(2):
                        b = 2 * i + s
                        load_keys(sp, b + 2, s, free=(kt_turned, 2 * NG * (b + 1)))
                        for t in range(2):
                            sp.wait_ge(og_done, 2 * b + t + 1)
                            load_gates(2 * b + 2 + t, t)
                        load_values(b + 2, s, free=(dpv_done, b + 1))
                for t in range(2):
                    sp.wait_ge(og_done, JT - 4 + t + 1)
                    load_gates(JT - 2 + t, t)

            @block.tensor
            def _(pe):
                def turn_pages(b, s, g):
                    if g >= 2:
                        pe.wait_ge(ds_done, NG * b + g - 1)
                    for half in range(2):
                        f = 2 * g + half
                        if f >= 3:
                            e = kev_act if (f - 3) % 2 == 0 else kev_dve
                            pe.wait_ge(e, NG * b + (f - 3) // 2 + 1)
                        for q in range(4):
                            mm = pe.transpose(ps[:, 3 + f % 3, q * P:(q + 1) * P],
                                              kpage[s][:, 4 * half + q, g * VD:(g + 1) * VD], ident)
                        mm.then_inc(kt_turned, 1)

                def score(b, g):
                    for half in range(2):
                        pe.wait_ge(kev_act if half == 0 else kev_dve, NG * b + g + 1)
                        pe.matmul(ps[:, half, :], Qz[:, g, :], kT[:, g % 2, 512 * half:512 * half + 512],
                                  start=g == 0, stop=g == NG - 1)
                    pe.matmul(ps[:, 2, 0:NT], Qz[:, g, :], knew[:, g, bass.ds(NT * b, NT)],
                              start=g == 0, stop=g == NG - 1).then_inc(ds_done, 1)

                def join(b):
                    pe.wait_ge(zc_ready, b + 1)
                    for page in range(PAGES):
                        pe.matmul(ps[:, 6, 64 * page:64 * page + 64], pd[:, page * P:(page + 1) * P], zc[:, :],
                                  start=True, stop=True)
                    pe.wait_ge(do_ready, b)
                    pe.matmul(ps[0:NT, 7, 64:128], pd[:, PAST:PAST + NT], zc[:, :], start=True, stop=True
                              ).then_inc(at_turned, 1)

                def scores(b, s, i, before=None, last=None):
                    pe.wait_ge(keys_in[s], 16 * PAGES * (i + 1))
                    turn_pages(b, s, 0)
                    if before is None:
                        pe.wait_ge(qk_in, 48)
                    for g in range(NG):
                        if g + 1 < NG:
                            turn_pages(b, s, g + 1)
                        if g == 0:
                            pe.wait_ge(qz_ready, b + 1)
                            if before is not None:
                                pe.wait_ge(dexp, b)
                        score(b, g)
                        if g == 0 and last is not None:
                            choose(last)
                        if g == 1 and before is not None:
                            join(before)

                def values(b, s, i):
                    pe.wait_ge(values_in[s], 16 * (PAGES + 1) * (i + 1))
                    pe.wait_ge(at_ready, 2 * b + 2)
                    for page in range(PAGES):
                        pe.matmul(ps[0:NG * GH * NT, 7, :], aTd[:, page, :], vpage[s][:, page, :],
                                  start=page == 0, stop=False)
                    pe.matmul(ps[0:NG * GH * NT, 7, :], aTn[:, :], vnew[s][:, :], start=False, stop=True
                              ).then_inc(dpv_done, 1)

                def choose(b):
                    pe.wait_ge(od_ready, b + 1)
                    n = GH * NT
                    for g in range(NG):
                        mm = pe.matmul(ps[:, 7, n * g:n * g + n], od[:, g * VD:(g + 1) * VD],
                                       ident[0:NG * n, n * g:n * g + n], start=True, stop=True)
                    mm.then_inc(sel_done, 1)

                scores(0, 0, 0)
                pe.wait_ge(root_step, 2)
                pe.transpose(ps[:, 7, 0:P], ssq[:, :], ident).then_inc(root_step, 1)
                pe.wait_ge(root_step, 4)
                scores(1, 1, 0, before=0)
                values(0, 0, 0)
                with pe.Fori(0, NB // 2 - 1) as i:
                    for s in range(2):
                        b = 2 * i + s + 1
                        scores(b + 1, s, i + 1, before=b, last=b - 1)
                        values(b, 1 - s, i + s)
                choose(NB - 2)
                join(NB - 1)
                values(NB - 1, 1, NB // 2 - 1)
                choose(NB - 1)
                pe.wait_ge(smp_step, 1)
                pe.matmul(ps[:, 0, :], ones[:, :], dsq[:, :], start=True, stop=True).then_inc(smp_step, 1)

            @block.scalar
            def _(act):
                def keys_out(b, g):
                    act.wait_ge(kt_turned, 2 * NG * b + 2 * g + 1)
                    if g >= 2:
                        act.wait_ge(ds_done, NG * b + g - 1)
                    act.activation(kT[:, g % 2, 0:512], ps[:, 3 + (2 * g) % 3, :], ACT.Copy).then_inc(kev_act, 1)

                def exps(b):
                    act.wait_ge(dmx, b + 1)
                    act.activation(pd[:, 0:PAST], ps[:, 0:2, :].rearrange("p b n -> p (b n)"), ACT.Exp,
                                   bias=st6[:, 2:3], accum_out=st6[:, 3:4])
                    act.activation(pd[:, PAST:PAST + NT], snew[:, :], ACT.Exp,
                                   bias=st6[:, 2:3], accum_out=st6[:, 4:5]).then_inc(dexp, 1)

                def joined_out(b):
                    act.wait_ge(at_turned, b + 1)
                    act.activation(aTd[:, :, :].rearrange("p a n -> p (a n)"), ps[:, 6, :], ACT.Copy
                                   ).then_inc(at_ready, 1)

                def values_out(b):
                    act.wait_ge(dpv_done, b + 1)
                    act.activation(od[:, :], ps[0:NG * GH * NT, 7, :], ACT.Copy).then_inc(od_ready, 1)

                def chosen_out(b):
                    act.wait_ge(sel_done, b + 1)
                    act.activation(OG[:, :, bass.ds(NP_TOK + NT * b, NT)],
                                   ps[:, 7, 0:64].rearrange("p (h t) -> p h t", t=NT), ACT.Copy).then_inc(do_ready, 1)

                def sequence(b, last=None):
                    for g in range(NG):
                        keys_out(b + 1, g)
                        if g == 1 and last is not None:
                            chosen_out(last)
                        if g == JOIN_AFTER:
                            joined_out(b)
                    exps(b + 1)
                    values_out(b)
                act.activation(ssq[:, :], ssq[:, :], ACT.Sqrt, scale=1.0 / VD, bias=eps_rms).then_inc(root_step, 1)
                for g in range(NG):
                    keys_out(0, g)
                act.wait_ge(root_step, 3)
                act.activation(rT[:, :], ps[:, 7, 0:P], ACT.Copy).then_inc(root_step, 1)
                exps(0)
                sequence(0)
                with act.Fori(1, NB - 1) as b:
                    sequence(b, last=b - 1)
                chosen_out(NB - 2)
                joined_out(NB - 1)
                values_out(NB - 1)
                chosen_out(NB - 1)
                act.wait_ge(do_ready, NB)
                act.activation(dsq[:, :].rearrange("p (h n) -> p h n", h=JT), OG[:, :, NP_TOK:T], ACT.Square
                               ).then_inc(smp_step, 1)
                act.wait_ge(smp_step, 2)
                act.activation(dstd[:, :], ps[:, 0, :], ACT.Sqrt, scale=1.0 / VD, bias=eps_rms).then_inc(smp_step, 1)

            @block.vector
            def _(dve):
                dve.memset(Qz[:, :, :], 0.0).then_inc(qz_zero, 1)
                dve.wait_ge(root_step, 1)
                dve.reciprocal(ssq[:, :], ssq[:, :]).then_inc(root_step, 1)
                dve.wait_ge(qz_zero, 1)
                dve.wait_ge(qk_in, 48)
                qz_ap = Qz[:, :, :]
                step = qz_ap.ap[0][0]

                def queries(b):
                    dve.wait_ge(ds_done, NG * b)
                    for c in range(2):
                        dst = bass.AP(qz_ap.tensor, HD * c * step + 16 * c,
                                      [[step, HD], [P + 32, NG], [NT, GH], [1, NT]])
                        src = qsT[HD * c:HD * c + HD, :, bass.ds(NT * b, NT)].rearrange("p (g h) t -> p g h t", g=NG)
                        ins = dve.tensor_copy(dst, src)
                    ins.then_inc(qz_ready, 1)

                def keys_out(b, g):
                    dve.wait_ge(kt_turned, 2 * NG * b + 2 * g + 2)
                    if g >= 2:
                        dve.wait_ge(ds_done, NG * b + g - 1)
                    dve.tensor_copy(kT[:, g % 2, 512:1024], ps[:, 3 + (2 * g + 1) % 3, :]).then_inc(kev_dve, 1)

                def softmax(b):
                    dve.wait_ge(ds_done, NG * b + NG)
                    dve.tensor_tensor(snew[:, :], ps[:, 2, 0:NT], newmask, ALU.add
                                      ).then_inc(dve_step.sem, dve_step.up())
                    dve.tensor_reduce(st6[:, 0:1], ps[:, 0:2, :].rearrange("p b n -> p (b n)"), AX.X, ALU.max,
                                      negate=True)
                    dve.wait_ge(dve_step.sem, dve_step.now())
                    dve.tensor_reduce(st6[:, 1:2], snew[:, :], AX.X, ALU.max, negate=True
                                      ).then_inc(dve_step.sem, dve_step.up())
                    dve.wait_ge(dve_step.sem, dve_step.now())
                    dve.tensor_tensor(st6[:, 2:3], st6[:, 0:1], st6[:, 1:2], ALU.min).then_inc(dmx, 1)
                    dve.wait_ge(dexp, b + 1)
                    dve.tensor_tensor(st6[:, 5:6], st6[:, 3:4], st6[:, 4:5], ALU.add
                                      ).then_inc(dve_step.sem, dve_step.up())
                    dve.wait_ge(dve_step.sem, dve_step.now())
                    dve.reciprocal(st6[:, 6:7], st6[:, 5:6]).then_inc(dve_step.sem, dve_step.up())
                    dve.wait_ge(dve_step.sem, dve_step.now())
                    dve.tensor_tensor(st6[:, 7:8], st6[:, 6:7], rowcoef, ALU.mult
                                      ).then_inc(dve_step.sem, dve_step.up())
                    dve.wait_ge(dve_step.sem, dve_step.now())
                    dve.tensor_scalar(zc[:, :], rowsel, st6[:, 7:8], None, ALU.mult).then_inc(zc_ready, 1)

                def joined_out(b):
                    dve.wait_ge(dpv_done, b)
                    dve.wait_ge(at_turned, b + 1)
                    dve.tensor_copy(aTn[:, :], ps[0:NT, 7, 64:128]).then_inc(at_ready, 1)

                def scale(h, s, n):
                    og = OG[:, bass.ds(h, 1), 0:NP_TOK].rearrange("p o n -> p (o n)")
                    dve.wait_ge(rb_in[s], 32 * (n + 1))
                    dve.scalar_tensor_tensor(out=og, in0=og, scalar=subg, in1=rb[s][:, :], op0=ALU.mult,
                                             op1=ALU.mult).then_inc(og_scaled, 1)
                queries(0)
                for g in range(NG):
                    keys_out(0, g)
                softmax(0)
                with dve.Fori(0, NB - 1) as b:
                    dve_step.enter(b, 0, 5)
                    queries(b + 1)
                    for g in range(NG):
                        keys_out(b + 1, g)
                        if g == JOIN_AFTER:
                            joined_out(b)
                    softmax(b + 1)
                    for s in range(2):
                        scale(2 * b + s, s, b)
                dve_step.leave(NB - 1)
                joined_out(NB - 1)
                for s in range(2):
                    scale(JT - 2 + s, s, NB - 1)
                og = OG[:, :, NP_TOK:T]
                d3 = dstd[:, :].rearrange("p (h n) -> p h n", h=JT)
                dve.wait_ge(smp_step, 3)
                dve.reciprocal(dstd[:, :], dstd[:, :]).then_inc(smp_step, 1)
                dve.wait_ge(smp_step, 4)
                dve.scalar_tensor_tensor(out=og, in0=og, scalar=subg, in1=d3, op0=ALU.mult, op1=ALU.mult
                                         ).then_inc(smp_step, 1)
                dve.wait_ge(smp_step, 5)
                dve.tensor_tensor(og, og, sgs[:, :, :], ALU.mult).then_inc(smp_step, 1)

            @block.gpsimd
            def _(pool):
                with pool.Fori(0, JT // 2) as i:
                    for s in range(2):
                        h = 2 * i + s
                        og = OG[:, bass.ds(h, 1), 0:NP_TOK].rearrange("p o n -> p (o n)")
                        pool.wait_ge(og_scaled, h + 1)
                        pool.tensor_tensor(og, og, sgh[s][:, :], ALU.mult).then_inc(og_done, 1)
                pool.wait_ge(smp_step, 6)

        yo = [place(f"yo{t}", [P, D], F32, slot(t)) for t in range(NXT)]
        gfin = place("g_final", [P, D], F32, slot(45))
        ohi_ready, y_turned, yo_act, yo_pool, yo_dve, gfin_in, y_out = (sem(x) for x in (
            "ohi_ready", "y_turned", "yo_act", "yo_pool", "yo_dve", "gfin_in", "y_out"))

        def y_banks(t):
            return 2 * ((t + 1) % 4)

        def o_lo(engine, j, done):
            engine.wait_ge(ohi_ready, j + 1)
            og, hi = (x[:, bass.ds(j, 1), :].rearrange("p o n -> p (o n)") for x in (OG, Ghi))
            engine.tensor_tensor(Glo[:, bass.ds(j, 1), :].rearrange("p o n -> p (o n)"), og, hi.bitcast(F32),
                                 ALU.subtract).then_inc(done, 1)

        with nc.Block() as block:
            @block.sync
            def _(sp):
                sp.dma_start(gfin[:, :], a["final_norm_g"].rearrange("(o d) -> o d", o=1).partition_broadcast(P)
                             ).then_inc(gfin_in, 16)
                out_proj_sp(sp, outp[1], U_AOUT, w_aout, res_d[1], None)
                for t in range(NXT):
                    sp.wait_ge(yo_pool, t + 1)
                    sp.wait_ge(yo_dve, t + 1)
                    if t < QT:
                        sp.dma_start(o["y_prompt"][0, t * P:(t + 1) * P, :], yo[t][:, :]).then_inc(y_out, 16)
                    else:
                        sp.dma_start(o["y_sample"].rearrange("b t d -> (b t) d"), yo[t][P - NS_TOK:P, :]
                                     ).then_inc(y_out, 16)
                sp.wait_ge(y_out, 16 * NXT)

            @block.tensor
            def _(pe):
                out_proj_pe(pe, outp[1], U_AOUT,
                            lambda k: (Norm.lo_pool, norms[2].pool + k // 3 + 1) if k % 3 == 2 else
                            (Norm.lo_dve, norms[2].dve + k - k // 3 + 1))
                norm_total(pe, outp[1], norms[2])
                for t in range(NXT):
                    c0 = min(t * P, T - P)
                    if t == 3:
                        pe.wait_ge(Norm.std_ready, norms[2].o + 1)
                    if t >= 4:
                        pe.wait_ge(yo_act, t - 3)
                        pe.wait_ge(yo_dve, t - 3)
                    for k in range(KD):
                        mm = pe.transpose(ps[:, y_banks(t) + k // 4, (k % 4) * P:(k % 4 + 1) * P],
                                          Y[:, k, c0:c0 + P], ident)
                    mm.then_inc(y_turned, 1)

            @block.scalar
            def _(act):
                with act.Fori(0, JT) as j:
                    act.activation(Ghi[:, bass.ds(j, 1), :].rearrange("p o n -> p (o n)"),
                                   OG[:, bass.ds(j, 1), :].rearrange("p o n -> p (o n)"), ACT.Copy
                                   ).then_inc(ohi_ready, 1)
                out_proj_act(act, outp[1], norms[2], U_AOUT, False)
                norm_std(act, norms[2])
                act.wait_ge(Norm.rstd_ready, norms[2].o + 1)
                for t in range(NXT):
                    act.wait_ge(y_turned, t + 1)
                    act.activation(yo[t][:, 512:1024], ps[:, y_banks(t) + 1, :], ACT.Copy, scale=ncol[:, t:t + 1]
                                   ).then_inc(yo_act, 1)

            @block.vector
            def _(dve):
                with dve.Fori(0, JT // 3) as i:
                    for s in range(2):
                        o_lo(dve, 3 * i + s, Norm.lo_dve)
                o_lo(dve, JT - 1, Norm.lo_dve)
                out_proj_dve(dve, outp[1], U_AOUT)
                norm_rstd(dve, norms[2])
                dve.wait_ge(Norm.rstd_ready, norms[2].o + 1)
                dve.wait_ge(gfin_in, 16)
                for t in range(NXT):
                    dve.wait_ge(y_turned, t + 1)
                    dve.scalar_tensor_tensor(out=yo[t][:, 0:512], in0=ps[:, y_banks(t), :], scalar=ncol[:, t:t + 1],
                                             in1=gfin[:, 0:512], op0=ALU.mult, op1=ALU.mult).then_inc(yo_dve, 1)

            @block.gpsimd
            def _(pool):
                with pool.Fori(0, JT // 3) as i:
                    o_lo(pool, 3 * i + 2, Norm.lo_pool)
                out_proj_pool(pool, norms[2], U_AOUT, False)
                pool.wait_ge(gfin_in, 16)
                for t in range(NXT):
                    pool.wait_ge(yo_act, t + 1)
                    pool.tensor_tensor(yo[t][:, 512:1024], yo[t][:, 512:1024], gfin[:, 512:1024], ALU.mult
                                       ).then_inc(yo_pool, 1)


_INS = ["x_prompt", "x_sample", "state_conv", "cache_k", "cache_v", "page_table", "norm_g", "final_norm_g",
        "conv_w_in", "conv_dw_w", "conv_dw_b", "conv_ln_g", "conv_ln_b", "conv_w_out",
        "attn_w_in", "attn_lambda_q1", "attn_lambda_k1", "attn_lambda_q2", "attn_lambda_k2",
        "attn_subln_g", "attn_w_out"]
_OUTS = [("y_prompt", (1, NP_TOK, D)), ("y_sample", (NB, NT, D)),
         ("conv_state_prompt", (1, 1, PAD, E)), ("conv_state_sample", (1, NB, PAD, E)),
         ("k_rows_prompt", (1, 1, NP_TOK, NG, 2 * HD)), ("v_rows_prompt", (1, 1, NP_TOK, NG, VD)),
         ("k_rows_sample", (1, NB, NT, NG, 2 * HD)), ("v_rows_sample", (1, NB, NT, NG, VD))]


def kernel(**inputs):
    import concourse.bacc as _bacc
    from concourse.bass_utils import run_bass_kernel_spmd as _run

    nc = _bacc.Bacc("TRN2", target_bir_lowering=False, num_devices=1, dynamic_dma_scratch_size=1024)
    arrays = {name: np.ascontiguousarray(inputs[name]) for name in _INS}
    arrays.update(host_constants())
    a = {name: nc.dram_tensor(name, x.shape, mybir.dt.from_np(x.dtype), kind="ExternalInput").ap()
         for name, x in arrays.items()}
    o = {name: nc.dram_tensor(name, shape, F32, kind="ExternalOutput").ap() for name, shape in _OUTS}
    build(nc, a, o)
    r = _run(nc, [arrays], core_ids=[0])
    return tuple(r.results[0][name] for name, _ in _OUTS)
```
